# Optimizing a Trainium2 kernel written in Bass

```python
import math
import jax, jax.numpy as jnp
from jax import lax
import numpy as np

D_MODEL = 1024
BATCH = 1
SEQ = 512
DEPTH = 2

N_MIXERS = 2
DILATED_GROUPS = ((128, 1), (512, 4), (2048, 16))
N_DIL_GROUPS = len(DILATED_GROUPS)
A_HEADS = 16
A_HEAD_DIM = D_MODEL // A_HEADS
ATTN_BLOCK = 128
ROPE_THETA = 10000.0
GDN_HEADS = 8
GDN_HEAD_DIM = D_MODEL // GDN_HEADS
GDN_WIDTH = GDN_HEADS * GDN_HEAD_DIM
CONV_WIDTH = 4
GDN_CHUNK = 64
N_EXPERTS = 64
TOP_K = 8
N_EXPERT_GROUPS = 8
TOPK_GROUPS = 4
EXPERT_DIM = 256
SHARED_DIM = 256
ROUTED_SCALE = 2.5
MOE_BLOCK = 128
ALPHA = (2 * DEPTH) ** 0.25
BETA = (8 * DEPTH) ** -0.25
LN_EPS = 1e-5
RMS_EPS = 1e-6

kernel_name = "hybrid_dilated_attn_gdn_moe_deepnorm"

def layer_norm(x, g, b):
    xf = x.astype(jnp.float32)
    mu = jnp.mean(xf, -1, keepdims=True)
    var = jnp.mean(jnp.square(xf - mu), -1, keepdims=True)
    return ((xf - mu) * lax.rsqrt(var + LN_EPS) * g + b).astype(x.dtype)

def modulate(x, c, w_ada, b_ada):
    shift, scale, gate = jnp.split(c @ w_ada + b_ada, 3, axis=-1)
    h = x * (1.0 + scale[:, None, :]) + shift[:, None, :]
    return h, 1.0 + gate[:, None, :]

def deepnorm_residual(x, y, gate, g, b):
    return layer_norm(ALPHA * x + gate * y, g, b)

def rotary(t, positions):
    half = t.shape[-1] // 2
    inv_freq = ROPE_THETA ** (-jnp.arange(half, dtype=jnp.float32) / half)
    ang = positions.astype(jnp.float32)[..., None] * inv_freq
    cos = jnp.cos(ang)[:, :, None, :]
    sin = jnp.sin(ang)[:, :, None, :]
    t1 = t[..., :half].astype(jnp.float32)
    t2 = t[..., half:].astype(jnp.float32)
    return jnp.concatenate([t1 * cos - t2 * sin, t2 * cos + t1 * sin], axis=-1)

def dilated_window_attention(q, k, v, window, dil):
    B, H, S, hd = q.shape
    steps = window // dil
    assert steps <= ATTN_BLOCK
    span = dil * ATTN_BLOCK
    Sp = -(-S // span) * span
    L = Sp // dil
    nb = L // ATTN_BLOCK
    pad = ((0, 0), (0, 0), (0, Sp - S), (0, 0))

    def by_residue(t):
        return jnp.pad(t, pad).reshape(B, H, L, dil, hd).transpose(0, 1, 3, 2, 4)

    def kv_blocks(t):
        t = jnp.pad(by_residue(t), ((0, 0), (0, 0), (0, 0), (ATTN_BLOCK, 0), (0, 0)))
        t = t.reshape(B, H, dil, nb + 1, ATTN_BLOCK, hd)
        return jnp.concatenate([t[:, :, :, :-1], t[:, :, :, 1:]], axis=-2)

    qb = by_residue(q).reshape(B, H, dil, nb, ATTN_BLOCK, hd)
    kb = kv_blocks(k)
    vb = kv_blocks(v)
    s = jnp.einsum('bhrnqd,bhrnkd->bhrnqk', qb, kb)
    qi = jnp.arange(ATTN_BLOCK)[:, None]
    kj = jnp.arange(2 * ATTN_BLOCK)[None, :]
    dist = qi + ATTN_BLOCK - kj
    band = (dist >= 0) & (dist <= steps)
    before_start = (jnp.arange(nb)[:, None, None] == 0) & (kj[None] < ATTN_BLOCK)
    valid = band[None] & ~before_start
    s = jnp.where(valid, s, -jnp.inf)
    m = jnp.max(s, axis=-1, keepdims=True)
    p = jnp.exp(s - m)
    l = jnp.sum(p, axis=-1, keepdims=True)
    o = jnp.einsum('bhrnqk,bhrnkd->bhrnqd', p, vb) / l
    lse = (m + jnp.log(l))[..., 0]
    o = o.reshape(B, H, dil, L, hd).transpose(0, 1, 3, 2, 4).reshape(B, H, Sp, hd)[:, :, :S]
    lse = lse.reshape(B, H, dil, L).transpose(0, 1, 3, 2).reshape(B, H, Sp)[:, :, :S]
    return o, lse

def dilated_attention_mixer(h, positions, w_in, w_out):
    B, S, D = h.shape
    proj = (h @ w_in).reshape(B, S, N_DIL_GROUPS, 3, A_HEADS, A_HEAD_DIM)
    scale = A_HEAD_DIM ** -0.5
    outs, lses = [], []
    for gi, (window, dil) in enumerate(DILATED_GROUPS):
        q = (rotary(proj[:, :, gi, 0], positions) * scale).transpose(0, 2, 1, 3)
        k = rotary(proj[:, :, gi, 1], positions).transpose(0, 2, 1, 3)
        v = proj[:, :, gi, 2].astype(jnp.float32).transpose(0, 2, 1, 3)
        o, lse = dilated_window_attention(q, k, v, window, dil)
        outs.append(o)
        lses.append(lse)
    wts = jax.nn.softmax(jnp.stack(lses), axis=0)
    o = jnp.sum(wts[..., None] * jnp.stack(outs), axis=0)
    o = o.transpose(0, 2, 1, 3).reshape(B, S, A_HEADS * A_HEAD_DIM).astype(h.dtype)
    return o @ w_out

def causal_depthwise_conv(x, w):
    K = w.shape[0]
    S = x.shape[1]
    xp = jnp.pad(x, ((0, 0), (K - 1, 0), (0, 0)))
    y = xp[:, 0:S] * w[0]
    for j in range(1, K):
        y = y + xp[:, j:j + S] * w[j]
    return y

def l2_normalize(t):
    return t * lax.rsqrt(jnp.sum(jnp.square(t), -1, keepdims=True) + RMS_EPS)

def gated_delta_rule(q, k, v, g, beta):
    B, S, H, dk = q.shape
    dv = v.shape[-1]
    C = GDN_CHUNK
    N = S // C

    def chunks(t):
        t = jnp.moveaxis(t.astype(jnp.float32), 2, 1)
        return t.reshape((B, H, N, C) + t.shape[3:])

    q, k, v, g, beta = chunks(q), chunks(k), chunks(v), chunks(g), chunks(beta)
    gc = jnp.cumsum(g, axis=-1)
    causal = jnp.tril(jnp.ones((C, C), bool))
    strict = jnp.tril(jnp.ones((C, C), bool), -1)
    decay = jnp.exp(jnp.where(causal, gc[..., :, None] - gc[..., None, :], -jnp.inf))
    kb = k * beta[..., None]
    lower = jnp.where(strict, jnp.einsum('bhnid,bhnjd->bhnij', kb, k) * decay, 0.0)
    a_mat = lower + jnp.eye(C, dtype=jnp.float32)
    rhs = jnp.concatenate([v * beta[..., None], kb * jnp.exp(gc)[..., None]], axis=-1)
    sol = lax.linalg.triangular_solve(a_mat, rhs, left_side=True, lower=True,
                                      unit_diagonal=True)
    u, w = sol[..., :dv], sol[..., dv:]
    qk = jnp.einsum('bhnid,bhnjd->bhnij', q, k) * decay
    qg = q * jnp.exp(gc)[..., None]
    kdec = k * jnp.exp(gc[..., -1:] - gc)[..., None]
    glast = jnp.exp(gc[..., -1])

    def step(state, xs):
        u_n, w_n, qk_n, qg_n, kdec_n, gl_n = xs
        v_new = u_n - jnp.einsum('bhcd,bhde->bhce', w_n, state)
        o = (jnp.einsum('bhcd,bhde->bhce', qg_n, state)
             + jnp.einsum('bhij,bhje->bhie', qk_n, v_new))
        state = state * gl_n[..., None, None] + jnp.einsum('bhcd,bhce->bhde', kdec_n, v_new)
        return state, o

    xs = tuple(jnp.moveaxis(t, 2, 0) for t in (u, w, qk, qg, kdec, glast))
    _, o = lax.scan(step, jnp.zeros((B, H, dk, dv), jnp.float32), xs)
    return o.transpose(1, 0, 3, 2, 4).reshape(B, S, H, dv)

def gated_deltanet_mixer(h, w_in, conv_w, a_log, dt_bias, norm_w, w_out):
    B, S, D = h.shape
    H, dh, W = GDN_HEADS, GDN_HEAD_DIM, GDN_WIDTH
    proj = h @ w_in
    qkv = jax.nn.silu(causal_depthwise_conv(proj[..., :3 * W], conv_w))
    z = proj[..., 3 * W:4 * W].astype(jnp.float32).reshape(B, S, H, dh)
    a = proj[..., 4 * W:4 * W + H].astype(jnp.float32)
    b = proj[..., 4 * W + H:].astype(jnp.float32)
    qkv = qkv.astype(jnp.float32).reshape(B, S, 3, H, dh)
    q = l2_normalize(qkv[:, :, 0]) * dh ** -0.5
    k = l2_normalize(qkv[:, :, 1])
    v = qkv[:, :, 2]
    beta = jax.nn.sigmoid(b)
    g = -jnp.exp(a_log.astype(jnp.float32)) * jax.nn.softplus(a + dt_bias)
    o = gated_delta_rule(q, k, v, g, beta)
    o = o * lax.rsqrt(jnp.mean(jnp.square(o), -1, keepdims=True) + RMS_EPS) * norm_w
    o = o * jax.nn.silu(z)
    return o.reshape(B, S, W).astype(h.dtype) @ w_out

def swiglu(x, w1, w3, w2):
    return (jax.nn.silu(x @ w1) * (x @ w3)) @ w2

def moe(h, router_w, router_bias, w1, w3, w2, ws1, ws3, ws2):
    B, S, D = h.shape
    T = B * S
    xt = h.reshape(T, D)
    scores = jax.nn.sigmoid((xt @ router_w).astype(jnp.float32))
    biased = scores + router_bias.astype(jnp.float32)
    grp = biased.reshape(T, N_EXPERT_GROUPS, N_EXPERTS // N_EXPERT_GROUPS)
    gscore = jnp.sum(lax.top_k(grp, 2)[0], axis=-1)
    _, gidx = lax.top_k(gscore, TOPK_GROUPS)
    gmask = jnp.any(gidx[..., :, None] == jnp.arange(N_EXPERT_GROUPS), axis=-2)
    emask = jnp.repeat(gmask, N_EXPERTS // N_EXPERT_GROUPS, axis=-1)
    _, eidx = lax.top_k(jnp.where(emask, biased, -jnp.inf), TOP_K)
    gates = jnp.take_along_axis(scores, eidx, axis=-1)
    gates = gates / jnp.sum(gates, -1, keepdims=True) * ROUTED_SCALE

    n_assign = T * TOP_K
    flat_e = eidx.reshape(-1)
    flat_tok = jnp.repeat(jnp.arange(T, dtype=jnp.int32), TOP_K)
    flat_w = gates.reshape(-1)
    order = jnp.argsort(flat_e)
    se, stok, sw = flat_e[order], flat_tok[order], flat_w[order]
    counts = jnp.bincount(flat_e, length=N_EXPERTS)
    start = jnp.cumsum(counts) - counts
    padded = (counts + MOE_BLOCK - 1) // MOE_BLOCK * MOE_BLOCK
    pend = jnp.cumsum(padded)
    pstart = pend - padded
    dest = pstart[se] + jnp.arange(n_assign) - start[se]
    n_blocks = -(-n_assign // MOE_BLOCK) + N_EXPERTS
    P = n_blocks * MOE_BLOCK
    row_tok = jnp.full((P,), T, jnp.int32).at[dest].set(stok)
    row_w = jnp.zeros((P,), jnp.float32).at[dest].set(sw)
    blk_e = jnp.minimum(jnp.searchsorted(pend, jnp.arange(n_blocks) * MOE_BLOCK, side='right'),
                        N_EXPERTS - 1)
    x_pad = jnp.concatenate([xt, jnp.zeros((1, D), xt.dtype)], axis=0)

    def expert_block(acc, blk):
        tok, wt, e = blk
        y = swiglu(x_pad[tok], w1[e], w3[e], w2[e])
        return acc.at[tok].add(y * wt[:, None].astype(y.dtype)), None

    acc, _ = lax.scan(expert_block, jnp.zeros((T + 1, D), xt.dtype),
                      (row_tok.reshape(n_blocks, MOE_BLOCK),
                       row_w.reshape(n_blocks, MOE_BLOCK), blk_e))
    out = acc[:T] + swiglu(xt, ws1, ws3, ws2)
    return out.reshape(B, S, D)

def setup_inputs(seed: int = 0) -> dict:
    key = jax.random.key(seed)
    ks = jax.random.split(key, 24)
    D = D_MODEL
    n_a = (DEPTH + 1) // 2
    n_b = DEPTH // 2
    H = GDN_HEADS

    def nrm(k, shape, s):
        return jax.random.normal(k, shape, jnp.float32) * s

    x = nrm(ks[0], (BATCH, SEQ, D), 1.0)
    c = nrm(ks[1], (BATCH, D), 1.0)
    positions = jnp.broadcast_to(jnp.arange(SEQ, dtype=jnp.int32), (BATCH, SEQ))
    ada_w = nrm(ks[2], (DEPTH, 2, D, 3 * D), 0.1 * D ** -0.5)
    ada_b = nrm(ks[3], (DEPTH, 2, 3 * D), 0.02)
    ln_g = 1.0 + nrm(ks[4], (DEPTH, 2, D), 0.02)
    ln_b = nrm(ks[5], (DEPTH, 2, D), 0.02)
    attn_w_in = nrm(ks[6], (n_a, D, N_DIL_GROUPS * 3 * A_HEADS * A_HEAD_DIM), D ** -0.5)
    attn_w_out = nrm(ks[7], (n_a, A_HEADS * A_HEAD_DIM, D), BETA * (A_HEADS * A_HEAD_DIM) ** -0.5)
    gdn_w_in = nrm(ks[8], (n_b, D, 4 * GDN_WIDTH + 2 * H), D ** -0.5)
    gdn_conv_w = nrm(ks[9], (n_b, CONV_WIDTH, 3 * GDN_WIDTH), CONV_WIDTH ** -0.5)
    gdn_a_log = jnp.log(jax.random.uniform(ks[10], (n_b, H), jnp.float32, 1.0, 16.0))
    dt = jnp.exp(jax.random.uniform(ks[11], (n_b, H), jnp.float32,
                                    math.log(1e-3), math.log(1e-1)))
    gdn_dt_bias = jnp.log(jnp.expm1(dt))
    gdn_norm_w = 1.0 + nrm(ks[12], (n_b, GDN_HEAD_DIM), 0.02)
    gdn_w_out = nrm(ks[13], (n_b, GDN_WIDTH, D), BETA * GDN_WIDTH ** -0.5)
    router_w = nrm(ks[14], (DEPTH, D, N_EXPERTS), D ** -0.5)
    router_bias = nrm(ks[15], (DEPTH, N_EXPERTS), 0.01)
    expert_w1 = nrm(ks[16], (DEPTH, N_EXPERTS, D, EXPERT_DIM), D ** -0.5)
    expert_w3 = nrm(ks[17], (DEPTH, N_EXPERTS, D, EXPERT_DIM), D ** -0.5)
    expert_w2 = nrm(ks[18], (DEPTH, N_EXPERTS, EXPERT_DIM, D), BETA * EXPERT_DIM ** -0.5)
    shared_w1 = nrm(ks[19], (DEPTH, D, SHARED_DIM), D ** -0.5)
    shared_w3 = nrm(ks[20], (DEPTH, D, SHARED_DIM), D ** -0.5)
    shared_w2 = nrm(ks[21], (DEPTH, SHARED_DIM, D), BETA * SHARED_DIM ** -0.5)
    return {"x": x, "c": c, "positions": positions, "ada_w": ada_w, "ada_b": ada_b,
            "ln_g": ln_g, "ln_b": ln_b, "attn_w_in": attn_w_in, "attn_w_out": attn_w_out,
            "gdn_w_in": gdn_w_in, "gdn_conv_w": gdn_conv_w, "gdn_a_log": gdn_a_log,
            "gdn_dt_bias": gdn_dt_bias, "gdn_norm_w": gdn_norm_w, "gdn_w_out": gdn_w_out,
            "router_w": router_w, "router_bias": router_bias, "expert_w1": expert_w1,
            "expert_w3": expert_w3, "expert_w2": expert_w2, "shared_w1": shared_w1,
            "shared_w3": shared_w3, "shared_w2": shared_w2}

def reference(x, c, positions, ada_w, ada_b, ln_g, ln_b, attn_w_in, attn_w_out,
              gdn_w_in, gdn_conv_w, gdn_a_log, gdn_dt_bias, gdn_norm_w, gdn_w_out,
              router_w, router_bias, expert_w1, expert_w3, expert_w2,
              shared_w1, shared_w3, shared_w2):
    for i in range(DEPTH):
        j = i // N_MIXERS
        h, gate = modulate(x, c, ada_w[i, 0], ada_b[i, 0])
        if i % N_MIXERS == 0:
            y = dilated_attention_mixer(h, positions, attn_w_in[j], attn_w_out[j])
        else:
            y = gated_deltanet_mixer(h, gdn_w_in[j], gdn_conv_w[j], gdn_a_log[j],
                                     gdn_dt_bias[j], gdn_norm_w[j], gdn_w_out[j])
        x = deepnorm_residual(x, y, gate, ln_g[i, 0], ln_b[i, 0])
        h, gate = modulate(x, c, ada_w[i, 1], ada_b[i, 1])
        y = moe(h, router_w[i], router_bias[i], expert_w1[i], expert_w3[i], expert_w2[i],
                shared_w1[i], shared_w3[i], shared_w2[i])
        x = deepnorm_residual(x, y, gate, ln_g[i, 1], ln_b[i, 1])
    return x


_drawn_inputs = setup_inputs


def setup_inputs(seed=0):
    import zlib

    import numpy as np

    out = dict(_drawn_inputs(seed))
    spreads = {}
    factors = {'gdn_norm_w': 3.587}
    for name, (base, spread) in spreads.items():
        noise = np.random.default_rng([zlib.crc32(name.encode()), seed]).standard_normal(out[name].shape)
        drawn = base * np.exp(spread * noise) if base else spread * noise
        out[name] = __import__('jax').numpy.asarray(drawn.astype(out[name].dtype))
    for name, factor in factors.items():
        out[name] = (out[name] * factor).astype(out[name].dtype)
    return out
```

```python
from contextlib import ExitStack

import numpy as np
import concourse.bass as bass
from concourse import mybir

F32 = mybir.dt.float32
BF16 = mybir.dt.bfloat16
I32 = mybir.dt.int32
U32 = mybir.dt.uint32
ALU = mybir.AluOpType
ACT = mybir.ActivationFunctionType
AX = mybir.AxisListType

P = 128
SEQ, D = 512, 1024
TT = SEQ // P
KT = D // P
DEPTH = 2
ALPHA = (2 * DEPTH) ** 0.25
LN_EPS, RMS_EPS = 1e-5, 1e-6
NEG = -1e30

HEADS, HD = 16, 64
GROUPS = 3
WINDOW0 = 128
QUADS = HEADS // 4
QF = 4 * HD
RES = 4
ROPE_THETA = 10000.0

GH, GD = 8, 128
CONV = 4

NE, TOPK, NG, TOPG = 64, 8, 8, 4
ED = 256
CAP = P
OVB = SEQ * TOPK // (CAP + 1)
ROUTED_SCALE = 2.5
NYG = 8


class Stage:

    def __init__(self, nc, tag):
        self.nc, self.tag, self.ctx, self.sems = nc, tag, ExitStack(), []

    def sb(self, name, shape, dt=F32):
        return self.ctx.enter_context(self.nc.sbuf_tensor(f"{self.tag}_{name}", shape, dt))

    def ps(self, name, shape, dt=F32):
        return self.ctx.enter_context(self.nc.psum_tensor(f"{self.tag}_{name}", shape, dt))

    def sem(self, name):
        s = self.ctx.enter_context(self.nc.semaphore(f"{self.tag}_{name}"))
        self.sems.append(s)
        return s

    def close(self, gathers=False):
        if gathers:
            self.nc.gpsimd.dma_reset()
        for s in self.sems:
            self.nc.gpsimd.sem_clear(s)
        self.nc.all_engine_barrier()
        self.ctx.close()


class Chain:

    def __init__(self, eng, sem, base=0):
        self.eng, self.sem, self.base, self.n = eng, sem, base, 0

    def do(self, ins):
        ins.then_inc(self.sem, 1)
        self.n += 1
        return ins

    def sync(self):
        self.eng.wait_ge(self.sem, self.base + self.n)


class Core:
    pass


def alloc_core(nc, ctx):
    c = Core()

    def sb(name, shape, dt=F32):
        return ctx.enter_context(nc.sbuf_tensor(f"core_{name}", shape, dt))

    c.x = sb("x", [P, TT, D])
    c.hT = sb("hT", [P, KT, SEQ])
    c.ada = sb("ada", [P, 3, D])
    c.cb = sb("cb", [P, KT, P])
    c.ident = sb("ident", [P, P])
    c.ones = sb("ones", [P, P])
    c.upper = sb("upper", [P, P])
    return c


def setup_stage(nc, c, A):
    st = Stage(nc, "setup")
    ct = st.sb("ct", [P, KT])
    loaded, filled, selected = st.sem("loaded"), st.sem("filled"), st.sem("selected")
    spread = st.sem("spread")
    with nc.Block() as block:
        @block.sync
        def _(sp):
            sp.dma_start(ct[:], A["c"].rearrange("a (p k) -> p (a k)", k=KT)).then_inc(loaded, 16)
            sp.dma_start(c.x[:], A["x"][0].rearrange("(t p) d -> p t d", p=P)).then_inc(loaded, 16)

        @block.vector
        def _(dve):
            nc.vector.memset(c.ident[:], 0.0).then_inc(filled, 1)
            nc.vector.memset(c.upper[:], 1.0).then_inc(filled, 1)
            nc.vector.memset(c.ones[:], 1.0).then_inc(filled, 1)
            dve.wait_ge(loaded, 32)
            nc.vector.tensor_copy(c.cb[:], ct[:].rearrange("p (k o) -> p k o", o=1).broadcast_to([P, KT, P])).then_inc(spread, 1)
            dve.wait_ge(spread, 1)

        @block.gpsimd
        def _(pool):
            pool.wait_ge(filled, 3)
            pool.affine_select(out=c.ident[:], in_=c.ident[:], compare_op=ALU.not_equal, fill=1.0, base=0,
                               pattern=[[-1, P]], channel_multiplier=1).then_inc(selected, 1)
            pool.affine_select(out=c.upper[:], in_=c.upper[:], compare_op=ALU.is_ge, fill=0.0, base=0,
                               pattern=[[1, P]], channel_multiplier=-1).then_inc(selected, 1)
            pool.wait_ge(selected, 2)
    st.close()


def norm_stage(nc, c, A, norm, mod, h_rows=None, out=None):
    st = Stage(nc, f"norm{norm}")
    SLOTS = 2
    sem = st.sem
    rows_in, x_out, h_out = sem("rows_in"), sem("x_out"), sem("h_out")
    bias_in = sem("bias_in")
    w_in = [sem(f"w_in{i}") for i in range(SLOTS)]
    w_used, ada_sum, ada_ready = sem("w_used"), sem("ada_sum"), sem("ada_ready")
    dve_step, var_ready, std_ready = sem("dve_step"), sem("var_ready"), sem("std_ready")
    x_ready, h_ready, turned, laid = sem("x_ready"), sem("h_ready"), sem("turned"), sem("laid")
    if norm is not None:
        g = st.sb("g", [P, D])
        b = st.sb("b", [P, D])
        stats = st.sb("stats", [P, TT, 2, 6])
        mv = st.sb("mv", [P, TT, 2])
        std = st.sb("std", [P, TT])
        eps = st.sb("eps", [P, 1])
        xn = st.sb("xn", [P, 2, D])
    if mod is not None:
        w = st.sb("w", [P, SLOTS, 3 * D])
        bias = st.sb("bias", [P, 3 * D])
        h = st.sb("h", [P, TT, D])
        ada_ps = [st.ps(f"ada{n}", [P, 512]) for n in range(6)]
        tp = [st.ps(f"tp{n}", [P, 4, P]) for n in range(2)]
        aw = A["ada_w"][mod // 2, mod % 2].rearrange("(p k) n -> p k n", k=KT)

    def row(t, i):
        return t[i // 2, i % 2].rearrange("(a n) -> a n", a=1).partition_broadcast(P)

    with nc.Block() as block:
        @block.sync
        def _(sp):
            if mod is not None:
                for k in range(KT):
                    if k >= SLOTS:
                        sp.wait_ge(w_used, k - SLOTS + 1)
                    sp.dma_start(w[:, k % SLOTS], aw[:, k]).then_inc(w_in[k % SLOTS], 16)
            for t in range(TT):
                if h_rows is not None:
                    sp.wait_ge(h_ready, t + 1)
                    sp.dma_start(h_rows[t * P:(t + 1) * P, :], h[:, t]).then_inc(h_out, 16)
                if out is not None:
                    sp.wait_ge(x_ready, t + 1)
                    sp.dma_start(out[0, t * P:(t + 1) * P, :], c.x[:, t]).then_inc(x_out, 16)
            if h_rows is not None:
                sp.wait_ge(h_out, 16 * TT)
            if out is not None:
                sp.wait_ge(x_out, 16 * TT)

        @block.scalar
        def _(act):
            if norm is not None:
                act.dma_start(g[:], row(A["ln_g"], norm)).then_inc(rows_in, 16)
                act.dma_start(b[:], row(A["ln_b"], norm)).then_inc(rows_in, 16)
            if mod is not None:
                act.dma_start(bias[:], row(A["ada_b"], mod)).then_inc(bias_in, 16)
            if norm is not None:
                for t in range(TT):
                    act.wait_ge(var_ready, t + 1)
                    nc.scalar.activation(std[:, t:t + 1], mv[:, t, 1:2], ACT.Sqrt, bias=eps[:]).then_inc(std_ready, 1)
            if mod is not None:
                for t in range(TT):
                    for q in range(2):
                        act.wait_ge(turned, 2 * t + q + 1)
                        nc.scalar.copy(c.hT[:, 4 * q:4 * q + 4, t * P:(t + 1) * P], tp[q][:]).then_inc(laid, 1)
                act.wait_ge(laid, 2 * TT)

        @block.vector
        def _(dve):
            ch = Chain(dve, dve_step)
            if norm is not None:
                ch.do(nc.vector.memset(eps[:], LN_EPS))
                for t in range(TT):
                    for q in range(2):
                        ch.do(nc.vector.bn_stats(stats[:, t, q], c.x[:, t, q * 512:(q + 1) * 512]))
                ch.sync()
                for t in range(TT):
                    nc.vector.bn_aggr(mv[:, t], stats[:, t]).then_inc(var_ready, 1)
                dve.wait_ge(var_ready, TT)
                dve.wait_ge(std_ready, TT)
                ch.do(nc.vector.reciprocal(std[:], std[:]))
                dve.wait_ge(rows_in, 32)
                ch.sync()
                for t in range(TT):
                    ch.do(nc.vector.tensor_scalar(xn[:, t % 2], c.x[:, t], mv[:, t, 0:1], std[:, t:t + 1],
                                                  ALU.subtract, ALU.mult))
                    ch.sync()
                    ch.do(nc.vector.tensor_tensor(xn[:, t % 2], xn[:, t % 2], g[:], ALU.mult))
                    ch.sync()
                    nc.vector.tensor_tensor(c.x[:, t], xn[:, t % 2], b[:], ALU.add).then_inc(x_ready, 1)
                dve.wait_ge(x_ready, TT)
            if mod is not None:
                dve.wait_ge(ada_sum, 1)
                dve.wait_ge(bias_in, 16)
                for n in range(6):
                    o = c.ada[:, n // 2, n % 2 * 512:(n % 2 + 1) * 512]
                    nc.vector.scalar_tensor_tensor(out=o, in0=ada_ps[n][:], scalar=0.0 if n < 2 else 1.0,
                                                   in1=bias[:, n * 512:(n + 1) * 512],
                                                   op0=ALU.add, op1=ALU.add).then_inc(ada_ready, 1)
                dve.wait_ge(ada_ready, 6)
                for t in range(TT):
                    ch.do(nc.vector.tensor_tensor(h[:, t], c.x[:, t], c.ada[:, 1], ALU.mult))
                    ch.sync()
                    nc.vector.tensor_tensor(h[:, t], h[:, t], c.ada[:, 0], ALU.add).then_inc(h_ready, 1)
                dve.wait_ge(h_ready, TT)

        @block.tensor
        def _(pe):
            if mod is not None:
                for k in range(KT):
                    pe.wait_ge(w_in[k % SLOTS], 16 * (k // SLOTS + 1))
                    for n in range(6):
                        last = nc.tensor.matmul(ada_ps[n][:], c.cb[:, k], w[:, k % SLOTS, n * 512:(n + 1) * 512],
                                                start=k == 0, stop=k == KT - 1)
                    last.then_inc(w_used if k < KT - 1 else ada_sum, 1)
                for t in range(TT):
                    pe.wait_ge(h_ready, t + 1)
                    for q in range(2):
                        if t:
                            pe.wait_ge(laid, 2 * t - 1 + q)
                        for k in range(4):
                            last = nc.tensor.transpose(tp[q][:, k], h[:, t, 4 * q + k::KT], c.ident[:])
                        last.then_inc(turned, 1)
    st.close()


def attention_stage(nc, c, A, y_rows=None):
    st = Stage(nc, "attn")
    SLOTS = 3
    CH = 3 * GROUPS
    NPROJ = 2 * CH
    PC = 2 * SLOTS
    NROT = 4 * GROUPS
    UNITS = 4 * RES
    KEYS = SEQ + 2 * P
    C1, C2 = 6.28125, float(np.float32(0.0019350051879882812))
    C3 = float(2 * np.pi - C1 - C2)
    ROUND = 12582912.0

    w = st.sb("w", [P, SLOTS, KT, QF])
    v = st.sb("v", [P, GROUPS, TT, QF])
    q = st.sb("q", [P, GROUPS, 2, 2, SEQ])
    k = st.sb("k", [P, GROUPS, 2, SEQ])
    raw = st.sb("raw", [P, 2, SEQ])
    swp = st.sb("swp", [P, 2, SEQ])
    rot = st.sb("rot", [P, 2, SEQ])
    cos = st.sb("cos", [P, SEQ])
    sin = st.sb("sin", [P, SEQ])
    mask = st.sb("mask", [P, RES, KEYS])
    sm = st.sb("sm", [P, 2, KEYS])
    prob = st.sb("prob", [P, 2, KEYS])
    probT = st.sb("probT", [P, 2, KEYS])
    o = st.sb("o", [P, 2, P])
    oT = st.sb("oT", [P, KT, SEQ])
    small = st.sb("small", [P, 12])
    top = small[:, 0:2]
    bias = small[:, 2:4]
    den = small[:, 4:8]
    rden = small[:, 8:12]
    freq = st.sb("freq", [P, 2])
    halfpi = st.sb("halfpi", [P, 1])
    pos = st.sb("pos", [P, SEQ], I32)
    diff = st.sb("diff", [P, P], I32)
    zero = st.sb("zero", [P, 1, SEQ])

    proj = [st.ps(f"proj{n}", [P, 512]) for n in range(2)]
    sc = st.ps("sc", [P, 1024])
    tp = st.ps("tp", [P, 8, P])
    pv = st.ps("pv", [P, 512])
    po = st.ps("po", [P, 512])

    sem = st.sem
    w_in = [sem(f"w_in{n}") for n in range(SLOTS)]
    proj_done, proj_free = sem("proj_done"), sem("proj_free")
    raw_ready, rot_done = sem("raw_ready"), sem("rot_done")
    swp_in = [sem(f"swp_in{n}") for n in range(2)]
    sc_done, sm_ready, bias_ready, p_ready = sem("sc_done"), sem("sm_ready"), sem("bias_ready"), sem("p_ready")
    tp_done, pT_ready, pv_done, o_ready = sem("tp_done"), sem("pT_ready"), sem("pv_done"), sem("o_ready")
    oT_done, oT_ready = sem("oT_done"), sem("oT_ready")
    dve_step, pool_step, tables_in, angle_ready = sem("dve_step"), sem("pool_step"), sem("tables_in"), sem("angle_ready")
    sin_ready, diff_ready, parity_ready, mask_ready = sem("sin_ready"), sem("diff_ready"), sem("parity_ready"), sem("mask_ready")
    turn_seen, zero_ready, cleared = sem("turn_seen"), sem("zero_ready"), sem("cleared")
    y_done, y_used = sem("y_done"), sem("y_used")
    DVE_T = NROT // 2 + 2 * NROT + UNITS

    half = HD // 2
    f = np.arange(P)
    table = np.stack([ROPE_THETA ** (-(f % half).astype(np.float32) / np.float32(half)),
                      np.where(f % HD < half, -1.0, 1.0)], 1).astype(np.float32)
    table_dram = nc.inline_tensor(table, "rope_table")
    w_dram = A["attn_w_in"][0].rearrange("(p k) (g s n) -> p k g s n", k=KT, g=GROUPS, s=3)
    wo_dram = A["attn_w_out"][0].rearrange("(k p) n -> p k n", p=P)
    chunks = [(g, s) for g in range(GROUPS) for s in (2, 0, 1)]

    with nc.Block() as block:
        @block.sync
        def _(sp):
            with sp.Fori(0, QUADS) as i:
                for n, (g, s) in enumerate(chunks):
                    sp.wait_ge(proj_done, NPROJ * i + 2 * n + 2)
                    sp.sem_inc(turn_seen, 1)
                    sp.dma_start(w[:, n % SLOTS], w_dram[:, :, g, s, bass.ds(i * QF, QF)]).then_inc(w_in[n % SLOTS], 16)
            for n in range(4):
                if n < SLOTS:
                    sp.wait_ge(proj_done, NPROJ * QUADS + 2 * n + 2)
                else:
                    sp.wait_ge(y_done, TT * (n - SLOTS + 1))
                sp.dma_start(w[:, n % SLOTS], wo_dram[:, :, n * QF:(n + 1) * QF]).then_inc(w_in[n % SLOTS], 16)
            if y_rows is not None:
                sp.wait_ge(cleared, 16)

        @block.scalar
        def _(act):
            act.dma_start(pos[:], A["positions"][0].rearrange("(a n) -> a n", a=1).partition_broadcast(P)).then_inc(tables_in, 16)
            act.dma_start(freq[:], table_dram.ap()).then_inc(tables_in, 16)
            act.wait_ge(angle_ready, 2)
            nc.scalar.activation(sin[:], raw[:, 0], ACT.Sin).then_inc(sin_ready, 1)
            nc.scalar.activation(cos[:], raw[:, 1], ACT.Sin, scale=-1.0, bias=halfpi[:]).then_inc(sin_ready, 1)
            act.sem_inc(proj_free, 2)
            act.sem_inc(pT_ready, 1)
            if y_rows is not None:
                act.wait_ge(zero_ready, 1)
                to = y_rows[NE * CAP:].rearrange("(p b) (n d) -> p (b n) d", p=P, d=SEQ)
                act.dma_start(to, zero[:].broadcast_to(list(to.shape))).then_inc(cleared, 16)
            with act.Fori(0, QUADS) as i:
                n = m = 0
                for g, s in chunks:
                    for half_ in range(2):
                        act.wait_ge(proj_done, NPROJ * i + n + 1 + PC)
                        if s == 2:
                            nc.scalar.copy(v[:, g, 2 * half_:2 * half_ + 2, :],
                                           proj[n % 2][:].rearrange("p (t f) -> p t f", f=QF)).then_inc(proj_free, 1)
                        else:
                            act.wait_ge(rot_done, NROT * i + m + 1)
                            nc.scalar.copy(raw[:, m % 2], proj[n % 2][:]).then_inc(proj_free, 1)
                            act.wait_ge(proj_free, NPROJ * i + n + 3)
                            for d in range(4):
                                e = d ^ 1
                                act.dma_start(swp[32 * d:32 * d + 32, m % 2], raw[32 * e:32 * e + 32, m % 2])\
                                   .then_inc(swp_in[m % 2], 16)
                            m += 1
                        n += 1
                for step in range(UNITS + 1):
                    u = step - 1
                    if u >= 0:
                        act.wait_ge(tp_done, UNITS * i + u + 3)
                        act.wait_ge(pv_done, UNITS * i + u + 1)
                        nc.scalar.copy(probT[:, u % 2], tp[:, 0:6].rearrange("p b q -> p (b q)")).then_inc(pT_ready, 1)
                    u = step
                    if u < UNITS:
                        act.wait_ge(bias_ready, UNITS * i + u + 1)
                        act.wait_ge(tp_done, UNITS * i + u + 1)
                        nc.scalar.activation(prob[:, u % 2], sm[:, u % 2], ACT.Exp, bias=bias[:, u % 2:u % 2 + 1],
                                             scale=HD ** -0.5, accum_out=den[:, u % 4:u % 4 + 1]).then_inc(p_ready, 1)

        @block.gpsimd
        def _(pool):
            ch = Chain(pool, pool_step)
            ch.do(pool.iota(diff[:], pattern=[[-1, P]], base=P, channel_multiplier=1))
            ch.do(pool.memset(mask[:, :, 0:SEQ + P], 0.0))
            ch.sync()
            pool.sem_inc(diff_ready, 1)
            pool.wait_ge(parity_ready, 1)
            for t in range(2):
                m = mask[:, 0, SEQ + t * P:SEQ + (t + 1) * P]
                ch.do(pool.affine_select(out=m, in_=m, compare_op=ALU.is_ge, fill=NEG, base=0,
                                         pattern=[[-1, P]], channel_multiplier=1))
            ch.sync()
            for r in range(RES):
                m = mask[:, r, 0:SEQ]
                if r:
                    ch.do(pool.tensor_copy(mask[:, r, SEQ:KEYS], mask[:, 0, SEQ:KEYS]))
                ch.do(pool.affine_select(out=m, in_=m, compare_op=ALU.is_ge, fill=NEG, base=r,
                                         pattern=[[-1, SEQ]], channel_multiplier=RES))
                ch.sync()
                pool.affine_select(out=m, in_=m, compare_op=ALU.is_ge, fill=NEG, base=WINDOW0 - r,
                                   pattern=[[1, SEQ]], channel_multiplier=-RES).then_inc(mask_ready, 1)
            pool.wait_ge(mask_ready, RES)

        @block.vector
        def _(dve):
            dve.sem_inc(rot_done, 2)
            dve.sem_inc(sm_ready, 1)
            dve.sem_inc(o_ready, 1)
            ch = Chain(dve, dve_step)
            nc.vector.memset(zero[:], 0.0).then_inc(zero_ready, 1)
            ch.do(nc.vector.memset(q[:], 0.0))
            ch.do(nc.vector.memset(halfpi[:], float(np.pi / 2)))
            dve.wait_ge(pool_step, 2)
            ch.do(nc.vector.tensor_single_scalar(diff[:], diff[:], 3, ALU.bitwise_and))
            ch.sync()
            nc.vector.tensor_scalar(mask[:, 0, SEQ + P:KEYS], diff[:], 0.0, NEG, ALU.not_equal, ALU.mult).then_inc(parity_ready, 1)
            dve.wait_ge(tables_in, 32)
            ang, turns, rest = raw[:, 1], swp[:, 0], raw[:, 0]
            ch.do(nc.vector.tensor_scalar(ang, pos[:], freq[:, 0:1], None, ALU.mult))
            ch.sync()
            ch.do(nc.vector.tensor_scalar(turns, ang, float(1 / (2 * np.pi)), ROUND, ALU.mult, ALU.add))
            ch.sync()
            ch.do(nc.vector.tensor_scalar(turns, turns, ROUND, None, ALU.subtract))
            ch.sync()
            for part, src in ((C1, ang), (C2, rest), (C3, rest)):
                ch.do(nc.vector.scalar_tensor_tensor(out=rest, in0=turns, scalar=-part, in1=src, op0=ALU.mult, op1=ALU.add))
                ch.sync()
            lim = 3.1415925
            nc.vector.tensor_scalar(rest, rest, lim, -lim, ALU.min, ALU.max).then_inc(angle_ready, 1)
            dve.wait_ge(angle_ready, 1)
            nc.vector.scalar_tensor_tensor(out=ang, in0=rest, scalar=-1.0, in1=rest, op0=ALU.mult, op1=ALU.max).then_inc(angle_ready, 1)
            dve.wait_ge(sin_ready, 2)
            ch.do(nc.vector.tensor_scalar(sin[:], sin[:], freq[:, 1:2], None, ALU.mult))
            dve.wait_ge(mask_ready, RES)
            ch.sync()
            first = ch.n

            with dve.Fori(0, QUADS) as i:
                ch = Chain(dve, dve_step, DVE_T * i + first)
                m = 0
                for g in range(GROUPS):
                    for s in range(2):
                        for pair in range(2):
                            dve.wait_ge(proj_free, NPROJ * i + 2 * 3 * g + 2 * (s + 1) + pair + 3)
                            ch.do(nc.vector.tensor_tensor(rot[:, 0], raw[:, m % 2], cos[:], ALU.mult))
                            dve.wait_ge(swp_in[m % 2], 64 * (NROT // 2) * i + 64 * (m // 2 + 1))
                            ch.do(nc.vector.tensor_tensor(rot[:, 1], swp[:, m % 2], sin[:], ALU.mult))
                            ch.sync()
                            a = rot[:, 0].rearrange("p (j r) -> p j r", r=RES)
                            b = rot[:, 1].rearrange("p (j r) -> p j r", r=RES)
                            if s == 0:
                                for hh in range(2):
                                    rows = slice(HD * hh, HD * hh + HD)
                                    to = q[rows, g, pair, hh].rearrange("p (r j) -> p j r", r=RES)
                                    ins = nc.vector.tensor_tensor(to, a[rows], b[rows], ALU.add)
                                    if hh == 0:
                                        ch.do(ins)
                            else:
                                to = k[:, g, pair]
                                if g == 0:
                                    ins = nc.vector.tensor_tensor(to, rot[:, 0], rot[:, 1], ALU.add)
                                else:
                                    ins = nc.vector.tensor_tensor(to.rearrange("p (r j) -> p j r", r=RES), a, b, ALU.add)
                            ins.then_inc(rot_done, 1)
                            dve.wait_ge(rot_done, NROT * i + m + 3)
                            m += 1
                for step in range(UNITS + 4):
                    u = step
                    if u < UNITS:
                        r = u // 2 % RES
                        if u:
                            dve.wait_ge(mask_ready, RES)
                        dve.wait_ge(sc_done, UNITS * i + u + 1)
                        dve.wait_ge(p_ready, UNITS * i + u + 1)
                        if u == 0:
                            dve.sem_inc(turn_seen, 1)
                        nc.vector.tensor_tensor_reduce(sm[:, u % 2], sc[:, 0:KEYS], mask[:, r], 1.0, -3e38,
                                                       ALU.add, ALU.max, top[:, u % 2:u % 2 + 1]).then_inc(sm_ready, 1)
                        dve.wait_ge(sm_ready, UNITS * i + u + 2)
                        nc.vector.tensor_scalar(bias[:, u % 2:u % 2 + 1], top[:, u % 2:u % 2 + 1], -HD ** -0.5, None,
                                                ALU.mult).then_inc(bias_ready, 1)
                    u = step - 2
                    if 0 <= u < UNITS:
                        hh, slot = u % 2, u // 2 % 2
                        dve.wait_ge(p_ready, UNITS * i + u + 3)
                        ch.do(nc.vector.reciprocal(rden[:, u % 4:u % 4 + 1], den[:, u % 4:u % 4 + 1]))
                        dve.wait_ge(pv_done, UNITS * i + u + 3)
                        ch.sync()
                        nc.vector.tensor_scalar(o[:, slot, HD * hh:HD * hh + HD], pv[:, HD * hh:HD * hh + HD],
                                                rden[:, u % 4:u % 4 + 1], None, ALU.mult).then_inc(o_ready, 1)
                    u = step - 3
                    if u >= 0 and u % 2:
                        pair, r = u // 8, u // 2 % RES
                        dve.wait_ge(oT_done, UNITS // 2 * i + u // 2 + 1)
                        nc.vector.tensor_scalar(oT[:, bass.ds(2 * i + pair, 1), r::RES].rearrange("p a q -> p (a q)"),
                                                po[:, 0:P], 1.0, None, ALU.mult).then_inc(oT_ready, 1)
                assert DVE_T == ch.n, ch.n
            out = Chain(dve, dve_step, DVE_T * QUADS + first)
            for n in range(4):
                for t in range(TT):
                    j = n * TT + t
                    cols = slice(n * QF, (n + 1) * QF)
                    dve.wait_ge(y_done, j + 1)
                    nc.vector.tensor_tensor(rot[:, j % 2, 0:QF], proj[j % 2][:, 0:QF], c.ada[:, 2, cols], ALU.mult).then_inc(y_used, 1)
                    dve.wait_ge(y_used, j + 1)
                    out.do(nc.vector.scalar_tensor_tensor(out=c.x[:, t, cols], in0=c.x[:, t, cols], scalar=ALPHA,
                                                          in1=rot[:, j % 2, 0:QF], op0=ALU.mult, op1=ALU.add))
                    out.sync()

        @block.tensor
        def _(pe):
            pe.sem_inc(proj_done, PC)
            pe.sem_inc(tp_done, 2)
            pe.sem_inc(pv_done, 2)
            pe.sem_inc(p_ready, 2)
            with pe.Fori(0, QUADS) as i:
                n = 0
                for j, (g, s) in enumerate(chunks):
                    pe.wait_ge(w_in[j % SLOTS], 16 * (CH // SLOTS) * i + 16 * (j // SLOTS + 1))
                    for half_ in range(2):
                        pe.wait_ge(proj_free, NPROJ * i + n + 1)
                        if s == 2:
                            for t in range(2 * half_, 2 * half_ + 2):
                                toks = slice(t * P, (t + 1) * P) if g == 0 else slice(t, SEQ, RES)
                                for kk in range(KT):
                                    last = nc.tensor.matmul(proj[n % 2][:, t % 2 * QF:(t % 2 + 1) * QF],
                                                            c.hT[:, kk, toks], w[:, j % SLOTS, kk], start=kk == 0, stop=kk == KT - 1)
                        else:
                            for kk in range(KT):
                                last = nc.tensor.matmul(proj[n % 2][:], w[:, j % SLOTS, kk, half_ * P:(half_ + 1) * P],
                                                        c.hT[:, kk, :], start=kk == 0, stop=kk == KT - 1)
                        last.then_inc(proj_done, 1)
                        n += 1
                for step in range(UNITS + 4):
                    u = step
                    if u < UNITS:
                        pair, r, hh = u // 8, u // 2 % RES, u % 2
                        if u == 0:
                            pe.wait_ge(rot_done, NROT * (i + 1) + 2)
                        pe.wait_ge(sm_ready, UNITS * i + u + 1)
                        qs = [q[:, g, pair, hh, r * P:(r + 1) * P] for g in range(GROUPS)]
                        nc.tensor.matmul(sc[:, 0:SEQ], qs[0], k[:, 0, pair], start=True, stop=True)
                        for g in (1, 2):
                            last = nc.tensor.matmul(sc[:, SEQ + (g - 1) * P:SEQ + g * P], qs[g],
                                                    k[:, g, pair, r * P:(r + 1) * P], start=True, stop=True)
                        last.then_inc(sc_done, 1)
                    u = step - 1
                    if 0 <= u < UNITS:
                        pe.wait_ge(p_ready, UNITS * i + u + 3)
                        pe.wait_ge(pT_ready, UNITS * i + u + 1)
                        for b in range(6):
                            last = nc.tensor.transpose(tp[:, b], prob[:, u % 2, b * P:(b + 1) * P], c.ident[:])
                        last.then_inc(tp_done, 1)
                    u = step - 2
                    if 0 <= u < UNITS:
                        pair, r = u // 8, u // 2 % RES
                        pe.wait_ge(pT_ready, UNITS * i + u + 2)
                        pe.wait_ge(o_ready, UNITS * i + u + 1)
                        for b in range(6):
                            g, t = (0, b) if b < 4 else (b - 3, r)
                            last = nc.tensor.matmul(pv[:, 0:P], probT[:, u % 2, b * P:(b + 1) * P],
                                                    v[:, g, t, pair * P:(pair + 1) * P], start=b == 0, stop=b == 5)
                        last.then_inc(pv_done, 1)
                    u = step - 3
                    if u >= 0 and u % 2:
                        pe.wait_ge(o_ready, UNITS * i + u + 2)
                        if u > 1:
                            pe.wait_ge(oT_ready, UNITS // 2 * i + u // 2)
                        nc.tensor.transpose(po[:, 0:P], o[:, u // 2 % 2], c.ident[:]).then_inc(oT_done, 1)
                pe.wait_ge(oT_ready, UNITS // 2 * (i + 1))
            for n in range(4):
                pe.wait_ge(w_in[n % SLOTS], 16 * (CH // SLOTS) * QUADS + 16 * (n // SLOTS + 1))
                for t in range(TT):
                    j = n * TT + t
                    if j >= 2:
                        pe.wait_ge(y_used, j - 1)
                    for kk in range(KT):
                        last = nc.tensor.matmul(proj[j % 2][:, 0:QF], oT[:, kk, t * P:(t + 1) * P], w[:, n % SLOTS, kk],
                                                start=kk == 0, stop=kk == KT - 1)
                    last.then_inc(y_done, 1)
    st.close()


def moe_stage(nc, c, A, l, h_rows, y_rows):
    st = Stage(nc, f"moe{l}")
    NEP = NE + 4
    BIG = 1e5
    PICKED = 1e30
    F2 = 2 * ED

    w13 = st.sb("w13", [P, 2, 2, KT, ED])
    w2 = st.sb("w2", [P, 2, 2, D])
    xg = st.sb("xg", [P, 2, D])
    xT = st.sb("xT", [P, 2, KT, P])
    act_s = st.sb("act_s", [P, 2, F2])
    hh = st.sb("hh", [P, 2, ED])
    hT2 = st.sb("hT2", [P, 2, 2, P])
    ysb = st.sb("ysb", [P, 2, D])
    acc = st.sb("acc", [P, TT, D])
    rw = st.sb("rw", [P, KT, NE])
    rb = st.sb("rb", [P, NE])
    lgT = st.sb("lgT", [NE, SEQ])
    sg = st.sb("sg", [P, TT, NE])
    biased = st.sb("biased", [P, TT, NE])
    g8 = st.sb("g8", [P, TT, NG, 8])
    gpad = st.sb("gpad", [P, TT, 16])
    grep = st.sb("grep", [P, TT, 8])
    gm = st.sb("gm", [P, TT, 16])
    v8 = st.sb("v8", [P, TT, 8])
    e8 = st.sb("e8", [P, TT, 8], U32)
    e8f = st.sb("e8f", [P, TT, 8])
    left = st.sb("left", [P, TT, NE])
    sel = st.sb("sel", [P, TT, NE], BF16)
    hot = st.sb("hot", [P, TOPK, NE])
    picked = st.sb("picked", [P, TOPK, NE])
    gate = st.sb("gate", [P, TT, TOPK])
    gsum = st.sb("gsum", [P, TT])
    pos = st.sb("pos", [P, TT, NEP])
    row = st.sb("row", [P, TT, NE])
    rowk = st.sb("rowk", [P, TT, TOPK], U32)
    cnt = st.sb("cnt", [P, NE])
    nov = st.sb("nov", [P, NE])
    incl = st.sb("incl", [P, NE])
    shift = st.sb("shift", [P, NE])
    ind = st.sb("ind", [P, OVB, NE])
    ovf = st.sb("ovf", [P, 2, OVB])
    ovi = st.sb("ovi", [1, OVB + 1], I32)
    ii = st.sb("ii", [P, P], I32)
    iota = st.sb("iota", [P, P])
    pidx = st.sb("pidx", [P, TT, 2], I32)
    tok = st.sb("tok", [P, TT, 2], BF16)
    onesb = st.sb("onesb", [P, P], BF16)
    before = st.sb("before", [P, P], BF16)
    onehot = st.sb("onehot", [P, 2, TT, P], BF16)
    pcol = st.sb("pcol", [P, TT])
    idx = st.sb("idx", [P, 2], U32)

    ph = st.ps("ph", [P, 512])
    tx = [st.ps(f"tx{n}", [P, 4, P]) for n in range(2)]
    th = st.ps("th", [P, 2, P])
    py = [st.ps(f"py{n}", [P, 512]) for n in range(2)]
    pr = st.ps("pr", [P, 512])
    pi = st.ps("pi", [P, 512])

    sem = st.sem
    small_in, consts = sem("small_in"), sem("consts")
    sh_in, sh_h, sh_silu, sh_hh, sh_th, sh_hT, sh_y, sh_acc = [sem("sh_" + x) for x in "in h silu hh th hT y acc".split()]
    lg_done, lg_ready, lg_turned, sg_ready = sem("lg_done"), sem("lg_ready"), sem("lg_turned"), sem("sg_ready")
    dve_step, iota_ready, sel_ready, pos_done, route_ready = (sem("dve_step"), sem("iota_ready"), sem("sel_ready"),
                                                              sem("pos_done"), sem("route_ready"))
    w13_in = [sem(f"w13_in{n}") for n in range(2)]
    w2_in = [sem(f"w2_in{n}") for n in range(2)]
    xg_in, ov_xg_in = [sem(f"xg_in{n}") for n in range(2)], sem("ov_xg_in")
    y_out = [sem(f"y_out{n}") for n in range(2)]
    hot_ready, idx_done, idx_ready, gathering = sem("hot_ready"), sem("idx_done"), sem("idx_ready"), sem("gathering")
    tx_done, xT_act, xT_dve = sem("tx_done"), sem("xT_act"), sem("xT_dve")
    h_done, silu_ready, hh_ready, th_done, hT_ready = (sem("h_done"), sem("silu_ready"), sem("hh_ready"), sem("th_done"),
                                                       sem("hT_ready"))
    y_done, y_ready = sem("y_done"), sem("y_ready")
    ov = {x: sem("ov_" + x) for x in
          "w pcol hot idxp idx tx xTa xTd h silu hh th hT y ysb out turn".split()}
    yg_in = [sem(f"yg_in{n}") for n in range(NYG)]
    yg_used = sem("yg_used")
    yg = w13[:].rearrange("p s a k e -> p (s a k e)").rearrange("p (n d) -> p n d", d=D)

    def w13_src(wt):
        return wt.rearrange("(p k) n -> p k n", k=KT)

    def flat(ap):
        return ap.rearrange("p k n -> p (k n)")

    w1d = A["expert_w1"][l].rearrange("e (p k) n -> p e (k n)", k=KT)
    w3d = A["expert_w3"][l].rearrange("e (p k) n -> p e (k n)", k=KT)
    w2d = A["expert_w2"][l].rearrange("e (p k) n -> p e (k n)", k=2)

    def w13_slot(b, a):
        return w13[:, b, a].rearrange("p k n -> p (k n)")

    def w2_slot(b):
        return w2[:, b].rearrange("p k n -> p (k n)")

    ys = y_rows.rearrange("(b p) d -> p b d", p=P)

    with nc.Block() as block:
        @block.sync
        def _(sp):
            sp.dma_start(rw[:], A["router_w"][l].rearrange("(p k) n -> p k n", k=KT)).then_inc(small_in, 16)
            sp.dma_start(rb[:], A["router_bias"][l].rearrange("(a n) -> a n", a=1).partition_broadcast(P)).then_inc(small_in, 16)
            for a, name in enumerate(("shared_w1", "shared_w3")):
                sp.dma_start(w13_slot(0, a), flat(w13_src(A[name][l]))).then_inc(sh_in, 16)
            sp.dma_start(w2_slot(0), A["shared_w2"][l].rearrange("(p k) n -> p (k n)", k=2)).then_inc(sh_in, 16)
            sp.wait_ge(sh_h, TT)
            sp.wait_ge(sh_y, TT)
            with sp.Fori(0, NE // 2) as i:
                for b in range(2):
                    e = 2 * i + b
                    sp.wait_ge(h_done, 2 * i + b + 1)
                    sp.sem_inc(gathering, 1)
                    sp.dma_start(w13_slot(b, 0), w1d[:, bass.ds(e, 1)].rearrange("p a n -> p (a n)")).then_inc(w13_in[b], 16)
                    sp.dma_start(w13_slot(b, 1), w3d[:, bass.ds(e, 1)].rearrange("p a n -> p (a n)")).then_inc(w13_in[b], 16)
                    sp.wait_ge(y_done, 2 * i + b + 1)
                    sp.sem_inc(gathering, 1)
                    sp.dma_start(w2_slot(b), w2d[:, bass.ds(e, 1)].rearrange("p a n -> p (a n)")).then_inc(w2_in[b], 16)
            sp.wait_ge(y_done, NE + 2)
            sp.wait_ge(route_ready, 1)
            total = sp.value_load(ovi[0:1, OVB:OVB + 1], min_val=0, max_val=OVB)
            with sp.Fori(0, OVB) as j:
                with sp.If(j < total):
                    e = sp.value_load(ovi[0:1, bass.ds(j, 1)], min_val=0, max_val=NE - 1)
                    sp.dma_start(w13_slot(0, 0), w1d[:, bass.ds(e, 1)].rearrange("p a n -> p (a n)")).then_inc(ov["w"], 16)
                    sp.dma_start(w13_slot(0, 1), w3d[:, bass.ds(e, 1)].rearrange("p a n -> p (a n)")).then_inc(ov["w"], 16)
                    sp.dma_start(w2_slot(0), w2d[:, bass.ds(e, 1)].rearrange("p a n -> p (a n)")).then_inc(ov["w"], 16)
                    sp.wait_ge(ov["out"], 16 * j + 16)
                    sp.sem_inc(ov["turn"], 1)

        @block.scalar
        def _(act):
            act.wait_ge(lg_done, 1)
            nc.scalar.copy(lgT[:], pr[0:NE, :]).then_inc(lg_ready, 1)
            act.wait_ge(lg_turned, 1)
            nc.scalar.activation(sg[:], pi[:, 0:TT * NE].rearrange("p (t e) -> p t e", e=NE), ACT.Sigmoid).then_inc(sg_ready, 1)
            for t in range(TT):
                act.wait_ge(sh_h, t + 1)
                if t >= 2:
                    act.wait_ge(sh_hh, t - 1)
                nc.scalar.activation(act_s[:, t % 2, 0:ED], ph[:, 0:ED], ACT.Silu).then_inc(sh_silu, 1)
                nc.scalar.copy(act_s[:, t % 2, ED:F2], ph[:, ED:F2]).then_inc(sh_silu, 1)
                act.wait_ge(sh_th, t + 1)
                nc.scalar.copy(hT2[:, t % 2], th[:]).then_inc(sh_hT, 1)
                for n in range(2):
                    act.wait_ge(sh_y, t + 1)
                    nc.scalar.copy(acc[:, t, n * 512:(n + 1) * 512], py[n][:]).then_inc(sh_acc, 1)
            act.wait_ge(tx_done, 1)
            nc.scalar.copy(xT[:, 0, 0:4], tx[0][:]).then_inc(xT_act, 1)
            act.sem_inc(y_ready, 1)
            act.sem_inc(y_out[0], 16)
            act.sem_inc(y_out[1], 16)
            with act.Fori(0, NE // 2) as i:
                for b in range(2):
                    act.wait_ge(h_done, 2 * i + b + 3)
                    nc.scalar.activation(act_s[:, b, 0:ED], ph[:, 0:ED], ACT.Silu).then_inc(silu_ready, 1)
                    act.wait_ge(tx_done, 4 * i + 2 * b + 4)
                    nc.scalar.copy(xT[:, 1 - b, 0:4], tx[0][:]).then_inc(xT_act, 1)
                    act.wait_ge(th_done, 2 * i + b + 1)
                    nc.scalar.copy(hT2[:, b], th[:]).then_inc(hT_ready, 1)
                    act.wait_ge(y_out[b], 16 * i + 16)
                    act.wait_ge(y_done, 2 * i + b + 3)
                    for n in range(2):
                        nc.scalar.copy(ysb[:, b, n * 512:(n + 1) * 512], py[n][:]).then_inc(y_ready, 1)
                    act.wait_ge(y_ready, 4 * i + 2 * b + 3)
                    act.dma_start(ys[:, bass.ds(2 * i + b, 1)].rearrange("p a d -> p (a d)"), ysb[:, b]).then_inc(y_out[b], 16)
            act.wait_ge(y_out[0], 16 * (NE // 2) + 16)
            act.wait_ge(y_out[1], 16 * (NE // 2) + 16)
            total = act.value_load(ovi[0:1, OVB:OVB + 1], min_val=0, max_val=OVB)
            with act.Fori(0, OVB) as j:
                with act.If(j < total):
                    act.wait_ge(ov["tx"], 2 * j + 2)
                    nc.scalar.copy(xT[:, 0, 0:4], tx[0][:]).then_inc(ov["xTa"], 1)
                    act.wait_ge(ov["h"], j + 1)
                    nc.scalar.activation(act_s[:, 0, 0:ED], ph[:, 0:ED], ACT.Silu).then_inc(ov["silu"], 1)
                    act.wait_ge(ov["th"], j + 1)
                    nc.scalar.copy(hT2[:, 0], th[:]).then_inc(ov["hT"], 1)
                    act.wait_ge(ov["y"], j + 1)
                    for n in range(2):
                        nc.scalar.copy(ysb[:, 0, n * 512:(n + 1) * 512], py[n][:]).then_inc(ov["ysb"], 1)
                    act.wait_ge(ov["ysb"], 2 * j + 2)
                    act.dma_start(ys[:, bass.ds(j + NE, 1)].rearrange("p a d -> p (a d)"), ysb[:, 0]).then_inc(ov["out"], 16)
                    act.wait_ge(ov["out"], 16 * j + 16)
                    act.sem_inc(ov["turn"], 1)

        @block.gpsimd
        def _(pool):
            pool.iota(ii[:], pattern=[[1, P]], base=0, channel_multiplier=0).then_inc(iota_ready, 1)
            pool.iota(pidx[:, :, 0], pattern=[[P, TT]], base=0, channel_multiplier=0).then_inc(iota_ready, 1)
            pool.iota(pidx[:, :, 1], pattern=[[0, TT]], base=0, channel_multiplier=1).then_inc(iota_ready, 1)
            pool.memset(before[:], 1.0).then_inc(iota_ready, 1)
            pool.wait_ge(iota_ready, 4)
            pool.affine_select(out=before[:], in_=before[:], compare_op=ALU.is_gt, fill=0.0, base=0,
                               pattern=[[1, P]], channel_multiplier=-1).then_inc(iota_ready, 1)
            for t in range(TT):
                pool.wait_ge(sh_silu, 2 * t + 2)
                if t >= 2:
                    pool.wait_ge(sh_th, t - 1)
                pool.tensor_tensor(hh[:, t % 2], act_s[:, t % 2, 0:ED], act_s[:, t % 2, ED:F2], ALU.mult).then_inc(sh_hh, 1)
            for b in range(2):
                pool.wait_ge(idx_ready, b + 1)
                pool.indirect_dma_start(xg[:, b], None, h_rows, bass.IndirectOffsetOnAxis(ap=idx[:, b:b + 1], axis=0))\
                    .then_inc(xg_in[b], 16)
            with pool.Fori(0, NE // 2) as i:
                for b in range(2):
                    pool.wait_ge(idx_ready, 2 * i + b + 3)
                    pool.wait_ge(tx_done, 4 * i + 2 * b + 2)
                    pool.sem_inc(gathering, 1)
                    pool.indirect_dma_start(xg[:, b], None, h_rows, bass.IndirectOffsetOnAxis(ap=idx[:, b:b + 1], axis=0))\
                        .then_inc(xg_in[b], 16)
            pool.wait_ge(xg_in[0], 16 * (NE // 2 + 1))
            pool.wait_ge(xg_in[1], 16 * (NE // 2 + 1))
            total = pool.value_load(ovi[0:1, OVB:OVB + 1], min_val=0, max_val=OVB)
            with pool.Fori(0, OVB) as j:
                with pool.If(j < total):
                    pool.wait_ge(ov["idx"], j + 1)
                    pool.sem_inc(gathering, 1)
                    pool.indirect_dma_start(xg[:, 0], None, h_rows, bass.IndirectOffsetOnAxis(ap=idx[:, 0:1], axis=0))\
                        .then_inc(ov_xg_in, 16)
                    pool.wait_ge(ov["out"], 16 * j + 16)
                    pool.sem_inc(ov["turn"], 1)
            pool.wait_ge(y_out[0], 16 * (NE // 2) + 16)
            pool.wait_ge(y_out[1], 16 * (NE // 2) + 16)
            pool.wait_ge(y_done, NE + 2)
            for t in range(TT):
                for k in range(TOPK):
                    n = t * TOPK + k
                    if n >= NYG:
                        pool.wait_ge(yg_used, n - NYG + 1)
                    pool.indirect_dma_start(yg[:, n % NYG], None, y_rows,
                                            bass.IndirectOffsetOnAxis(ap=rowk[:, t, k:k + 1], axis=0)).then_inc(yg_in[n % NYG], 16)

        @block.vector
        def _(dve):
            ch = Chain(dve, dve_step)
            dve.wait_ge(iota_ready, 5)
            ch.do(nc.vector.tensor_copy(iota[:], ii[:]))
            nc.vector.tensor_copy(tok[:], pidx[:]).then_inc(consts, 1)
            nc.vector.memset(onesb[:], 1.0).then_inc(consts, 1)
            ch.do(nc.vector.memset(gpad[:], NEG))
            ch.do(nc.vector.memset(grep[:], NEG))
            ch.do(nc.vector.memset(pos[:], BIG))
            dve.wait_ge(small_in, 32)
            dve.wait_ge(sg_ready, 1)
            rbb = rb[:].rearrange("p (a n) -> p a n", a=1).broadcast_to([P, TT, NE])
            ch.do(nc.vector.tensor_tensor(biased[:], sg[:], rbb, ALU.add))
            ch.sync()
            for t in range(TT):
                for g in range(NG):
                    ch.do(nc.vector.max(g8[:, t, g], biased[:, t, g * 8:(g + 1) * 8]))
            ch.sync()
            ch.do(nc.vector.tensor_tensor(gpad[:, :, 0:NG], g8[:, :, :, 0], g8[:, :, :, 1], ALU.add))
            ch.sync()
            for t in range(TT):
                ch.do(nc.vector.max(v8[:, t], gpad[:, t, 0:NG]))
            ch.sync()
            ch.do(nc.vector.tensor_copy(grep[:, :, 0:TOPG], v8[:, :, 0:TOPG]))
            ch.sync()
            for t in range(TT):
                ch.do(nc.vector.match_replace(gm[:, t], grep[:, t], gpad[:, t], PICKED))
            ch.sync()
            ch.do(nc.vector.tensor_scalar(gm[:], gm[:], PICKED, NEG, ALU.not_equal, ALU.mult))
            ch.sync()
            gmb = gm[:, :, 0:NG].rearrange("p t (g o) -> p t g o", o=1).broadcast_to([P, TT, NG, 8])
            ch.do(nc.vector.tensor_tensor(biased[:].rearrange("p t (g e) -> p t g e", e=8),
                                          biased[:].rearrange("p t (g e) -> p t g e", e=8), gmb, ALU.add))
            ch.sync()
            for t in range(TT):
                ch.do(nc.vector.max(v8[:, t], biased[:, t]))
            ch.sync()
            for t in range(TT):
                ch.do(nc.vector.max_index(e8[:, t], v8[:, t], biased[:, t]))
                ch.do(nc.vector.match_replace(left[:, t], v8[:, t], biased[:, t], PICKED))
            ch.sync()
            nc.vector.tensor_scalar(sel[:], left[:], PICKED, None, ALU.is_equal).then_inc(sel_ready, 1)
            ch.do(nc.vector.tensor_copy(e8f[:], e8[:]))
            dve.wait_ge(sel_ready, 1)
            dve.wait_ge(pos_done, 1)
            ch.do(nc.vector.tensor_copy(cnt[:], pr[:, TT * NE:(TT + 1) * NE]))
            ch.sync()
            ch.do(nc.vector.tensor_scalar(nov[:], cnt[:], float(CAP), None, ALU.is_gt))
            ch.sync()
            for n in range(2, SEQ // CAP):
                ch.do(nc.vector.scalar_tensor_tensor(out=nov[:], in0=cnt[:], scalar=float(n * CAP), in1=nov[:],
                                                     op0=ALU.is_gt, op1=ALU.add))
                ch.sync()
            ch.do(nc.vector.tensor_tensor_scan(incl[:], c.ones[:, 0:NE], nov[:], 0.0, ALU.mult, ALU.add))
            ch.sync()
            ch.do(nc.vector.tensor_tensor(shift[:], incl[:], nov[:], ALU.subtract))
            ch.sync()
            ch.do(nc.vector.tensor_tensor(shift[:], shift[:], iota[:, 0:NE], ALU.subtract))
            ch.sync()
            ch.do(nc.vector.tensor_scalar(shift[:], shift[:], float(CAP), float((NE - 1) * CAP), ALU.mult, ALU.add))
            prt = pr[:, 0:TT * NE].rearrange("p (t e) -> p t e", e=NE)
            ch.do(nc.vector.tensor_scalar(row[:], prt, float(CAP), None, ALU.is_ge))
            ch.sync()

            def over_tiles(ap):
                return ap.rearrange("p (a n) -> p a n", a=1).broadcast_to([P, TT, NE])

            ch.do(nc.vector.tensor_tensor(row[:], row[:], over_tiles(shift[:]), ALU.mult))
            ch.sync()
            ch.do(nc.vector.tensor_tensor(row[:], row[:], prt, ALU.add))
            ch.sync()
            ch.do(nc.vector.scalar_tensor_tensor(out=row[:], in0=over_tiles(iota[:, 0:NE]), scalar=float(CAP), in1=row[:],
                                                 op0=ALU.mult, op1=ALU.add))
            ch.do(nc.vector.tensor_scalar(left[:], sel[:], -BIG, BIG, ALU.mult, ALU.add))
            ch.sync()
            nc.vector.tensor_tensor(pos[:, :, 0:NE], left[:], prt, ALU.add).then_inc(hot_ready, 1)
            dve.wait_ge(hot_ready, 1)

            def one_hot(col, b):
                return nc.vector.tensor_tensor(onehot[:, b], iota[:].rearrange("p (a n) -> p a n", a=1).broadcast_to([P, TT, P]),
                                               col.broadcast_to([P, TT, P]), ALU.is_equal)

            def number(b):
                with nc.allow_low_precision(reason="sums of small integers"):
                    return nc.vector.tensor_reduce(idx[:, b:b + 1], pi[:, 0:2], AX.X, ALU.add)

            for e in range(3):
                one_hot(pos[:, :, e:e + 1], e % 2).then_inc(hot_ready, 1)
                dve.wait_ge(idx_done, e + 1)
                if e == 2:
                    dve.wait_ge(xg_in[0], 16)
                number(e % 2).then_inc(idx_ready, 1)
            for t in range(TT):
                ex = e8f[:, t].rearrange("p (k o) -> p k o", o=1).broadcast_to([P, TOPK, NE])
                ch.do(nc.vector.tensor_tensor(hot[:], iota[:, 0:NE].rearrange("p (a n) -> p a n", a=1).broadcast_to([P, TOPK, NE]),
                                              ex, ALU.is_equal))
                ch.sync()
                for src, dst in ((sg, gate), (row, rowk)):
                    ch.do(nc.vector.tensor_tensor(picked[:], hot[:], src[:, t].rearrange("p (a n) -> p a n", a=1)
                                                  .broadcast_to([P, TOPK, NE]), ALU.mult))
                    ch.sync()
                    with nc.allow_low_precision(reason="the row numbers are integers"):
                        ch.do(nc.vector.tensor_reduce(dst[:, t], picked[:], AX.X, ALU.add))
                    ch.sync()
            ch.do(nc.vector.tensor_reduce(gsum[:], gate[:], AX.X, ALU.add))
            ch.sync()
            ch.do(nc.vector.reciprocal(gsum[:], gsum[:]))
            ch.sync()
            ch.do(nc.vector.scalar_tensor_tensor(out=gate[:], in0=gate[:], scalar=ROUTED_SCALE,
                                                 in1=gsum[:].rearrange("p (t o) -> p t o", o=1).broadcast_to([P, TT, TOPK]),
                                                 op0=ALU.mult, op1=ALU.mult))
            jj = iota[:, 0:OVB].rearrange("p (j o) -> p j o", o=1).broadcast_to([P, OVB, NE])
            ch.do(nc.vector.tensor_tensor(ind[:], incl[:].rearrange("p (a n) -> p a n", a=1).broadcast_to([P, OVB, NE]), jj, ALU.is_le))
            ch.sync()
            ch.do(nc.vector.tensor_reduce(ovf[:, 0], ind[:], AX.X, ALU.add))
            ch.sync()
            ch.do(nc.vector.tensor_tensor(ind[:], ind[:], nov[:].rearrange("p (a n) -> p a n", a=1).broadcast_to([P, OVB, NE]), ALU.mult))
            ch.do(nc.vector.tensor_scalar(ovi[0:1, 0:OVB], ovf[0:1, 0], float(NE - 1), None, ALU.min))
            ch.sync()
            ch.do(nc.vector.tensor_reduce(ovf[:, 1], ind[:], AX.X, ALU.add))
            ch.sync()
            ch.do(nc.vector.tensor_tensor(ovf[:, 1], iota[:, 0:OVB], ovf[:, 1], ALU.subtract))
            ch.sync()
            ch.do(nc.vector.tensor_scalar(ovf[:, 1], ovf[:, 1], float(CAP), float(CAP), ALU.mult, ALU.add))
            ch.sync()
            nc.vector.tensor_copy(ovi[0:1, OVB:OVB + 1], incl[0:1, NE - 1:NE]).then_inc(route_ready, 1)
            dve.wait_ge(route_ready, 1)

            dve.wait_ge(tx_done, 2)
            nc.vector.tensor_copy(xT[:, 0, 4:8], tx[1][:]).then_inc(xT_dve, 1)
            with dve.Fori(0, NE // 2) as i:
                for b in range(2):
                    dve.wait_ge(idx_done, 2 * i + b + 3)
                    one_hot(pos[:, :, bass.ds(2 * i + b + 3, 1)], 1 - b).then_inc(hot_ready, 1)
                    dve.wait_ge(silu_ready, 2 * i + b + 1)
                    nc.vector.tensor_tensor(hh[:, b], act_s[:, b, 0:ED], ph[:, ED:F2], ALU.mult).then_inc(hh_ready, 1)
                    dve.wait_ge(tx_done, 4 * i + 2 * b + 4)
                    nc.vector.tensor_copy(xT[:, 1 - b, 4:8], tx[1][:]).then_inc(xT_dve, 1)
                    dve.wait_ge(idx_done, 2 * i + b + 4)
                    number(1 - b).then_inc(idx_ready, 1)
            total = dve.value_load(ovi[0:1, OVB:OVB + 1], min_val=0, max_val=OVB)
            dve.wait_ge(xg_in[0], 16 * (NE // 2 + 1))
            dve.wait_ge(xg_in[1], 16 * (NE // 2 + 1))
            with dve.Fori(0, OVB) as j:
                with dve.If(j < total):
                    e = dve.value_load(ovi[0:1, bass.ds(j, 1)], min_val=0, max_val=NE - 1)
                    nc.vector.tensor_scalar(pcol[:], pos[:, :, bass.ds(e, 1)].rearrange("p t a -> p (t a)"),
                                            ovf[:, 1, bass.ds(j, 1)], None, ALU.subtract).then_inc(ov["pcol"], 1)
                    dve.wait_ge(ov["pcol"], j + 1)
                    one_hot(pcol[:].rearrange("p (t o) -> p t o", o=1), 0).then_inc(ov["hot"], 1)
                    dve.wait_ge(ov["idxp"], j + 1)
                    number(0).then_inc(ov["idx"], 1)
                    dve.wait_ge(ov["tx"], 2 * j + 2)
                    nc.vector.tensor_copy(xT[:, 0, 4:8], tx[1][:]).then_inc(ov["xTd"], 1)
                    dve.wait_ge(ov["silu"], j + 1)
                    nc.vector.tensor_tensor(hh[:, 0], act_s[:, 0, 0:ED], ph[:, ED:F2], ALU.mult).then_inc(ov["hh"], 1)
                    dve.wait_ge(ov["out"], 16 * j + 16)
                    dve.sem_inc(ov["turn"], 1)
            dve.wait_ge(sh_acc, 2 * TT)
            for t in range(TT):
                for k in range(TOPK):
                    n = t * TOPK + k
                    dve.wait_ge(yg_in[n % NYG], 16 * (n // NYG + 1))
                    nc.vector.scalar_tensor_tensor(out=acc[:, t], in0=yg[:, n % NYG], scalar=gate[:, t, k:k + 1],
                                                   in1=acc[:, t], op0=ALU.mult, op1=ALU.add).then_inc(yg_used, 1)
                    dve.wait_ge(yg_used, n + 1)
                ch.do(nc.vector.tensor_tensor(acc[:, t], acc[:, t], c.ada[:, 2], ALU.mult))
                ch.sync()
                ch.do(nc.vector.scalar_tensor_tensor(out=c.x[:, t], in0=c.x[:, t], scalar=ALPHA, in1=acc[:, t],
                                                     op0=ALU.mult, op1=ALU.add))
            ch.sync()

        @block.tensor
        def _(pe):
            def up(xt, b, done):
                for k in range(KT):
                    last = nc.tensor.matmul(ph[:], xt(k), w13[:, b, :, k], start=k == 0, stop=k == KT - 1)
                last.then_inc(done, 1)

            def turn_h(b, done):
                for k in range(2):
                    last = nc.tensor.transpose(th[:, k], hh[:, b, k::2], c.ident[:])
                last.then_inc(done, 1)

            def down(b, wb, done):
                for n in range(2):
                    for k in range(2):
                        last = nc.tensor.matmul(py[n][:], hT2[:, b, k], w2[:, wb, k, n * 512:(n + 1) * 512],
                                                start=k == 0, stop=k == 1)
                last.then_inc(done, 1)

            def turn_x(b, done):
                for n in range(2):
                    for k in range(4):
                        last = nc.tensor.transpose(tx[n][:, k], xg[:, b, 4 * n + k::KT], c.ident[:])
                    last.then_inc(done, 1)

            def rows(b, done):
                for t in range(TT):
                    last = nc.tensor.matmul(pi[:, 0:2], onehot[:, b, t], tok[:, t], start=t == 0, stop=t == TT - 1)
                last.then_inc(done, 1)

            pe.wait_ge(small_in, 32)
            for k in range(KT):
                last = nc.tensor.matmul(pr[0:NE, :], rw[:, k], c.hT[:, k], start=k == 0, stop=k == KT - 1)
            last.then_inc(lg_done, 1)
            pe.wait_ge(lg_ready, 1)
            for t in range(TT):
                last = nc.tensor.transpose(pi[:, t * NE:(t + 1) * NE], lgT[:, t * P:(t + 1) * P], c.ident[0:NE, 0:NE])
            last.then_inc(lg_turned, 1)
            pe.wait_ge(sh_in, 48)
            for t in range(TT):
                if t:
                    pe.wait_ge(sh_silu, 2 * t)
                up(lambda k: c.hT[:, k, t * P:(t + 1) * P], 0, sh_h)
                if t == 2:
                    pe.wait_ge(sel_ready, 1)
                    pe.wait_ge(consts, 2)
                    for tt in range(TT):
                        for s in range(tt + 1):
                            nc.tensor.matmul(pr[:, tt * NE:(tt + 1) * NE], before[:] if s == tt else onesb[:], sel[:, s],
                                             start=s == 0, stop=s == tt)
                    for s in range(TT):
                        last = nc.tensor.matmul(pr[:, TT * NE:(TT + 1) * NE], onesb[:], sel[:, s], start=s == 0, stop=s == TT - 1)
                    last.then_inc(pos_done, 1)
                pe.wait_ge(sh_hh, t + 1)
                if t:
                    pe.wait_ge(sh_hT, t)
                turn_h(t % 2, sh_th)
                pe.wait_ge(sh_hT, t + 1)
                if t:
                    pe.wait_ge(sh_acc, 2 * t)
                down(t % 2, 0, sh_y)
            for e in range(3):
                pe.wait_ge(sg_ready, 1)
                pe.wait_ge(hot_ready, e + 2)
                if e:
                    pe.wait_ge(idx_ready, e)
                rows(e % 2, idx_done)
            pe.wait_ge(xg_in[0], 16)
            turn_x(0, tx_done)
            pe.sem_inc(h_done, 2)
            pe.sem_inc(y_done, 2)
            pe.wait_ge(sh_silu, 2 * TT)
            pe.wait_ge(sh_acc, 2 * TT)
            pe.wait_ge(idx_ready, 3)
            pe.sem_inc(hh_ready, 1)
            with pe.Fori(0, NE // 2) as i:
                for b in range(2):
                    pe.wait_ge(w13_in[b], 32 * i + 32)
                    pe.wait_ge(xT_act, 2 * i + b + 1)
                    pe.wait_ge(xT_dve, 2 * i + b + 1)
                    pe.wait_ge(hh_ready, 2 * i + b + 1)
                    up(lambda k: xT[:, b, k], b, h_done)
                    pe.wait_ge(xg_in[1 - b], 16 * i + (16 if b == 0 else 32))
                    turn_x(1 - b, tx_done)
                    pe.wait_ge(hh_ready, 2 * i + b + 2)
                    turn_h(b, th_done)
                    pe.wait_ge(hot_ready, 2 * i + b + 5)
                    pe.wait_ge(idx_ready, 2 * i + b + 3)
                    rows(1 - b, idx_done)
                    pe.wait_ge(hT_ready, 2 * i + b + 1)
                    pe.wait_ge(w2_in[b], 16 * i + 16)
                    pe.wait_ge(y_ready, 4 * i + 2 * b + 1)
                    down(b, b, y_done)
            total = pe.value_load(ovi[0:1, OVB:OVB + 1], min_val=0, max_val=OVB)
            with pe.Fori(0, OVB) as j:
                with pe.If(j < total):
                    pe.wait_ge(ov["hot"], j + 1)
                    rows(0, ov["idxp"])
                    pe.wait_ge(ov_xg_in, 16 * j + 16)
                    turn_x(0, ov["tx"])
                    pe.wait_ge(ov["w"], 48 * j + 48)
                    pe.wait_ge(ov["xTa"], j + 1)
                    pe.wait_ge(ov["xTd"], j + 1)
                    up(lambda k: xT[:, 0, k], 0, ov["h"])
                    pe.wait_ge(ov["hh"], j + 1)
                    turn_h(0, ov["th"])
                    pe.wait_ge(ov["hT"], j + 1)
                    down(0, 0, ov["y"])
                    pe.wait_ge(ov["out"], 16 * j + 16)
                    pe.sem_inc(ov["turn"], 1)
    st.close(gathers=True)


def delta_stage(nc, c, A):
    st = Stage(nc, "gdn")
    HP = 2
    TURNS = GH // HP
    PF = HP * GD
    KINDS = 4
    K_, Q_, V_, Z_ = 1, 0, 2, 3
    NCONV = 3 * HP
    W = GH * GD
    TH = TT * GH
    BASE = 16
    LEVELS = (16, 32, 64)

    w = st.sb("w", [P, 2, KT, PF])
    raw = st.sb("raw", [P, 2, CONV - 1 + SEQ])
    acc = st.sb("acc", [P, 2, SEQ])
    oT = st.sb("oT", [P, GH, SEQ])
    wab = st.sb("wab", [P, KT, 2 * GH])
    abT = st.sb("abT", [2 * GH, SEQ])
    convw = st.sb("convw", [CONV * 3 * GH, P])
    convT = st.sb("convT", [P, CONV, 3, GH])
    cw = st.sb("cw", [P, CONV, 3, HP])
    nw = st.sb("nw", [P, 1])
    eps = st.sb("eps", [P, 1])
    dtb = st.sb("dtb", [P, GH])
    alog = st.sb("alog", [P, GH])
    soft = st.sb("soft", [P, 5, TT, GH])
    tab = st.sb("tab", [P, 7, TT, GH])
    G_, NGC, NBEG, KD, BE, NBE, GL = range(7)
    cur = st.sb("cur", [P, 7, TT, HP])
    masks = st.sb("masks", [P, 6, P])

    def tiles(name):
        return [st.sb(f"{name}{h}", [P, TT, P]) for h in range(HP)]

    kT, qT, vT, zs, qg, dT, vn, kbe, kdec, vb, M, P0, P1, Q0, Q1, E0, E1, qkT = [
        tiles(x) for x in "kT qT vT zs qg dT vn kbe kdec vb M P0 P1 Q0 Q1 E0 E1 qkT".split()]
    wT = vT
    S = st.sb("S", [P, HP, 2, P])
    pj = [st.ps(f"pj{n}", [P, 512]) for n in range(2)]
    ps = [[st.ps(f"ps{h}{n}", [P, TT, P]) for n in range(3)] for h in range(HP)]

    r, q = np.arange(P)[:, None], np.arange(P)[None, :]
    below = (q < r) & (q // BASE == r // BASE)
    links = [(r // (2 * b) == q // (2 * b)) & (r // b % 2 == 1) & (q // b % 2 == 0) for b in LEVELS]
    table = np.stack([below, below.T] + links + [np.where(r <= q, 0.0, NEG)], 1).astype(np.float32)
    BELOW, ABOVE, LINK, CAUSAL = 0, 1, 2, 5
    mask_dram = nc.inline_tensor(table.reshape(P, -1), "delta_masks")

    sem = st.sem
    small_in, abw_in, conv_in = sem("small_in"), sem("abw_in"), sem("conv_in")
    w_in = [sem(f"w_in{n}") for n in range(2)]
    proj_done, proj_free, silu_ready, conv_ready = sem("proj_done"), sem("proj_free"), sem("silu_ready"), sem("conv_ready")
    ab_done, ab_copied, ab_turned, conv_turned = sem("ab_done"), sem("ab_copied"), sem("ab_turned"), sem("conv_turned")
    x_ready, act_small, g_ready, gc_done, kd_arg, tab_ready = (sem("x_ready"), sem("act_small"), sem("g_ready"), sem("gc_done"),
                                                               sem("kd_arg"), sem("tab_ready"))
    k_ln, q_ln, o_ln = sem("k_ln"), sem("q_ln"), sem("o_ln")
    dve_step, conv_step, cur_ready, gb_ready = sem("dve_step"), sem("conv_step"), sem("cur_ready"), sem("gb_ready")
    w_asked = sem("w_asked")
    (gc_row, eg_row, masked, dT_ready, kk_sq, kk_norm, k_rs, kT_ready, q_sq, q_norm, q_rs, qT_ready, k_turned, kbe_ready,
     kdec_ready, kk_done, G_ready, G_turned, M_ready, M_turned, Q_ready, P_ready, E_first, v_turned, vb_ready, qk_done,
     qk_ready, qg_ready) = [sem(x) for x in (
        "gc_row eg_row masked dT_ready k_sq k_norm k_rs kT_ready q_sq q_norm q_rs qT_ready k_turned kbe_ready "
        "kdec_ready kk_done G_ready G_turned M_ready M_turned Q_ready P_ready E_first v_turned vb_ready qk_done "
        "qk_ready qg_ready").split()]
    pw_done = [sem(f"pw_done{n}") for n in range(3)]
    pw_ready = [sem(f"pw_ready{n}") for n in range(3)]
    e_done = [sem(f"e_done{n}") for n in range(6)]
    e_ready = [sem(f"e_ready{n}") for n in range(6)]
    d_done = [sem(f"d_done{n}") for n in range(3)]
    d_ready = [sem(f"d_ready{n}") for n in range(3)]
    n_ready = [sem(f"n_ready{n}") for n in range(3)]
    y_done_ = [sem(f"y_done{n}") for n in range(3)]
    y_ready_ = [sem(f"y_ready{n}") for n in range(3)]
    w_done, w_ready = sem("w_done"), sem("w_ready")
    vn_done, vn_ready, s_done, s_ready, o_done = sem("vn_done"), sem("vn_ready"), sem("s_done"), sem("s_ready"), sem("o_done")
    o_sq, o_norm, o_rs, o_scaled, o_ready = sem("o_sq"), sem("o_norm"), sem("o_rs"), sem("o_scaled"), sem("o_ready")
    out_done, out_used = sem("out_done"), sem("out_used")

    w_dram = A["gdn_w_in"][0].rearrange("(p k) n -> p k n", k=KT)
    wo_dram = A["gdn_w_out"][0].rearrange("(k p) n -> p k n", p=P)
    order = [K_, Q_, V_, Z_]

    def rowp(ap):
        return ap.rearrange("(a n) -> a n", a=1).partition_broadcast(P)

    def flat(t):
        return t[:].rearrange("p t n -> p (t n)")

    def over_t(m):
        return m.rearrange("p (a n) -> p a n", a=1).broadcast_to([P, TT, P])

    def col(kind, h):
        return cur[:, kind, :, h:h + 1].broadcast_to([P, TT, P])

    with nc.Block() as block:
        @block.sync
        def _(sp):
            sp.dma_start(wab[:], w_dram[:, :, 4 * W:4 * W + 2 * GH]).then_inc(abw_in, 16)
            with sp.Fori(0, TURNS) as i:
                for n, kind in enumerate(order):
                    sp.wait_ge(proj_done, 2 * KINDS * i + 2 * n + 2)
                    sp.sem_inc(w_asked, 1)
                    sp.dma_start(w[:, n % 2], w_dram[:, :, bass.ds(i * PF + kind * W, PF)]).then_inc(w_in[n % 2], 16)
            for n in range(4):
                if n < 2:
                    sp.wait_ge(proj_done, 2 * KINDS * TURNS + 2 * n + 2)
                else:
                    sp.wait_ge(out_done, TT * (n - 1))
                sp.dma_start(w[:, n % 2], wo_dram[:, :, n * PF:(n + 1) * PF]).then_inc(w_in[n % 2], 16)

        @block.scalar
        def _(act):
            act.dma_start(convw[:], A["gdn_conv_w"][0].rearrange("j (m p) -> (j m) p", p=P)).then_inc(conv_in, 16)
            act.dma_start(nw[:], A["gdn_norm_w"][0].rearrange("(p a) -> p a", a=1)).then_inc(small_in, 16)
            act.dma_start(dtb[:], rowp(A["gdn_dt_bias"][0])).then_inc(small_in, 16)
            act.dma_start(alog[:], rowp(A["gdn_a_log"][0])).then_inc(small_in, 16)
            act.dma_start(masks[:], mask_dram.ap().rearrange("p (m n) -> p m n", n=P)).then_inc(small_in, 16)
            act.wait_ge(ab_done, 1)
            nc.scalar.copy(abT[:], pj[0][0:2 * GH, :]).then_inc(ab_copied, 1)
            act.wait_ge(ab_turned, 1)
            abv = pj[1][:, 0:2 * TH].rearrange("p (t n) -> p t n", t=TT)
            nc.scalar.activation(tab[:, BE], abv[:, :, GH:2 * GH], ACT.Sigmoid).then_inc(act_small, 1)
            act.wait_ge(small_in, 64)
            nc.scalar.activation(alog[:], alog[:], ACT.Exp).then_inc(act_small, 1)
            act.wait_ge(x_ready, 1)
            nc.scalar.activation(soft[:, 1], soft[:, 1], ACT.Exp, scale=-1.0).then_inc(act_small, 1)
            act.wait_ge(x_ready, 2)
            nc.scalar.activation(soft[:, 3], soft[:, 2], ACT.Ln).then_inc(act_small, 1)
            act.wait_ge(gc_done, 1)
            gcv = pj[1][:, 0:2 * TH].rearrange("p (s t n) -> p s t n", s=2, t=TT)
            nc.scalar.activation(soft[:, 0], gcv[:, 0], ACT.Exp).then_inc(act_small, 1)
            nc.scalar.activation(tab[:, GL], gcv[:, 1], ACT.Exp).then_inc(act_small, 1)
            act.wait_ge(kd_arg, 1)
            nc.scalar.activation(tab[:, KD], soft[:, 1], ACT.Exp).then_inc(act_small, 1)
            act.sem_inc(silu_ready, 2)
            act.sem_inc(proj_free, 2)

            with act.Fori(0, TURNS) as i:
                def copy_raw(m):
                    act.wait_ge(proj_done, 2 * KINDS * i + m + 5)
                    act.wait_ge(conv_ready, NCONV * i + m + 1)
                    nc.scalar.copy(raw[:, m % 2, CONV - 1:], pj[m % 2][:]).then_inc(proj_free, 1)

                def silu(m, dst):
                    act.wait_ge(conv_ready, NCONV * i + m + 3)
                    nc.scalar.activation(flat(dst), acc[:, m % 2], ACT.Silu).then_inc(silu_ready, 1)

                copy_raw(0), copy_raw(1), silu(0, kT[0]), silu(1, kT[1])
                copy_raw(2), silu(2, qT[0]), copy_raw(3), silu(3, qT[1])
                for h in range(HP):
                    act.wait_ge(kk_norm, 2 * i + h + 1)
                    nc.scalar.activation(E1[h][:], ps[h][1][:], ACT.Ln, bias=eps[:]).then_inc(k_ln, 1)
                copy_raw(4)
                for h in range(HP):
                    act.wait_ge(q_norm, 2 * i + h + 1)
                    nc.scalar.activation(E0[h][:], ps[h][2][:], ACT.Ln, bias=eps[:]).then_inc(q_ln, 1)
                for h in range(HP):
                    act.wait_ge(k_ln, 2 * i + h + 1)
                    nc.scalar.activation(E1[h][:], E1[h][:], ACT.Exp, scale=-0.5).then_inc(k_rs, 1)
                for h in range(HP):
                    act.wait_ge(q_ln, 2 * i + h + 1)
                    nc.scalar.activation(E0[h][:], E0[h][:], ACT.Exp, scale=-0.5).then_inc(q_rs, 1)
                for h in range(HP):
                    n = 2 * i + h + 1
                    act.wait_ge(masked, n)
                    nc.scalar.activation(qg[h][:], ps[h][0][:], ACT.Exp).then_inc(eg_row, 1)
                    for t in range(TT):
                        last = nc.scalar.activation(dT[h][:, t], P1[h][:, t], ACT.Exp, bias=cur[:, NGC, t, h:h + 1])
                    last.then_inc(dT_ready, 1)
                silu(4, vT[0]), copy_raw(5), silu(5, vT[1])
                for h in range(HP):
                    act.wait_ge(proj_done, 2 * KINDS * i + 6 + h + 5)
                    nc.scalar.activation(flat(zs[h]), pj[h][:], ACT.Silu).then_inc(proj_free, 1)
                for s, (pd, qd) in enumerate(((P1, Q1), (P0, Q0), (P1, None))):
                    for h in range(HP):
                        act.wait_ge(pw_done[s], 2 * i + h + 1)
                        if s == 1:
                            act.wait_ge(E_first, 2 * i + h + 1)
                        last = nc.scalar.copy(pd[h][:], ps[h][1][:])
                        if qd is not None:
                            last = nc.scalar.copy(qd[h][:], ps[h][2][:])
                        last.then_inc(pw_ready[s], 1)
                for s in range(3):
                    for h in range(HP):
                        act.wait_ge(d_done[s], 2 * i + h + 1)
                        nc.scalar.copy(Q0[h][:], ps[h][1][:]).then_inc(d_ready[s], 1)
                        act.wait_ge(y_done_[s], 2 * i + h + 1)
                        nc.scalar.copy(Q1[h][:], ps[h][2][:]).then_inc(y_ready_[s], 1)
                for h in range(HP):
                    act.wait_ge(w_done, 2 * i + h + 1)
                    nc.scalar.copy(wT[h][:], ps[h][2][:]).then_inc(w_ready, 1)
                for t in range(TT):
                    for h in range(HP):
                        act.wait_ge(vn_done, 2 * TT * i + 2 * t + h + 1)
                        nc.scalar.copy(vn[h][:, t], ps[h][1][:, t]).then_inc(vn_ready, 1)
                for h in range(HP):
                    act.wait_ge(o_done, 2 * i + h + 1)
                    nc.scalar.activation(P1[h][:], ps[h][0][:], ACT.Square, scale=GD ** -0.5).then_inc(o_sq, 1)
                for h in range(HP):
                    act.wait_ge(o_norm, 2 * i + h + 1)
                    nc.scalar.activation(Q1[h][:], ps[h][1][:], ACT.Ln, bias=eps[:]).then_inc(o_ln, 1)
                for h in range(HP):
                    act.wait_ge(o_ln, 2 * i + h + 1)
                    nc.scalar.activation(Q1[h][:], Q1[h][:], ACT.Exp, scale=-0.5).then_inc(o_rs, 1)

        @block.gpsimd
        def _(pool):
            pool.wait_ge(tab_ready, 1)
            with pool.Fori(0, TURNS) as i:
                for h in range(HP):
                    pool.wait_ge(cur_ready, 2 * i + 2)
                    pool.tensor_tensor(Q1[h][:], over_t(c.ones[:]), col(G_, h), ALU.mult).then_inc(gb_ready, 1)
                for h in range(HP):
                    pool.wait_ge(silu_ready, NCONV * i + h + 3)
                    pool.tensor_tensor(E1[h][:], kT[h][:], kT[h][:], ALU.mult).then_inc(kk_sq, 1)
                for h in range(HP):
                    pool.wait_ge(silu_ready, NCONV * i + h + 5)
                    pool.tensor_tensor(E0[h][:], qT[h][:], qT[h][:], ALU.mult).then_inc(q_sq, 1)
                for h in range(HP):
                    pool.wait_ge(qT_ready, 2 * i + h + 1)
                    pool.wait_ge(eg_row, 2 * i + h + 1)
                    pool.tensor_tensor(qg[h][:], qT[h][:], qg[h][:], ALU.mult).then_inc(qg_ready, 1)
                for h in range(HP):
                    pool.wait_ge(M_ready, 2 * i + h + 1)
                    pool.tensor_tensor(P0[h][:], M[h][:], over_t(masks[:, BELOW]), ALU.mult).then_inc(P_ready, 1)
                for s, dst in enumerate((P0, P1, P0)):
                    for h in range(HP):
                        pool.wait_ge((e_done[1], e_done[2], y_done_[0])[s], 2 * i + h + 1)
                        if s == 0:
                            pool.wait_ge(pw_done[2], 2 * i + h + 1)
                        pool.tensor_tensor(dst[h][:], M[h][:], over_t(masks[:, LINK + s]), ALU.mult).then_inc(n_ready[s], 1)

        @block.vector
        def _(dve):
            ch = Chain(dve, dve_step)
            dve.sem_inc(conv_ready, 2)
            dve.sem_inc(o_ready, 2)
            ch.do(nc.vector.memset(raw[:, :, 0:CONV - 1], 0.0))
            ch.do(nc.vector.memset(eps[:], RMS_EPS))
            dve.wait_ge(small_in, 64)
            dve.wait_ge(conv_turned, 1)
            ch.do(nc.vector.tensor_copy(convT[:].rearrange("p a b c -> p (a b c)"), pj[0][:, 0:CONV * 3 * GH]))
            dve.wait_ge(act_small, 1)
            abv = pj[1][:, 0:2 * TH].rearrange("p (t n) -> p t n", t=TT)
            x, e, u, ln, fix = [soft[:, n] for n in range(5)]
            ch.do(nc.vector.tensor_tensor(x, abv[:, :, 0:GH], dtb[:].rearrange("p (a n) -> p a n", a=1).broadcast_to([P, TT, GH]), ALU.add))
            ch.sync()
            nc.vector.scalar_tensor_tensor(out=e, in0=x, scalar=-1.0, in1=x, op0=ALU.mult, op1=ALU.max).then_inc(x_ready, 1)
            dve.wait_ge(act_small, 3)
            nc.vector.tensor_scalar(u, e, 1.0, None, ALU.add).then_inc(x_ready, 1)
            dve.wait_ge(x_ready, 2)
            ch.do(nc.vector.tensor_scalar(fix, u, -1.0, None, ALU.add))
            ch.sync()
            ch.do(nc.vector.tensor_tensor(fix, e, fix, ALU.subtract))
            dve.wait_ge(act_small, 4)
            ch.do(nc.vector.reciprocal(u, u))
            ch.sync()
            ch.do(nc.vector.tensor_tensor(fix, fix, u, ALU.mult))
            ch.sync()
            ch.do(nc.vector.tensor_tensor(fix, fix, ln, ALU.add))
            ch.sync()
            ch.do(nc.vector.scalar_tensor_tensor(out=fix, in0=x, scalar=0.0, in1=fix, op0=ALU.max, op1=ALU.add))
            ch.sync()
            nc.vector.scalar_tensor_tensor(out=tab[:, G_], in0=fix, scalar=-1.0,
                                           in1=alog[:].rearrange("p (a n) -> p a n", a=1).broadcast_to([P, TT, GH]),
                                           op0=ALU.mult, op1=ALU.mult).then_inc(g_ready, 1)
            dve.wait_ge(act_small, 6)
            gcv = pj[1][:, 0:2 * TH].rearrange("p (s t n) -> p s t n", s=2, t=TT)
            ch.do(nc.vector.tensor_scalar(tab[:, NGC], gcv[:, 0], -1.0, None, ALU.mult))
            ch.sync()
            nc.vector.tensor_tensor(e, gcv[:, 1], tab[:, NGC], ALU.add).then_inc(kd_arg, 1)
            ch.do(nc.vector.tensor_scalar(tab[:, NBE], tab[:, BE], -1.0, None, ALU.mult))
            ch.sync()
            dve.wait_ge(act_small, 7)
            nc.vector.tensor_tensor(tab[:, NBEG], tab[:, NBE], x, ALU.mult).then_inc(tab_ready, 1)
            dve.wait_ge(tab_ready, 1)
            first = ch.n

            with dve.Fori(0, TURNS) as i:
                nc.vector.tensor_scalar(cur[:], tab[:, :, :, bass.ds(HP * i, HP)], 1.0, None, ALU.mult).then_inc(cur_ready, 1)
                nc.vector.tensor_scalar(cw[:], convT[:, :, :, bass.ds(HP * i, HP)], 1.0, None, ALU.mult).then_inc(cur_ready, 1)
                dve.wait_ge(cur_ready, 2 * i + 2)

                def conv(m, kind):
                    dve.wait_ge(proj_free, 2 * KINDS * i + m + 3)
                    dve.wait_ge(silu_ready, NCONV * i + m + 1)
                    for j in range(CONV):
                        src, to = raw[:, m % 2, j:j + SEQ], acc[:, m % 2]
                        wj = cw[:, j, kind, m % 2:m % 2 + 1]
                        if j == 0:
                            last = nc.vector.tensor_scalar(to, src, wj, None, ALU.mult)
                        else:
                            last = nc.vector.scalar_tensor_tensor(out=to, in0=src, scalar=wj, in1=to, op0=ALU.mult, op1=ALU.add)
                        if j < CONV - 1:
                            last.then_inc(conv_step, 1)
                            dve.wait_ge(conv_step, 3 * NCONV * i + 3 * m + j + 1)
                    last.then_inc(conv_ready, 1)

                def with_column(out, in_, kind, h, done):
                    nc.vector.tensor_tensor(out[:], in_[:], col(kind, h), ALU.mult).then_inc(done, 1)

                def mask_causal(h):
                    dve.wait_ge(gc_row, 2 * i + h + 1)
                    nc.vector.tensor_tensor(P1[h][:], ps[h][0][:], over_t(masks[:, CAUSAL]), ALU.add).then_inc(masked, 1)

                def norm_k(h):
                    dve.wait_ge(k_rs, 2 * i + h + 1)
                    nc.vector.tensor_tensor(kT[h][:], kT[h][:], E1[h][:], ALU.mult).then_inc(kT_ready, 1)

                def norm_q(h):
                    dve.wait_ge(q_rs, 2 * i + h + 1)
                    nc.vector.scalar_tensor_tensor(out=qT[h][:], in0=qT[h][:], scalar=GD ** -0.5, in1=E0[h][:],
                                                   op0=ALU.mult, op1=ALU.mult).then_inc(qT_ready, 1)

                def keys(h):
                    dve.wait_ge(k_turned, 2 * i + h + 1)
                    with_column(kbe[h], ps[h][2], NBEG, h, kbe_ready)
                    with_column(kdec[h], ps[h][2], KD, h, kdec_ready)
                    dve.wait_ge(kk_done, 2 * i + h + 1)
                    dve.wait_ge(dT_ready, 2 * i + h + 1)
                    nc.vector.tensor_tensor(Q1[h][:], ps[h][1][:], dT[h][:], ALU.mult).then_inc(G_ready, 1)

                conv(0, K_), conv(1, K_), mask_causal(0), mask_causal(1)
                conv(2, Q_), conv(3, Q_), conv(4, V_)
                norm_k(0), norm_k(1), norm_q(0), norm_q(1), keys(0), keys(1), conv(5, V_)
                for h in range(HP):
                    dve.wait_ge(G_turned, 2 * i + h + 1)
                    with_column(M[h], ps[h][1], NBE, h, M_ready)
                for h in range(HP):
                    n = 2 * i + h + 1
                    dve.wait_ge(v_turned, n)
                    with_column(vb[h], ps[h][2], BE, h, vb_ready)
                    dve.wait_ge(M_turned, n)
                    nc.vector.tensor_tensor(Q0[h][:], ps[h][1][:], over_t(masks[:, ABOVE]), ALU.mult).then_inc(Q_ready, 1)
                    dve.wait_ge(qk_done, n)
                    nc.vector.tensor_tensor(qkT[h][:], ps[h][0][:], dT[h][:], ALU.mult).then_inc(qk_ready, 1)
                    dve.wait_ge(Q_ready, n)
                    nc.vector.tensor_tensor(E0[h][:], Q0[h][:], over_t(c.ident[:]), ALU.add).then_inc(E_first, 1)
                for s in range(6):
                    src, dst = (E0, E1) if s % 2 == 0 else (E1, E0)
                    for h in range(HP):
                        dve.wait_ge(e_done[s], 2 * i + h + 1)
                        dve.wait_ge(E_first if s == 0 else e_ready[s - 1], 2 * i + h + 1)
                        nc.vector.tensor_tensor(dst[h][:], ps[h][0][:], src[h][:], ALU.add).then_inc(e_ready[s], 1)
                for t in range(TT - 1):
                    for h in range(HP):
                        dve.wait_ge(s_done, 2 * (TT - 1) * i + 2 * t + h + 1)
                        if t == 0:
                            last = nc.vector.tensor_copy(S[:, h, 0], ps[h][2][:, t])
                        else:
                            dve.wait_ge(s_ready, 2 * (TT - 1) * i + 2 * (t - 1) + h + 1)
                            last = nc.vector.scalar_tensor_tensor(out=S[:, h, t % 2], in0=S[:, h, (t - 1) % 2],
                                                                  scalar=cur[:, GL, t, h:h + 1], in1=ps[h][2][:, t],
                                                                  op0=ALU.mult, op1=ALU.add)
                        last.then_inc(s_ready, 1)
                for h in range(HP):
                    n = 2 * i + h + 1
                    dve.wait_ge(o_rs, n)
                    nc.vector.scalar_tensor_tensor(out=kT[h][:], in0=ps[h][0][:], scalar=nw[:], in1=Q1[h][:],
                                                   op0=ALU.mult, op1=ALU.mult).then_inc(o_scaled, 1)
                    dve.wait_ge(o_scaled, n)
                    nc.vector.tensor_tensor(oT[:, bass.ds(2 * i + h, 1)].rearrange("p a n -> p (a n)"), flat(kT[h]), flat(zs[h]),
                                            ALU.mult).then_inc(o_ready, 1)
            out = Chain(dve, dve_step, first)
            for n in range(4):
                for t in range(TT):
                    j = n * TT + t
                    cols = slice(n * PF, (n + 1) * PF)
                    dve.wait_ge(out_done, j + 1)
                    nc.vector.tensor_tensor(acc[:, j % 2, 0:PF], pj[j % 2][:, 0:PF], c.ada[:, 2, cols], ALU.mult).then_inc(out_used, 1)
                    dve.wait_ge(out_used, j + 1)
                    out.do(nc.vector.scalar_tensor_tensor(out=c.x[:, t, cols], in0=c.x[:, t, cols], scalar=ALPHA,
                                                          in1=acc[:, j % 2, 0:PF], op0=ALU.mult, op1=ALU.add))
                    out.sync()

        @block.tensor
        def _(pe):
            def each(out, lhsT, rhs):
                for t in range(TT):
                    last = nc.tensor.matmul(out[:, t], lhsT(t), rhs(t), start=True, stop=True)
                return last

            def turn(out, src, done):
                for t in range(TT):
                    last = nc.tensor.transpose(out[:, t], src[:, t], c.ident[:])
                last.then_inc(done, 1)

            pe.wait_ge(abw_in, 16)
            for k in range(KT):
                last = nc.tensor.matmul(pj[0][0:2 * GH, :], wab[:, k], c.hT[:, k], start=k == 0, stop=k == KT - 1)
            last.then_inc(ab_done, 1)
            pe.wait_ge(ab_copied, 1)
            for t in range(TT):
                last = nc.tensor.transpose(pj[1][:, t * 2 * GH:(t + 1) * 2 * GH], abT[:, t * P:(t + 1) * P],
                                           c.ident[0:2 * GH, 0:2 * GH])
            last.then_inc(ab_turned, 1)
            NW = CONV * 3 * GH
            pe.wait_ge(conv_in, 16)
            nc.tensor.transpose(pj[0][:, 0:NW], convw[:], c.ident[0:NW, 0:NW]).then_inc(conv_turned, 1)
            pe.wait_ge(g_ready, 1)
            pe.wait_ge(act_small, 1)
            gflat = tab[:, G_].rearrange("p t n -> p (t n)")
            nc.tensor.matmul(pj[1][:, 0:TH], c.upper[:], gflat, start=True, stop=True)
            nc.tensor.matmul(pj[1][:, TH:2 * TH], c.ones[:], gflat, start=True, stop=True).then_inc(gc_done, 1)
            pe.wait_ge(tab_ready, 1)
            pe.sem_inc(proj_done, 4)

            with pe.Fori(0, TURNS) as i:
                def proj(m):
                    n, h = m // 2, m % 2
                    if h == 0:
                        pe.wait_ge(w_in[n % 2], 32 * i + 16 * (n // 2) + 16)
                    pe.wait_ge(proj_free, 2 * KINDS * i + m + 1)
                    for k in range(KT):
                        last = nc.tensor.matmul(pj[h][:], w[:, n % 2, k, h * P:(h + 1) * P], c.hT[:, k], start=k == 0, stop=k == KT - 1)
                    last.then_inc(proj_done, 1)

                def sum_squares(bank, sq, ready, h, done):
                    pe.wait_ge(ready, 2 * i + h + 1)
                    nc.tensor.matmul(bank[:].rearrange("p t n -> p (t n)"), c.ones[:], flat(sq), start=True, stop=True).then_inc(done, 1)

                def keys(h):
                    pe.wait_ge(kT_ready, 2 * i + h + 1)
                    turn(ps[h][2], kT[h], k_turned)
                    each(ps[h][1], lambda t: kT[h][:, t], lambda t: kT[h][:, t]).then_inc(kk_done, 1)

                def turn_g(h):
                    pe.wait_ge(G_ready, 2 * i + h + 1)
                    turn(ps[h][1], Q1[h], G_turned)

                def late(h):
                    n = 2 * i + h + 1
                    pe.wait_ge(silu_ready, NCONV * i + 4 + h + 3)
                    pe.wait_ge(qT_ready, n)
                    pe.wait_ge(kdec_ready, n)
                    turn(ps[h][2], vT[h], v_turned)
                    pe.wait_ge(M_ready, n)
                    turn(ps[h][1], M[h], M_turned)
                    each(ps[h][0], lambda t: kT[h][:, t], lambda t: qT[h][:, t]).then_inc(qk_done, 1)

                pe.wait_ge(o_ready, 2 * i + 2)
                proj(0)
                for h in range(HP):
                    pe.wait_ge(gb_ready, 2 * i + h + 1)
                    each(ps[h][0], lambda t: Q1[h][:, t], lambda t: c.upper[:]).then_inc(gc_row, 1)
                proj(1)
                proj(2), sum_squares(ps[0][1], E1[0], kk_sq, 0, kk_norm)
                proj(3), sum_squares(ps[1][1], E1[1], kk_sq, 1, kk_norm)
                sum_squares(ps[0][2], E0[0], q_sq, 0, q_norm)
                proj(4), sum_squares(ps[1][2], E0[1], q_sq, 1, q_norm)
                proj(5), keys(0), keys(1)
                proj(6), turn_g(0), turn_g(1)
                proj(7), late(0), late(1)
                for h in range(HP):
                    n = 2 * i + h + 1
                    pe.wait_ge(P_ready, n)
                    pe.wait_ge(Q_ready, n)
                    each(ps[h][1], lambda t: Q0[h][:, t], lambda t: P0[h][:, t])
                    each(ps[h][2], lambda t: P0[h][:, t], lambda t: Q0[h][:, t]).then_inc(pw_done[0], 1)
                for s, (p, q, e, ready) in enumerate(((P1, Q1, E0, E_first), (P0, Q0, E1, e_ready[0]), (P1, None, E0, e_ready[1]))):
                    for h in range(HP):
                        n = 2 * i + h + 1
                        pe.wait_ge(pw_ready[s], n)
                        if s < 2:
                            last = each(ps[h][1], lambda t: q[h][:, t], lambda t: p[h][:, t])
                            if s == 1:
                                last.then_inc(pw_done[2], 1)
                        if s == 0:
                            each(ps[h][2], lambda t: p[h][:, t], lambda t: q[h][:, t]).then_inc(pw_done[1], 1)
                            pe.wait_ge(qk_ready, n)
                        pe.wait_ge(ready, n)
                        each(ps[h][0], lambda t: p[h][:, t], lambda t: e[h][:, t]).then_inc(e_done[s], 1)
                for s in range(3):
                    link, e = (P0, P1, P0)[s], (E1, E0, E1)[s]
                    for h in range(HP):
                        n = 2 * i + h + 1
                        pe.wait_ge(e_ready[s + 2], n)
                        turn(ps[h][1], e[h], d_done[s])
                        pe.wait_ge(n_ready[s], n)
                        each(ps[h][2], lambda t: link[h][:, t], lambda t: e[h][:, t]).then_inc(y_done_[s], 1)
                    for h in range(HP):
                        n = 2 * i + h + 1
                        pe.wait_ge(d_ready[s], n)
                        pe.wait_ge(y_ready_[s], n)
                        each(ps[h][0], lambda t: Q0[h][:, t], lambda t: Q1[h][:, t]).then_inc(e_done[s + 3], 1)
                for h in range(HP):
                    n = 2 * i + h + 1
                    pe.wait_ge(e_ready[5], n)
                    pe.wait_ge(kbe_ready, n)
                    each(ps[h][2], lambda t: kbe[h][:, t], lambda t: E0[h][:, t]).then_inc(w_done, 1)
                for t in range(TT):
                    for h in range(HP):
                        n = 2 * i + h + 1
                        if t == 0:
                            pe.wait_ge(vb_ready, n)
                            pe.wait_ge(w_ready, n)
                        last = nc.tensor.matmul(ps[h][1][:, t], E0[h][:, t], vb[h][:, t], start=True, stop=t == 0)
                        if t:
                            pe.wait_ge(s_ready, 2 * (TT - 1) * i + 2 * (t - 1) + h + 1)
                            last = nc.tensor.matmul(ps[h][1][:, t], wT[h][:, t], S[:, h, (t - 1) % 2], start=False, stop=True)
                        last.then_inc(vn_done, 1)
                        if t:
                            if t == 1:
                                pe.wait_ge(qg_ready, n)
                            nc.tensor.matmul(ps[h][0][:, t], S[:, h, (t - 1) % 2], qg[h][:, t], start=True, stop=False)
                    for h in range(HP):
                        pe.wait_ge(vn_ready, 2 * TT * i + 2 * t + h + 1)
                        if t < TT - 1:
                            nc.tensor.matmul(ps[h][2][:, t], kdec[h][:, t], vn[h][:, t], start=True, stop=True).then_inc(s_done, 1)
                        last = nc.tensor.matmul(ps[h][0][:, t], vn[h][:, t], qkT[h][:, t], start=t == 0, stop=True)
                        if t == TT - 1:
                            last.then_inc(o_done, 1)
                for h in range(HP):
                    sum_squares(ps[h][1], P1[h], o_sq, h, o_norm)
            pe.wait_ge(o_ready, 2 * TURNS + 2)
            for n in range(4):
                pe.wait_ge(w_in[n % 2], 32 * TURNS + 16 * (n // 2) + 16)
                for t in range(TT):
                    j = n * TT + t
                    if j >= 2:
                        pe.wait_ge(out_used, j - 1)
                    else:
                        pe.wait_ge(proj_free, 2 * KINDS * TURNS + 2)
                    for k in range(KT):
                        last = nc.tensor.matmul(pj[j % 2][:, 0:PF], oT[:, k, t * P:(t + 1) * P], w[:, n % 2, k],
                                                start=k == 0, stop=k == KT - 1)
                    last.then_inc(out_done, 1)
    st.close()


def build(nc, A, out):
    h_rows = nc.dram_tensor("h_rows", (SEQ, D), F32).ap()
    y_rows = nc.dram_tensor("y_rows", ((NE + OVB) * CAP, D), F32).ap()
    with ExitStack() as ctx:
        c = alloc_core(nc, ctx)
        setup_stage(nc, c, A)
        norm_stage(nc, c, A, None, 0)
        attention_stage(nc, c, A, y_rows)
        norm_stage(nc, c, A, 0, 1, h_rows=h_rows)
        moe_stage(nc, c, A, 0, h_rows, y_rows)
        norm_stage(nc, c, A, 1, 2)
        delta_stage(nc, c, A)
        norm_stage(nc, c, A, 2, 3, h_rows=h_rows)
        moe_stage(nc, c, A, 1, h_rows, y_rows)
        norm_stage(nc, c, A, 3, None, out=out)


_INS = ("x", "c", "positions", "ada_w", "ada_b", "ln_g", "ln_b", "attn_w_in", "attn_w_out", "gdn_w_in", "gdn_conv_w",
        "gdn_a_log", "gdn_dt_bias", "gdn_norm_w", "gdn_w_out", "router_w", "router_bias", "expert_w1", "expert_w3",
        "expert_w2", "shared_w1", "shared_w3", "shared_w2")


def kernel(**inputs):
    import concourse.bacc as _bacc
    from concourse.bass_utils import run_bass_kernel_spmd as _run

    nc = _bacc.Bacc("TRN2", target_bir_lowering=False, num_devices=1)
    arrays, A = {}, {}
    for name in _INS:
        a = np.ascontiguousarray(inputs[name])
        arrays[f"in_{name}_dram"] = a
        A[name] = nc.dram_tensor(f"in_{name}_dram", a.shape, mybir.dt.from_np(a.dtype), kind="ExternalInput").ap()
    out = nc.dram_tensor("out_dram", (1, SEQ, D), F32, kind="ExternalOutput").ap()
    build(nc, A, out)
    r = _run(nc, [arrays], core_ids=[0])
    return r.results[0]["out_dram"]
```

```python
from contextlib import ExitStack

import numpy as np
import concourse.bass as bass
from concourse import mybir

F32 = mybir.dt.float32
BF16 = mybir.dt.bfloat16
I32 = mybir.dt.int32
U32 = mybir.dt.uint32
ALU = mybir.AluOpType
ACT = mybir.ActivationFunctionType
AX = mybir.AxisListType

P = 128
SEQ, D = 512, 1024
TT = SEQ // P
KT = D // P
DEPTH = 2
ALPHA = (2 * DEPTH) ** 0.25
LN_EPS, RMS_EPS = 1e-5, 1e-6
NEG = -1e30

HEADS, HD = 16, 64
GROUPS = 3
WINDOW0 = 128
QUADS = HEADS // 4
QF = 4 * HD
RES = 4
ROPE_THETA = 10000.0

GH, GD = 8, 128
CONV = 4

NE, TOPK, NG, TOPG = 64, 8, 8, 4
ED = 256
CAP = P
OVB = SEQ * TOPK // (CAP + 1)
ROUTED_SCALE = 2.5


class Stage:

    def __init__(self, nc, tag):
        self.nc, self.tag, self.ctx, self.sems = nc, tag, ExitStack(), []

    def sb(self, name, shape, dt=F32):
        return self.ctx.enter_context(self.nc.sbuf_tensor(f"{self.tag}_{name}", shape, dt))

    def ps(self, name, shape, dt=F32):
        return self.ctx.enter_context(self.nc.psum_tensor(f"{self.tag}_{name}", shape, dt))

    def sem(self, name):
        s = self.ctx.enter_context(self.nc.semaphore(f"{self.tag}_{name}"))
        self.sems.append(s)
        return s

    def close(self, gathers=False):
        if gathers:
            self.nc.gpsimd.dma_reset()
        for s in self.sems:
            self.nc.gpsimd.sem_clear(s)
        self.nc.all_engine_barrier()
        self.ctx.close()


class Chain:

    def __init__(self, eng, sem, base=0):
        self.eng, self.sem, self.base, self.n = eng, sem, base, 0

    def do(self, ins):
        ins.then_inc(self.sem, 1)
        self.n += 1
        return ins

    def sync(self):
        self.eng.wait_ge(self.sem, self.base + self.n)


class Core:
    pass


def alloc_core(nc, ctx):
    c = Core()

    def sb(name, shape, dt=F32):
        return ctx.enter_context(nc.sbuf_tensor(f"core_{name}", shape, dt))

    c.x = sb("x", [P, TT, D])
    c.hT = sb("hT", [P, KT, SEQ])
    c.ada = sb("ada", [P, 3, D])
    c.c = sb("c", [P, KT])
    c.ident = sb("ident", [P, P])
    c.ones = sb("ones", [P, P])
    c.upper = sb("upper", [P, P])
    return c


def setup_stage(nc, c, A):
    st = Stage(nc, "setup")
    loaded, filled, selected = st.sem("loaded"), st.sem("filled"), st.sem("selected")
    with nc.Block() as block:
        @block.sync
        def _(sp):
            sp.dma_start(c.c[:], A["c"].rearrange("a (p k) -> p (a k)", k=KT)).then_inc(loaded, 16)
            sp.dma_start(c.x[:], A["x"][0].rearrange("(t p) d -> p t d", p=P)).then_inc(loaded, 16)

        @block.vector
        def _(dve):
            nc.vector.memset(c.ident[:], 0.0).then_inc(filled, 1)
            nc.vector.memset(c.upper[:], 1.0).then_inc(filled, 1)
            nc.vector.memset(c.ones[:], 1.0).then_inc(filled, 1)
            dve.wait_ge(loaded, 32)

        @block.gpsimd
        def _(pool):
            pool.wait_ge(filled, 3)
            pool.affine_select(out=c.ident[:], in_=c.ident[:], compare_op=ALU.not_equal, fill=1.0, base=0,
                               pattern=[[-1, P]], channel_multiplier=1).then_inc(selected, 1)
            pool.affine_select(out=c.upper[:], in_=c.upper[:], compare_op=ALU.is_ge, fill=0.0, base=0,
                               pattern=[[1, P]], channel_multiplier=-1).then_inc(selected, 1)
            pool.wait_ge(selected, 2)
    st.close()


class AdaRows:
    TURNS = 4
    QA = 3 * D // TURNS

    def __init__(self, nc, c, st, A, mods, rows, slots):
        self.nc, self.c, self.slots, self.n = nc, c, slots, len(mods)
        self.first, self.rows = mods[0], rows
        self.steps = self.n * KT
        self.w = st.sb("ada_w", [P, slots, self.QA])
        self.acc = st.sb("ada_acc", [P, self.n, self.QA])
        self.row = st.sb("ada_row", [1, self.n, self.QA])
        self.w_in = [st.sem(f"ada_w_in{s}") for s in range(slots)]
        (self.asked, self.used, self.summed, self.ready, self.bias_in, self.stored) = [
            st.sem("ada_" + x) for x in "asked used summed ready bias_in stored".split()]
        self.aw = [A["ada_w"][m // 2, m % 2].rearrange("(p k) n -> p k n", k=KT) for m in mods]
        self.bias = A["ada_b"].rearrange("l s n -> (l s) n")

    def load(self, pool, i, j):
        pool.wait_ge(self.used, self.steps * i + j + 1)
        pool.sem_inc(self.asked, 1)
        pool.dma_start(self.w[:, j % self.slots], self.aw[j // KT][:, j % KT, bass.ds(i * self.QA, self.QA)])\
            .then_inc(self.w_in[j % self.slots], 16)

    def credits(self, dve):
        dve.sem_inc(self.used, self.slots)
        dve.sem_inc(self.summed, self.n)

    def add(self, dve, i, j):
        m, k, s = j // KT, j % KT, j % self.slots
        dve.wait_ge(self.w_in[s], 16 * (self.steps // self.slots) * i + 16 * (j // self.slots + 1))
        if k == 0:
            dve.wait_ge(self.summed, self.n * i + m + 1)
            ins = self.nc.vector.tensor_scalar(self.acc[:, m], self.w[:, s], self.c.c[:, k:k + 1], None, ALU.mult)
        else:
            dve.wait_ge(self.used, self.steps * i + j + self.slots)
            ins = self.nc.vector.scalar_tensor_tensor(out=self.acc[:, m], in0=self.w[:, s], scalar=self.c.c[:, k:k + 1],
                                                      in1=self.acc[:, m], op0=ALU.mult, op1=ALU.add)
        ins.then_inc(self.used, 1)

    def total(self, pe, i, m, outs):
        half = self.QA // 2
        pe.wait_ge(self.used, self.steps * i + KT * (m + 1) + self.slots)
        for n, out in enumerate(outs):
            last = self.nc.tensor.matmul(out, self.c.ones[:], self.acc[:, m, n * half:(n + 1) * half], start=True, stop=True)
        last.then_inc(self.summed, 1)

    def finish(self, dve, i, m, outs):
        half = self.QA // 2
        dve.wait_ge(self.bias_in, 16 * i + 16)
        dve.wait_ge(self.summed, self.n * i + m + 1 + self.n)
        for n, out in enumerate(outs):
            r = self.row[:, m, n * half:(n + 1) * half]
            self.nc.vector.tensor_tensor(r, out[0:1], r, ALU.add).then_inc(self.ready, 1)

    def cols(self, t, i):
        return t[self.first:self.first + self.n, bass.ds(i * self.QA, self.QA)].rearrange("(a m) n -> a m n", a=1)

    def load_bias(self, sp, i):
        sp.wait_ge(self.stored, 16 * i + 16)
        sp.sem_inc(self.asked, 1)
        sp.dma_start(self.row[:], self.cols(self.bias, i)).then_inc(self.bias_in, 16)

    def store(self, sp, i):
        sp.wait_ge(self.ready, 2 * self.n * i + 2 * self.n)
        sp.sem_inc(self.asked, 1)
        sp.dma_start(self.cols(self.rows, i), self.row[:]).then_inc(self.stored, 16)


def norm_stage(nc, c, A, norm, mod, ada_rows=None, h_rows=None, out=None):
    direct = mod is not None and ada_rows is None
    st = Stage(nc, f"norm{norm}")
    SLOTS = 2
    sem = st.sem
    rows_in, x_out, h_out = sem("rows_in"), sem("x_out"), sem("h_out")
    bias_in = sem("bias_in")
    w_in = [sem(f"w_in{i}") for i in range(SLOTS)]
    spread = sem("spread")
    w_used, ada_sum, ada_ready = sem("w_used"), sem("ada_sum"), sem("ada_ready")
    dve_step, var_ready, std_ready = sem("dve_step"), sem("var_ready"), sem("std_ready")
    x_ready, h_ready, turned, laid = sem("x_ready"), sem("h_ready"), sem("turned"), sem("laid")
    if norm is not None:
        g = st.sb("g", [P, D])
        b = st.sb("b", [P, D])
        stats = st.sb("stats", [P, TT, 2, 6])
        mv = st.sb("mv", [P, TT, 2])
        std = st.sb("std", [P, TT])
        eps = st.sb("eps", [P, 1])
        xn = st.sb("xn", [P, 2, D])
    if direct:
        w = st.sb("w", [P, SLOTS, 3 * D])
        bias = st.sb("bias", [P, 3 * D])
        cb = st.sb("cb", [P, KT, P])
        ada_ps = [st.ps(f"ada{n}", [P, 512]) for n in range(6)]
    if mod is not None:
        h = st.sb("h", [P, TT, D])
        tp = [st.ps(f"tp{n}", [P, 4, P]) for n in range(2)]
        aw = A["ada_w"][mod // 2, mod % 2].rearrange("(p k) n -> p k n", k=KT)

    def row(t, i):
        return t[i // 2, i % 2].rearrange("(a n) -> a n", a=1).partition_broadcast(P)

    with nc.Block() as block:
        @block.sync
        def _(sp):
            if direct:
                for k in range(KT):
                    if k >= SLOTS:
                        sp.wait_ge(w_used, k - SLOTS + 1)
                    sp.dma_start(w[:, k % SLOTS], aw[:, k]).then_inc(w_in[k % SLOTS], 16)
            for t in range(TT):
                if h_rows is not None:
                    sp.wait_ge(h_ready, t + 1)
                    sp.dma_start(h_rows[t * P:(t + 1) * P, :], h[:, t]).then_inc(h_out, 16)
                if out is not None:
                    sp.wait_ge(x_ready, t + 1)
                    sp.dma_start(out[0, t * P:(t + 1) * P, :], c.x[:, t]).then_inc(x_out, 16)
            if h_rows is not None:
                sp.wait_ge(h_out, 16 * TT)
            if out is not None:
                sp.wait_ge(x_out, 16 * TT)

        @block.scalar
        def _(act):
            if norm is not None:
                act.dma_start(g[:], row(A["ln_g"], norm)).then_inc(rows_in, 16)
                act.dma_start(b[:], row(A["ln_b"], norm)).then_inc(rows_in, 16)
            if direct:
                act.dma_start(bias[:], row(A["ada_b"], mod)).then_inc(bias_in, 16)
            elif mod is not None:
                act.dma_start(c.ada[:].rearrange("p a n -> p (a n)"),
                              ada_rows[mod].rearrange("(a n) -> a n", a=1).partition_broadcast(P)).then_inc(bias_in, 16)
            if norm is not None:
                for t in range(TT):
                    act.wait_ge(var_ready, t + 1)
                    nc.scalar.activation(std[:, t:t + 1], mv[:, t, 1:2], ACT.Sqrt, bias=eps[:]).then_inc(std_ready, 1)
            if mod is not None:
                for t in range(TT):
                    for q in range(2):
                        act.wait_ge(turned, 2 * t + q + 1)
                        nc.scalar.copy(c.hT[:, 4 * q:4 * q + 4, t * P:(t + 1) * P], tp[q][:]).then_inc(laid, 1)
                act.wait_ge(laid, 2 * TT)

        @block.vector
        def _(dve):
            ch = Chain(dve, dve_step)
            if direct:
                nc.vector.tensor_copy(cb[:], c.c[:].rearrange("p (k o) -> p k o", o=1).broadcast_to([P, KT, P])).then_inc(spread, 1)
            if norm is not None:
                ch.do(nc.vector.memset(eps[:], LN_EPS))
                for t in range(TT):
                    for q in range(2):
                        ch.do(nc.vector.bn_stats(stats[:, t, q], c.x[:, t, q * 512:(q + 1) * 512]))
                ch.sync()
                for t in range(TT):
                    nc.vector.bn_aggr(mv[:, t], stats[:, t]).then_inc(var_ready, 1)
                dve.wait_ge(var_ready, TT)
                dve.wait_ge(std_ready, TT)
                ch.do(nc.vector.reciprocal(std[:], std[:]))
                dve.wait_ge(rows_in, 32)
                ch.sync()
                for t in range(TT):
                    ch.do(nc.vector.tensor_scalar(xn[:, t % 2], c.x[:, t], mv[:, t, 0:1], std[:, t:t + 1],
                                                  ALU.subtract, ALU.mult))
                    ch.sync()
                    ch.do(nc.vector.tensor_tensor(xn[:, t % 2], xn[:, t % 2], g[:], ALU.mult))
                    ch.sync()
                    nc.vector.tensor_tensor(c.x[:, t], xn[:, t % 2], b[:], ALU.add).then_inc(x_ready, 1)
                dve.wait_ge(x_ready, TT)
            if mod is not None:
                dve.wait_ge(bias_in, 16)
                if direct:
                    dve.wait_ge(ada_sum, 1)
                    for n in range(6):
                        nc.vector.tensor_tensor(c.ada[:, n // 2, n % 2 * 512:(n % 2 + 1) * 512], ada_ps[n][:],
                                                bias[:, n * 512:(n + 1) * 512], ALU.add).then_inc(ada_ready, 1)
                    dve.wait_ge(ada_ready, 6)
                for t in range(TT):
                    ch.do(nc.vector.scalar_tensor_tensor(out=h[:, t], in0=c.ada[:, 1], scalar=1.0, in1=c.x[:, t],
                                                         op0=ALU.add, op1=ALU.mult))
                    ch.sync()
                    nc.vector.tensor_tensor(h[:, t], h[:, t], c.ada[:, 0], ALU.add).then_inc(h_ready, 1)
                dve.wait_ge(h_ready, TT)

        @block.tensor
        def _(pe):
            if direct:
                pe.wait_ge(spread, 1)
                for k in range(KT):
                    pe.wait_ge(w_in[k % SLOTS], 16 * (k // SLOTS + 1))
                    for n in range(6):
                        last = nc.tensor.matmul(ada_ps[n][:], cb[:, k], w[:, k % SLOTS, n * 512:(n + 1) * 512],
                                                start=k == 0, stop=k == KT - 1)
                    last.then_inc(w_used if k < KT - 1 else ada_sum, 1)
            if mod is not None:
                for t in range(TT):
                    pe.wait_ge(h_ready, t + 1)
                    for q in range(2):
                        if t:
                            pe.wait_ge(laid, 2 * t - 1 + q)
                        for k in range(4):
                            last = nc.tensor.transpose(tp[q][:, k], h[:, t, 4 * q + k::KT], c.ident[:])
                        last.then_inc(turned, 1)
    st.close()


def attention_stage(nc, c, A, ada_rows):
    st = Stage(nc, "attn")
    SLOTS = 3
    CH = 3 * GROUPS
    NPROJ = 2 * CH
    PC = 2 * SLOTS
    NROT = 4 * GROUPS
    UNITS = 4 * RES
    KEYS = SEQ + 2 * P
    C1, C2 = 6.28125, float(np.float32(0.0019350051879882812))
    C3 = float(2 * np.pi - C1 - C2)
    ROUND = 12582912.0

    w = st.sb("w", [P, SLOTS, KT, QF])
    v = st.sb("v", [P, GROUPS, TT, QF])
    q = st.sb("q", [P, GROUPS, 2, 2, SEQ])
    k = st.sb("k", [P, GROUPS, 2, SEQ])
    raw = st.sb("raw", [P, 2, SEQ])
    swp = st.sb("swp", [P, 2, SEQ])
    rot = st.sb("rot", [P, 2, SEQ])
    cos = st.sb("cos", [P, SEQ])
    sin = st.sb("sin", [P, SEQ])
    mask = st.sb("mask", [P, RES, KEYS])
    sm = st.sb("sm", [P, 2, KEYS])
    prob = st.sb("prob", [P, 2, KEYS])
    probT = st.sb("probT", [P, 2, KEYS])
    o = st.sb("o", [P, 2, P])
    oT = st.sb("oT", [P, KT, SEQ])
    small = st.sb("small", [P, 12])
    top = small[:, 0:2]
    bias = small[:, 2:4]
    den = small[:, 4:8]
    rden = small[:, 8:12]
    freq = st.sb("freq", [P, 2])
    halfpi = st.sb("halfpi", [P, 1])
    pos = st.sb("pos", [P, SEQ], I32)
    diff = st.sb("diff", [P, P], I32)
    ada = AdaRows(nc, c, st, A, (1, 2), ada_rows, 2)

    proj = [st.ps(f"proj{n}", [P, 512]) for n in range(2)]
    sc = st.ps("sc", [P, 1024])
    tp = st.ps("tp", [P, 8, P])
    pv = st.ps("pv", [P, 512])
    po = st.ps("po", [P, 512])

    sem = st.sem
    w_in = [sem(f"w_in{n}") for n in range(SLOTS)]
    proj_done, proj_free = sem("proj_done"), sem("proj_free")
    raw_ready, rot_done = sem("raw_ready"), sem("rot_done")
    swp_in = [sem(f"swp_in{n}") for n in range(2)]
    sc_done, sm_ready, bias_ready, p_ready = sem("sc_done"), sem("sm_ready"), sem("bias_ready"), sem("p_ready")
    tp_done, pT_ready, pv_done, o_ready = sem("tp_done"), sem("pT_ready"), sem("pv_done"), sem("o_ready")
    oT_done, oT_ready = sem("oT_done"), sem("oT_ready")
    dve_step, pool_step, tables_in, angle_ready = sem("dve_step"), sem("pool_step"), sem("tables_in"), sem("angle_ready")
    sin_ready, diff_ready, parity_ready, mask_ready = sem("sin_ready"), sem("diff_ready"), sem("parity_ready"), sem("mask_ready")
    turn_seen = sem("turn_seen")
    y_done, y_used = sem("y_done"), sem("y_used")
    DVE_T = NROT // 2 + 2 * NROT + UNITS

    half = HD // 2
    f = np.arange(P)
    table = np.stack([ROPE_THETA ** (-(f % half).astype(np.float32) / np.float32(half)),
                      np.where(f % HD < half, -1.0, 1.0)], 1).astype(np.float32)
    table_dram = nc.inline_tensor(table, "rope_table")
    w_dram = A["attn_w_in"][0].rearrange("(p k) (g s n) -> p k g s n", k=KT, g=GROUPS, s=3)
    wo_dram = A["attn_w_out"][0].rearrange("(k p) n -> p k n", p=P)
    side = [pv[:, P:P + ada.QA // 2], po[:, P:P + ada.QA // 2]]
    chunks = [(g, s) for g in range(GROUPS) for s in (2, 0, 1)]

    with nc.Block() as block:
        @block.sync
        def _(sp):
            sp.sem_inc(ada.stored, 16)
            with sp.Fori(0, QUADS) as i:
                ada.load_bias(sp, i)
                for n, (g, s) in enumerate(chunks):
                    sp.wait_ge(proj_done, NPROJ * i + 2 * n + 2)
                    sp.sem_inc(turn_seen, 1)
                    sp.dma_start(w[:, n % SLOTS], w_dram[:, :, g, s, bass.ds(i * QF, QF)]).then_inc(w_in[n % SLOTS], 16)
                ada.store(sp, i)
            for n in range(4):
                if n < SLOTS:
                    sp.wait_ge(proj_done, NPROJ * QUADS + 2 * n + 2)
                else:
                    sp.wait_ge(y_done, TT * (n - SLOTS + 1))
                sp.dma_start(w[:, n % SLOTS], wo_dram[:, :, n * QF:(n + 1) * QF]).then_inc(w_in[n % SLOTS], 16)
            sp.wait_ge(ada.stored, 16 * QUADS + 16)

        @block.scalar
        def _(act):
            act.dma_start(pos[:], A["positions"][0].rearrange("(a n) -> a n", a=1).partition_broadcast(P)).then_inc(tables_in, 16)
            act.dma_start(freq[:], table_dram.ap()).then_inc(tables_in, 16)
            act.wait_ge(angle_ready, 2)
            nc.scalar.activation(sin[:], raw[:, 0], ACT.Sin).then_inc(sin_ready, 1)
            nc.scalar.activation(cos[:], raw[:, 1], ACT.Sin, scale=-1.0, bias=halfpi[:]).then_inc(sin_ready, 1)
            act.sem_inc(proj_free, 2)
            act.sem_inc(pT_ready, 1)
            with act.Fori(0, QUADS) as i:
                n = m = 0
                for g, s in chunks:
                    for half_ in range(2):
                        act.wait_ge(proj_done, NPROJ * i + n + 1 + PC)
                        if s == 2:
                            nc.scalar.copy(v[:, g, 2 * half_:2 * half_ + 2, :],
                                           proj[n % 2][:].rearrange("p (t f) -> p t f", f=QF)).then_inc(proj_free, 1)
                        else:
                            act.wait_ge(rot_done, NROT * i + m + 1)
                            nc.scalar.copy(raw[:, m % 2], proj[n % 2][:]).then_inc(proj_free, 1)
                            act.wait_ge(proj_free, NPROJ * i + n + 3)
                            for d in range(4):
                                e = d ^ 1
                                act.dma_start(swp[32 * d:32 * d + 32, m % 2], raw[32 * e:32 * e + 32, m % 2])\
                                   .then_inc(swp_in[m % 2], 16)
                            m += 1
                        n += 1
                for step in range(UNITS + 1):
                    u = step - 1
                    if u >= 0:
                        act.wait_ge(tp_done, UNITS * i + u + 3)
                        act.wait_ge(pv_done, UNITS * i + u + 1)
                        nc.scalar.copy(probT[:, u % 2], tp[:, 0:6].rearrange("p b q -> p (b q)")).then_inc(pT_ready, 1)
                    u = step
                    if u < UNITS:
                        act.wait_ge(bias_ready, UNITS * i + u + 1)
                        act.wait_ge(tp_done, UNITS * i + u + 1)
                        nc.scalar.activation(prob[:, u % 2], sm[:, u % 2], ACT.Exp, bias=bias[:, u % 2:u % 2 + 1],
                                             scale=HD ** -0.5, accum_out=den[:, u % 4:u % 4 + 1]).then_inc(p_ready, 1)

        @block.gpsimd
        def _(pool):
            ch = Chain(pool, pool_step)
            ch.do(pool.iota(diff[:], pattern=[[-1, P]], base=P, channel_multiplier=1))
            ch.do(pool.memset(mask[:, :, 0:SEQ + P], 0.0))
            ch.sync()
            pool.sem_inc(diff_ready, 1)
            pool.wait_ge(parity_ready, 1)
            for t in range(2):
                m = mask[:, 0, SEQ + t * P:SEQ + (t + 1) * P]
                ch.do(pool.affine_select(out=m, in_=m, compare_op=ALU.is_ge, fill=NEG, base=0,
                                         pattern=[[-1, P]], channel_multiplier=1))
            ch.sync()
            for r in range(RES):
                m = mask[:, r, 0:SEQ]
                if r:
                    ch.do(pool.tensor_copy(mask[:, r, SEQ:KEYS], mask[:, 0, SEQ:KEYS]))
                ch.do(pool.affine_select(out=m, in_=m, compare_op=ALU.is_ge, fill=NEG, base=r,
                                         pattern=[[-1, SEQ]], channel_multiplier=RES))
                ch.sync()
                pool.affine_select(out=m, in_=m, compare_op=ALU.is_ge, fill=NEG, base=WINDOW0 - r,
                                   pattern=[[1, SEQ]], channel_multiplier=-RES).then_inc(mask_ready, 1)
            pool.wait_ge(mask_ready, RES)
            with pool.Fori(0, QUADS) as i:
                for j in range(ada.steps):
                    ada.load(pool, i, j)

        @block.vector
        def _(dve):
            dve.sem_inc(rot_done, 2)
            dve.sem_inc(sm_ready, 1)
            dve.sem_inc(o_ready, 1)
            ada.credits(dve)
            ch = Chain(dve, dve_step)
            ch.do(nc.vector.memset(q[:], 0.0))
            ch.do(nc.vector.memset(halfpi[:], float(np.pi / 2)))
            dve.wait_ge(pool_step, 2)
            ch.do(nc.vector.tensor_single_scalar(diff[:], diff[:], 3, ALU.bitwise_and))
            ch.sync()
            nc.vector.tensor_scalar(mask[:, 0, SEQ + P:KEYS], diff[:], 0.0, NEG, ALU.not_equal, ALU.mult).then_inc(parity_ready, 1)
            dve.wait_ge(tables_in, 32)
            ang, turns, rest = raw[:, 1], swp[:, 0], raw[:, 0]
            ch.do(nc.vector.tensor_scalar(ang, pos[:], freq[:, 0:1], None, ALU.mult))
            ch.sync()
            ch.do(nc.vector.tensor_scalar(turns, ang, float(1 / (2 * np.pi)), ROUND, ALU.mult, ALU.add))
            ch.sync()
            ch.do(nc.vector.tensor_scalar(turns, turns, ROUND, None, ALU.subtract))
            ch.sync()
            for part, src in ((C1, ang), (C2, rest), (C3, rest)):
                ch.do(nc.vector.scalar_tensor_tensor(out=rest, in0=turns, scalar=-part, in1=src, op0=ALU.mult, op1=ALU.add))
                ch.sync()
            lim = 3.1415925
            nc.vector.tensor_scalar(rest, rest, lim, -lim, ALU.min, ALU.max).then_inc(angle_ready, 1)
            dve.wait_ge(angle_ready, 1)
            nc.vector.scalar_tensor_tensor(out=ang, in0=rest, scalar=-1.0, in1=rest, op0=ALU.mult, op1=ALU.max).then_inc(angle_ready, 1)
            dve.wait_ge(sin_ready, 2)
            ch.do(nc.vector.tensor_scalar(sin[:], sin[:], freq[:, 1:2], None, ALU.mult))
            dve.wait_ge(mask_ready, RES)
            ch.sync()
            first = ch.n

            with dve.Fori(0, QUADS) as i:
                ch = Chain(dve, dve_step, DVE_T * i + first)
                m = 0
                for g in range(GROUPS):
                    for s in range(2):
                        for pair in range(2):
                            dve.wait_ge(proj_free, NPROJ * i + 2 * 3 * g + 2 * (s + 1) + pair + 3)
                            ch.do(nc.vector.tensor_tensor(rot[:, 0], raw[:, m % 2], cos[:], ALU.mult))
                            dve.wait_ge(swp_in[m % 2], 64 * (NROT // 2) * i + 64 * (m // 2 + 1))
                            ch.do(nc.vector.tensor_tensor(rot[:, 1], swp[:, m % 2], sin[:], ALU.mult))
                            ch.sync()
                            a = rot[:, 0].rearrange("p (j r) -> p j r", r=RES)
                            b = rot[:, 1].rearrange("p (j r) -> p j r", r=RES)
                            if s == 0:
                                for hh in range(2):
                                    rows = slice(HD * hh, HD * hh + HD)
                                    to = q[rows, g, pair, hh].rearrange("p (r j) -> p j r", r=RES)
                                    ins = nc.vector.tensor_tensor(to, a[rows], b[rows], ALU.add)
                                    if hh == 0:
                                        ch.do(ins)
                            else:
                                to = k[:, g, pair]
                                if g == 0:
                                    ins = nc.vector.tensor_tensor(to, rot[:, 0], rot[:, 1], ALU.add)
                                else:
                                    ins = nc.vector.tensor_tensor(to.rearrange("p (r j) -> p j r", r=RES), a, b, ALU.add)
                            ins.then_inc(rot_done, 1)
                            dve.wait_ge(rot_done, NROT * i + m + 3)
                            m += 1
                            if m <= 8:
                                ada.add(dve, i, 2 * m - 2)
                                ada.add(dve, i, 2 * m - 1)
                            if m in (8, 12):
                                ada.finish(dve, i, m // 4 - 2, side)
                for step in range(UNITS + 4):
                    u = step
                    if u < UNITS:
                        r = u // 2 % RES
                        if u:
                            dve.wait_ge(mask_ready, RES)
                        dve.wait_ge(sc_done, UNITS * i + u + 1)
                        dve.wait_ge(p_ready, UNITS * i + u + 1)
                        if u == 0:
                            dve.sem_inc(turn_seen, 1)
                        nc.vector.tensor_tensor_reduce(sm[:, u % 2], sc[:, 0:KEYS], mask[:, r], 1.0, -3e38,
                                                       ALU.add, ALU.max, top[:, u % 2:u % 2 + 1]).then_inc(sm_ready, 1)
                        dve.wait_ge(sm_ready, UNITS * i + u + 2)
                        nc.vector.tensor_scalar(bias[:, u % 2:u % 2 + 1], top[:, u % 2:u % 2 + 1], -HD ** -0.5, None,
                                                ALU.mult).then_inc(bias_ready, 1)
                    u = step - 2
                    if 0 <= u < UNITS:
                        hh, slot = u % 2, u // 2 % 2
                        dve.wait_ge(p_ready, UNITS * i + u + 3)
                        ch.do(nc.vector.reciprocal(rden[:, u % 4:u % 4 + 1], den[:, u % 4:u % 4 + 1]))
                        dve.wait_ge(pv_done, UNITS * i + u + 3)
                        ch.sync()
                        nc.vector.tensor_scalar(o[:, slot, HD * hh:HD * hh + HD], pv[:, HD * hh:HD * hh + HD],
                                                rden[:, u % 4:u % 4 + 1], None, ALU.mult).then_inc(o_ready, 1)
                    u = step - 3
                    if u >= 0 and u % 2:
                        pair, r = u // 8, u // 2 % RES
                        dve.wait_ge(oT_done, UNITS // 2 * i + u // 2 + 1)
                        nc.vector.tensor_scalar(oT[:, bass.ds(2 * i + pair, 1), r::RES].rearrange("p a q -> p (a q)"),
                                                po[:, 0:P], 1.0, None, ALU.mult).then_inc(oT_ready, 1)
                assert DVE_T == ch.n, ch.n
            out = Chain(dve, dve_step, DVE_T * QUADS + first)
            for n in range(4):
                for t in range(TT):
                    j = n * TT + t
                    cols = slice(n * QF, (n + 1) * QF)
                    dve.wait_ge(y_done, j + 1)
                    nc.vector.scalar_tensor_tensor(out=rot[:, j % 2, 0:QF], in0=c.ada[:, 2, cols], scalar=1.0,
                                                   in1=proj[j % 2][:, 0:QF], op0=ALU.add, op1=ALU.mult).then_inc(y_used, 1)
                    dve.wait_ge(y_used, j + 1)
                    out.do(nc.vector.scalar_tensor_tensor(out=c.x[:, t, cols], in0=c.x[:, t, cols], scalar=ALPHA,
                                                          in1=rot[:, j % 2, 0:QF], op0=ALU.mult, op1=ALU.add))
                    out.sync()

        @block.tensor
        def _(pe):
            pe.sem_inc(proj_done, PC)
            pe.sem_inc(tp_done, 2)
            pe.sem_inc(pv_done, 2)
            pe.sem_inc(p_ready, 2)
            with pe.Fori(0, QUADS) as i:
                n = 0
                for j, (g, s) in enumerate(chunks):
                    pe.wait_ge(w_in[j % SLOTS], 16 * (CH // SLOTS) * i + 16 * (j // SLOTS + 1))
                    for half_ in range(2):
                        pe.wait_ge(proj_free, NPROJ * i + n + 1)
                        if s == 2:
                            for t in range(2 * half_, 2 * half_ + 2):
                                toks = slice(t * P, (t + 1) * P) if g == 0 else slice(t, SEQ, RES)
                                for kk in range(KT):
                                    last = nc.tensor.matmul(proj[n % 2][:, t % 2 * QF:(t % 2 + 1) * QF],
                                                            c.hT[:, kk, toks], w[:, j % SLOTS, kk], start=kk == 0, stop=kk == KT - 1)
                        else:
                            for kk in range(KT):
                                last = nc.tensor.matmul(proj[n % 2][:], w[:, j % SLOTS, kk, half_ * P:(half_ + 1) * P],
                                                        c.hT[:, kk, :], start=kk == 0, stop=kk == KT - 1)
                        last.then_inc(proj_done, 1)
                        n += 1
                        if n == 2 * 6:
                            ada.total(pe, i, 0, side)
                pe.wait_ge(ada.ready, 4 * i + 2)
                ada.total(pe, i, 1, side)
                for step in range(UNITS + 4):
                    u = step
                    if u < UNITS:
                        pair, r, hh = u // 8, u // 2 % RES, u % 2
                        if u == 0:
                            pe.wait_ge(rot_done, NROT * (i + 1) + 2)
                        pe.wait_ge(sm_ready, UNITS * i + u + 1)
                        qs = [q[:, g, pair, hh, r * P:(r + 1) * P] for g in range(GROUPS)]
                        nc.tensor.matmul(sc[:, 0:SEQ], qs[0], k[:, 0, pair], start=True, stop=True)
                        for g in (1, 2):
                            last = nc.tensor.matmul(sc[:, SEQ + (g - 1) * P:SEQ + g * P], qs[g],
                                                    k[:, g, pair, r * P:(r + 1) * P], start=True, stop=True)
                        last.then_inc(sc_done, 1)
                    u = step - 1
                    if 0 <= u < UNITS:
                        pe.wait_ge(p_ready, UNITS * i + u + 3)
                        pe.wait_ge(pT_ready, UNITS * i + u + 1)
                        for b in range(6):
                            last = nc.tensor.transpose(tp[:, b], prob[:, u % 2, b * P:(b + 1) * P], c.ident[:])
                        last.then_inc(tp_done, 1)
                    u = step - 2
                    if 0 <= u < UNITS:
                        pair, r = u // 8, u // 2 % RES
                        pe.wait_ge(pT_ready, UNITS * i + u + 2)
                        pe.wait_ge(o_ready, UNITS * i + u + 1)
                        if u == 0:
                            pe.wait_ge(ada.ready, 4 * i + 4)
                        for b in range(6):
                            g, t = (0, b) if b < 4 else (b - 3, r)
                            last = nc.tensor.matmul(pv[:, 0:P], probT[:, u % 2, b * P:(b + 1) * P],
                                                    v[:, g, t, pair * P:(pair + 1) * P], start=b == 0, stop=b == 5)
                        last.then_inc(pv_done, 1)
                    u = step - 3
                    if u >= 0 and u % 2:
                        pe.wait_ge(o_ready, UNITS * i + u + 2)
                        if u > 1:
                            pe.wait_ge(oT_ready, UNITS // 2 * i + u // 2)
                        nc.tensor.transpose(po[:, 0:P], o[:, u // 2 % 2], c.ident[:]).then_inc(oT_done, 1)
                pe.wait_ge(oT_ready, UNITS // 2 * (i + 1))
            for n in range(4):
                pe.wait_ge(w_in[n % SLOTS], 16 * (CH // SLOTS) * QUADS + 16 * (n // SLOTS + 1))
                for t in range(TT):
                    j = n * TT + t
                    if j >= 2:
                        pe.wait_ge(y_used, j - 1)
                    for kk in range(KT):
                        last = nc.tensor.matmul(proj[j % 2][:, 0:QF], oT[:, kk, t * P:(t + 1) * P], w[:, n % SLOTS, kk],
                                                start=kk == 0, stop=kk == KT - 1)
                    last.then_inc(y_done, 1)
    st.close(gathers=True)


def moe_stage(nc, c, A, l, h_rows, y_rows):
    st = Stage(nc, f"moe{l}")
    BIG = 1e5
    PICKED = 1e30
    F2 = 2 * ED

    w13 = st.sb("w13", [P, 4, 2, KT, ED])
    w2 = st.sb("w2", [P, 2, 2, D])
    xg = st.sb("xg", [P, 2, D])
    xT = st.sb("xT", [P, 2, KT, P])
    act_s = st.sb("act_s", [P, 2, F2])
    hh = st.sb("hh", [P, 2, ED])
    hT2 = st.sb("hT2", [P, 2, 2, P])
    ysb = st.sb("ysb", [P, 2, D])
    acc = st.sb("acc", [P, TT, D])
    rw = st.sb("rw", [P, KT, NE])
    rb = st.sb("rb", [P, NE])
    lgT = st.sb("lgT", [NE, SEQ])
    sg = st.sb("sg", [P, TT, NE])
    biased = st.sb("biased", [P, TT, NE])
    g8 = st.sb("g8", [P, TT, NG, 8])
    gpad = st.sb("gpad", [P, TT, 16])
    grep = st.sb("grep", [P, TT, 8])
    gm = st.sb("gm", [P, TT, 16])
    v8 = st.sb("v8", [P, TT, 8])
    left = st.sb("left", [P, TT, NE])
    sel = st.sb("sel", [P, TT, NE], BF16)
    self32 = st.sb("self32", [P, TT, NE])
    kth = st.sb("kth", [P, TT, NE])
    hot = st.sb("hot", [P, TOPK, NE])
    gate = st.sb("gate", [P, TT, TOPK])
    gsum = st.sb("gsum", [P, TT])
    pos = st.sb("pos", [P, TT, NE])
    cnt = st.sb("cnt", [P, NE])
    nov = st.sb("nov", [P, NE])
    incl = st.sb("incl", [P, NE])
    ind = st.sb("ind", [P, OVB, NE])
    ovf = st.sb("ovf", [P, 2, OVB])
    ovi = st.sb("ovi", [1, OVB + 1], I32)
    ii = st.sb("ii", [P, P], I32)
    iota = st.sb("iota", [P, P])
    pidx = st.sb("pidx", [P, TT, 2], I32)
    tokf = st.sb("tokf", [P, TT, 2])
    num = st.sb("num", [P, TT, NE, 5], BF16)
    offs = st.sb("offs", [P, 5], BF16)
    onesb = st.sb("onesb", [P, P], BF16)
    before = st.sb("before", [P, P], BF16)
    onehot = st.sb("onehot", [P, 2, TT, P], BF16)
    pcol = st.sb("pcol", [P, TT])
    idx = st.sb("idx", [P, 2], U32)
    yidx = st.sb("yidx", [P, 4], U32)

    tx = [st.ps(f"tx{n}", [P, 4, P]) for n in range(2)]
    th = st.ps("th", [P, 2, P])
    py = [st.ps(f"py{n}", [P, 512]) for n in range(2)]
    pr = st.ps("pr", [P, 512])
    ph = [st.ps("ph", [P, 512]), pr]
    pi = st.ps("pi", [P, 512])

    sem = st.sem
    small_in, consts = sem("small_in"), sem("consts")
    sh_in, sh_h, sh_silu, sh_hh, sh_th, sh_hT, sh_y, sh_acc = [sem("sh_" + x) for x in "in h silu hh th hT y acc".split()]
    lg_done, lg_ready, lg_turned, sg_ready = sem("lg_done"), sem("lg_ready"), sem("lg_turned"), sem("sg_ready")
    dve_step, iota_ready, sel_ready, pos_done, route_ready = (sem("dve_step"), sem("iota_ready"), sem("sel_ready"),
                                                              sem("pos_done"), sem("route_ready"))
    w13_in = [sem(f"w13_in{n}") for n in range(4)]
    w2_in = [sem(f"w2_in{n}") for n in range(2)]
    xg_in, ov_xg_in = [sem(f"xg_in{n}") for n in range(2)], sem("ov_xg_in")
    y_out = [sem(f"y_out{n}") for n in range(2)]
    hot_ready, idx_done, idx_ready, gathering = sem("hot_ready"), sem("idx_done"), sem("idx_ready"), sem("gathering")
    tx_done, xT_act, xT_dve = sem("tx_done"), sem("xT_act"), sem("xT_dve")
    h_done, silu_ready, hh_ready, th_done, hT_ready = (sem("h_done"), sem("silu_ready"), sem("hh_ready"), sem("th_done"),
                                                       sem("hT_ready"))
    y_done, y_ready = sem("y_done"), sem("y_ready")
    ov = {x: sem("ov_" + x) for x in
          "w pcol hot idxp idx tx xTa xTd h silu hh th hT y ysb out turn".split()}
    YG = 2
    NYG = 8
    yg_in = [sem(f"yg_in{n}") for n in range(NYG)]
    yg_used = sem("yg_used")
    yg = w13[:].rearrange("p s a k e -> p (s a k e)").rearrange("p (n k d) -> p n k d", k=YG, d=D)

    def w13_src(wt):
        return wt.rearrange("(p k) n -> p k n", k=KT)

    def flat(ap):
        return ap.rearrange("p k n -> p (k n)")

    w1d = A["expert_w1"][l].rearrange("e (p k) n -> p e (k n)", k=KT)
    w3d = A["expert_w3"][l].rearrange("e (p k) n -> p e (k n)", k=KT)
    w2d = A["expert_w2"][l].rearrange("e (p k) n -> p e (k n)", k=2)

    def w13_slot(b, a):
        return w13[:, b, a].rearrange("p k n -> p (k n)")

    def w2_slot(b):
        return w2[:, b].rearrange("p k n -> p (k n)")

    def half(n):
        return slice(n * 512, (n + 1) * 512)

    FIRST, LAST = "first", "last"

    def for_all_steps(eng, step):
        for u in range(4):
            step(0, u, FIRST)
        with eng.Fori(1, NE // 4 - 1) as i:
            for u in range(4):
                step(i, u, None)
        for u in range(4):
            step(NE // 4 - 1, u, LAST)

    def column(t, e, where):
        return t[:, :, bass.ds(e, 1)] if where is None else t[:, :, e:e + 1]

    with nc.Block() as block:
        @block.sync
        def _(sp):
            sp.dma_start(rw[:], A["router_w"][l].rearrange("(p k) n -> p k n", k=KT)).then_inc(small_in, 16)
            sp.dma_start(rb[:], A["router_bias"][l].rearrange("(a n) -> a n", a=1).partition_broadcast(P)).then_inc(small_in, 16)
            def up_weights(e, slot):
                sp.dma_start(w13_slot(slot, 0), w1d[:, bass.ds(e, 1)].rearrange("p a n -> p (a n)")).then_inc(w13_in[slot], 16)
                sp.dma_start(w13_slot(slot, 1), w3d[:, bass.ds(e, 1)].rearrange("p a n -> p (a n)")).then_inc(w13_in[slot], 16)

            def down_weights(e, slot):
                sp.dma_start(w2_slot(slot), w2d[:, bass.ds(e, 1)].rearrange("p a n -> p (a n)")).then_inc(w2_in[slot], 16)

            for a, name in enumerate(("shared_w1", "shared_w3")):
                sp.dma_start(w13_slot(3, a), flat(w13_src(A[name][l]))).then_inc(sh_in, 16)
            sp.dma_start(w2_slot(1), A["shared_w2"][l].rearrange("(p k) n -> p (k n)", k=2)).then_inc(sh_in, 16)
            up_weights(0, 0), down_weights(0, 0), up_weights(1, 1), up_weights(2, 2)
            sp.wait_ge(sh_h, TT)
            sp.wait_ge(sh_y, TT)
            with sp.Fori(0, NE // 4 - 1) as i:
                for u in range(4):
                    e = 4 * i + u
                    sp.wait_ge(h_done, e + 3)
                    sp.sem_inc(gathering, 1)
                    up_weights(e + 3, (u + 3) % 4)
                    sp.wait_ge(y_done, e + 2)
                    sp.sem_inc(gathering, 1)
                    down_weights(e + 1, (u + 1) % 2)
            for e in range(NE - 4, NE - 1):
                if e + 3 < NE:
                    sp.wait_ge(h_done, e + 3)
                    up_weights(e + 3, 3)
                sp.wait_ge(y_done, e + 2)
                down_weights(e + 1, (e + 1) % 2)
            sp.wait_ge(y_done, NE + 2)
            sp.wait_ge(route_ready, 1)
            total = sp.value_load(ovi[0:1, OVB:OVB + 1], min_val=0, max_val=OVB)
            with sp.Fori(0, OVB) as j:
                with sp.If(j < total):
                    e = sp.value_load(ovi[0:1, bass.ds(j, 1)], min_val=0, max_val=NE - 1)
                    sp.dma_start(w13_slot(0, 0), w1d[:, bass.ds(e, 1)].rearrange("p a n -> p (a n)")).then_inc(ov["w"], 16)
                    sp.dma_start(w13_slot(0, 1), w3d[:, bass.ds(e, 1)].rearrange("p a n -> p (a n)")).then_inc(ov["w"], 16)
                    sp.dma_start(w2_slot(0), w2d[:, bass.ds(e, 1)].rearrange("p a n -> p (a n)")).then_inc(ov["w"], 16)
                    sp.wait_ge(ov["out"], 16 * j + 16)
                    sp.sem_inc(ov["turn"], 1)
            for b in range(2):
                sp.wait_ge(y_out[b], 16 * (NE // 2))
            for m in range(TT * TOPK // YG):
                t, k = m * YG // TOPK, m * YG % TOPK
                if m >= NYG:
                    sp.wait_ge(yg_used, YG * (m - NYG + 1))
                sp.dma_start(yg[:, m % NYG], y_rows.rearrange("(t p k) d -> p t k d", p=P, k=TOPK)[:, t, k:k + YG])\
                  .then_inc(yg_in[m % NYG], 16)

        @block.scalar
        def _(act):
            act.wait_ge(lg_done, 1)
            nc.scalar.copy(lgT[:], pr[0:NE, :]).then_inc(lg_ready, 1)
            act.wait_ge(lg_turned, 1)
            nc.scalar.activation(sg[:], pi[:, 0:TT * NE].rearrange("p (t e) -> p t e", e=NE), ACT.Sigmoid).then_inc(sg_ready, 1)
            for t in range(TT):
                act.wait_ge(sh_h, t + 1)
                if t >= 2:
                    act.wait_ge(sh_hh, t - 1)
                nc.scalar.activation(act_s[:, t % 2, 0:ED], ph[0][:, 0:ED], ACT.Silu).then_inc(sh_silu, 1)
                nc.scalar.copy(act_s[:, t % 2, ED:F2], ph[0][:, ED:F2]).then_inc(sh_silu, 1)
                act.wait_ge(sh_th, t + 1)
                nc.scalar.copy(hT2[:, t % 2], th[:]).then_inc(sh_hT, 1)
                for n in range(2):
                    act.wait_ge(sh_y, t + 1)
                    nc.scalar.copy(acc[:, t, n * 512:(n + 1) * 512], py[n][:]).then_inc(sh_acc, 1)
            def turned(k, slot):
                act.wait_ge(tx_done, 2 * k + 2)
                nc.scalar.copy(xT[:, slot, 0:4], tx[0][:]).then_inc(xT_act, 1)

            def silu(k, slot):
                act.wait_ge(h_done, k + 3)
                nc.scalar.activation(act_s[:, slot, 0:ED], ph[slot][:, 0:ED], ACT.Silu).then_inc(silu_ready, 1)

            def step(i, u, where):
                e, b = 4 * i + u, u % 2
                act.wait_ge(th_done, e + 1)
                nc.scalar.copy(hT2[:, b], th[:]).then_inc(hT_ready, 1)
                if where != LAST or u < 2:
                    turned(e + 2, b)
                if where != LAST or u < 3:
                    silu(e + 1, 1 - b)
                if where != FIRST or u >= 2:
                    act.wait_ge(y_out[b], 32 * i + 16 * (u // 2))
                act.wait_ge(y_done, e + 3)
                for n in range(2):
                    nc.scalar.copy(ysb[:, b, half(n)], py[n][:]).then_inc(y_ready, 1)

            act.sem_inc(y_ready, 1)
            turned(0, 0), silu(0, 0), turned(1, 1)
            for_all_steps(act, step)
            act.wait_ge(y_out[0], 16 * (NE // 2))
            act.wait_ge(y_out[1], 16 * (NE // 2))
            total = act.value_load(ovi[0:1, OVB:OVB + 1], min_val=0, max_val=OVB)
            with act.Fori(0, OVB) as j:
                with act.If(j < total):
                    act.wait_ge(ov["tx"], 2 * j + 2)
                    nc.scalar.copy(xT[:, 0, 0:4], tx[0][:]).then_inc(ov["xTa"], 1)
                    act.wait_ge(ov["h"], j + 1)
                    nc.scalar.activation(act_s[:, 0, 0:ED], ph[0][:, 0:ED], ACT.Silu).then_inc(ov["silu"], 1)
                    act.wait_ge(ov["th"], j + 1)
                    nc.scalar.copy(hT2[:, 0], th[:]).then_inc(ov["hT"], 1)
                    act.wait_ge(ov["y"], j + 1)
                    for n in range(2):
                        nc.scalar.copy(ysb[:, 0, n * 512:(n + 1) * 512], py[n][:]).then_inc(ov["ysb"], 1)
                    act.wait_ge(ov["out"], 16 * j + 16)
                    act.sem_inc(ov["turn"], 1)

        @block.gpsimd
        def _(pool):
            pool.iota(ii[:], pattern=[[1, P]], base=0, channel_multiplier=0).then_inc(iota_ready, 1)
            pool.iota(pidx[:, :, 0], pattern=[[P, TT]], base=-SEQ, channel_multiplier=0).then_inc(iota_ready, 1)
            pool.iota(pidx[:, :, 1], pattern=[[0, TT]], base=0, channel_multiplier=1).then_inc(iota_ready, 1)
            pool.memset(before[:], 1.0).then_inc(iota_ready, 1)
            pool.memset(xg[:], 0.0).then_inc(iota_ready, 1)
            pool.wait_ge(iota_ready, 5)
            pool.affine_select(out=before[:], in_=before[:], compare_op=ALU.is_gt, fill=0.0, base=0,
                               pattern=[[1, P]], channel_multiplier=-1).then_inc(iota_ready, 1)
            for t in range(TT):
                pool.wait_ge(sh_silu, 2 * t + 2)
                if t >= 2:
                    pool.wait_ge(sh_th, t - 1)
                pool.tensor_tensor(hh[:, t % 2], act_s[:, t % 2, 0:ED], act_s[:, t % 2, ED:F2], ALU.mult).then_inc(sh_hh, 1)

            def gather(b, done):
                pool.indirect_dma_start(xg[:, b], None, h_rows, bass.IndirectOffsetOnAxis(ap=idx[:, b:b + 1], axis=0),
                                        bounds_check=SEQ - 1, oob_is_err=False).then_inc(done, 16)

            def scatter(b, s, done):
                pool.indirect_dma_start(y_rows, bass.IndirectOffsetOnAxis(ap=yidx[:, s:s + 1], axis=0), ysb[:, b], None,
                                        bounds_check=SEQ * TOPK - 1, oob_is_err=False).then_inc(done, 16)

            for b in range(2):
                pool.wait_ge(idx_ready, 2 * b + 1)
                gather(b, xg_in[b])
            pool.wait_ge(idx_ready, 5)
            pool.wait_ge(tx_done, 2)
            gather(0, xg_in[0])

            def step(i, u, where):
                e, b = 4 * i + u, u % 2
                if where != LAST or u < 1:
                    pool.wait_ge(idx_ready, 2 * e + 7)
                    pool.wait_ge(tx_done, 2 * e + 4)
                    pool.sem_inc(gathering, 1)
                    gather(1 - b, xg_in[1 - b])
                pool.wait_ge(y_ready, 2 * e + 3)
                pool.sem_inc(gathering, 1)
                scatter(b, u, y_out[b])

            for_all_steps(pool, step)
            for b in range(2):
                pool.wait_ge(xg_in[b], 16 * (NE // 2))
                pool.wait_ge(y_out[b], 16 * (NE // 2))
            total = pool.value_load(ovi[0:1, OVB:OVB + 1], min_val=0, max_val=OVB)
            with pool.Fori(0, OVB) as j:
                with pool.If(j < total):
                    pool.wait_ge(ov["idx"], 2 * j + 2)
                    pool.sem_inc(gathering, 1)
                    gather(0, ov_xg_in)
                    pool.wait_ge(ov["ysb"], 2 * j + 2)
                    pool.sem_inc(gathering, 1)
                    scatter(0, 0, ov["out"])
                    pool.wait_ge(ov["out"], 16 * j + 16)
                    pool.sem_inc(ov["turn"], 1)

        @block.vector
        def _(dve):
            ch = Chain(dve, dve_step)
            dve.wait_ge(iota_ready, 6)
            ch.do(nc.vector.tensor_copy(iota[:], ii[:]))
            ch.do(nc.vector.tensor_copy(tokf[:], pidx[:]))
            for a in range(2):
                ch.do(nc.vector.memset(offs[:, 2 * a:2 * a + 1], float(SEQ * (1, TOPK)[a] // P)))
                ch.do(nc.vector.memset(offs[:, 2 * a + 1:2 * a + 2 + a], 0.0))
            ch.sync()
            for a in range(2):
                v = tokf[:].rearrange("p t (o a) -> p t o a", o=1).broadcast_to([P, TT, NE, 2])
                nc.vector.tensor_scalar(num[:, :, :, 2 * a:2 * a + 2], v, float((1, TOPK)[a]), None, ALU.mult).then_inc(consts, 1)
            nc.vector.memset(num[:, :, :, 4], 0.0).then_inc(consts, 1)
            nc.vector.memset(onesb[:], 1.0).then_inc(consts, 1)
            ch.do(nc.vector.memset(gpad[:], NEG))
            ch.do(nc.vector.memset(grep[:], NEG))
            dve.wait_ge(small_in, 32)
            dve.wait_ge(sg_ready, 1)
            rbb = rb[:].rearrange("p (a n) -> p a n", a=1).broadcast_to([P, TT, NE])
            ch.do(nc.vector.tensor_tensor(biased[:], sg[:], rbb, ALU.add))
            ch.sync()
            for t in range(TT):
                for g in range(NG):
                    ch.do(nc.vector.max(g8[:, t, g], biased[:, t, g * 8:(g + 1) * 8]))
            ch.sync()
            ch.do(nc.vector.tensor_tensor(gpad[:, :, 0:NG], g8[:, :, :, 0], g8[:, :, :, 1], ALU.add))
            ch.sync()
            for t in range(TT):
                ch.do(nc.vector.max(v8[:, t], gpad[:, t, 0:NG]))
            ch.sync()
            ch.do(nc.vector.tensor_copy(grep[:, :, 0:TOPG], v8[:, :, 0:TOPG]))
            ch.sync()
            for t in range(TT):
                ch.do(nc.vector.match_replace(gm[:, t], grep[:, t], gpad[:, t], PICKED))
            ch.sync()
            ch.do(nc.vector.tensor_scalar(gm[:], gm[:], PICKED, NEG, ALU.not_equal, ALU.mult))
            ch.sync()
            gmb = gm[:, :, 0:NG].rearrange("p t (g o) -> p t g o", o=1).broadcast_to([P, TT, NG, 8])
            ch.do(nc.vector.tensor_tensor(biased[:].rearrange("p t (g e) -> p t g e", e=8),
                                          biased[:].rearrange("p t (g e) -> p t g e", e=8), gmb, ALU.add))
            ch.sync()
            for t in range(TT):
                ch.do(nc.vector.max(v8[:, t], biased[:, t]))
            ch.sync()
            for t in range(TT):
                ch.do(nc.vector.match_replace(left[:, t], v8[:, t], biased[:, t], PICKED))
            ch.sync()
            nc.vector.tensor_scalar(sel[:], left[:], PICKED, None, ALU.is_equal).then_inc(sel_ready, 1)
            ch.do(nc.vector.tensor_scalar(self32[:], left[:], PICKED, None, ALU.is_equal))
            ch.sync()
            for t in range(TT):
                ch.do(nc.vector.tensor_tensor_scan(kth[:, t], c.ones[:, 0:NE], self32[:, t], 0.0, ALU.mult, ALU.add))
            ch.do(nc.vector.tensor_scalar(left[:], self32[:], -BIG, BIG, ALU.mult, ALU.add))
            ch.sync()
            ch.do(nc.vector.tensor_tensor(kth[:], kth[:], self32[:], ALU.subtract))
            ch.sync()
            dve.wait_ge(consts, 4)
            nc.vector.tensor_copy(num[:, :, 0:NE, 4], kth[:]).then_inc(consts, 1)
            dve.wait_ge(pos_done, 1)
            prt = pr[:, 0:TT * NE].rearrange("p (t e) -> p t e", e=NE)
            ch.do(nc.vector.tensor_copy(cnt[:], pr[:, TT * NE:(TT + 1) * NE]))
            nc.vector.tensor_tensor(pos[:, :, 0:NE], left[:], prt, ALU.add).then_inc(hot_ready, 1)
            dve.wait_ge(hot_ready, 1)
            dve.wait_ge(sel_ready, 1)
            def one_hot(col, b):
                return nc.vector.tensor_tensor(onehot[:, b], iota[:].rearrange("p (a n) -> p a n", a=1).broadcast_to([P, TT, P]),
                                               col.broadcast_to([P, TT, P]), ALU.is_equal)

            def to_gather(b):
                with nc.allow_low_precision(reason="sums of small integers"):
                    return nc.vector.tensor_reduce(idx[:, b:b + 1], pi[:, 0:2], AX.X, ALU.add)

            def to_write(s):
                with nc.allow_low_precision(reason="sums of small integers"):
                    return nc.vector.tensor_reduce(yidx[:, s:s + 1], pi[:, 2:5], AX.X, ALU.add)

            def turned(k, slot):
                dve.wait_ge(tx_done, 2 * k + 2)
                nc.vector.tensor_copy(xT[:, slot, 4:8], tx[1][:]).then_inc(xT_dve, 1)

            def product(k, slot):
                dve.wait_ge(silu_ready, k + 1)
                nc.vector.tensor_tensor(hh[:, slot], act_s[:, slot, 0:ED], ph[slot][:, ED:F2], ALU.mult).then_inc(hh_ready, 1)

            for e in range(3):
                one_hot(pos[:, :, e:e + 1], e % 2).then_inc(hot_ready, 1)
                dve.wait_ge(idx_done, e + 1)
                if e == 2:
                    dve.wait_ge(xg_in[0], 16)
                to_gather(e % 2).then_inc(idx_ready, 1)
                to_write(e).then_inc(idx_ready, 1)
            one_hot(pos[:, :, 3:4], 1).then_inc(hot_ready, 1)
            turned(0, 0), turned(1, 1), product(0, 0)

            def step(i, u, where):
                e, b = 4 * i + u, u % 2
                if where != LAST or u < 1:
                    dve.wait_ge(idx_done, e + 4)
                    to_gather(1 - b).then_inc(idx_ready, 1)
                if where != LAST:
                    one_hot(column(pos, e + 4, where), b).then_inc(hot_ready, 1)
                if where != LAST or u < 2:
                    turned(e + 2, b)
                if where != LAST or u < 3:
                    product(e + 1, 1 - b)
                if where == FIRST:
                    gates(u)
                if where != LAST or u < 1:
                    if where != FIRST or u:
                        dve.wait_ge(y_out[1 - b], 32 * i + 16 * ((u + 1) // 2))
                    to_write((u + 3) % 4).then_inc(idx_ready, 1)
                if where == FIRST and u == 3:
                    further_blocks()

            def gates(t):
                ch.do(nc.vector.tensor_tensor(kth[:, t], kth[:, t], left[:, t], ALU.add))
                ch.sync()
                ks = iota[:, 0:TOPK].rearrange("p (k o) -> p k o", o=1).broadcast_to([P, TOPK, NE])

                def per_k(ap):
                    return ap.rearrange("p (a n) -> p a n", a=1).broadcast_to([P, TOPK, NE])

                ch.do(nc.vector.tensor_tensor(hot[:], per_k(kth[:, t]), ks, ALU.is_equal))
                ch.sync()
                ch.do(nc.vector.tensor_tensor(hot[:], hot[:], per_k(sg[:, t]), ALU.mult))
                ch.sync()
                ch.do(nc.vector.tensor_reduce(gate[:, t], hot[:], AX.X, ALU.add))
                ch.sync()

            def further_blocks():
                ch.do(nc.vector.tensor_reduce(gsum[:], gate[:], AX.X, ALU.add))
                ch.sync()
                ch.do(nc.vector.reciprocal(gsum[:], gsum[:]))
                ch.sync()
                ch.do(nc.vector.scalar_tensor_tensor(out=gate[:], in0=gate[:], scalar=ROUTED_SCALE,
                                                     in1=gsum[:].rearrange("p (t o) -> p t o", o=1).broadcast_to([P, TT, TOPK]),
                                                     op0=ALU.mult, op1=ALU.mult))
                ch.sync()
                ch.do(nc.vector.tensor_scalar(nov[:], cnt[:], float(CAP), None, ALU.is_gt))
                ch.sync()
                for n in range(2, SEQ // CAP):
                    ch.do(nc.vector.scalar_tensor_tensor(out=nov[:], in0=cnt[:], scalar=float(n * CAP), in1=nov[:],
                                                         op0=ALU.is_gt, op1=ALU.add))
                    ch.sync()
                ch.do(nc.vector.tensor_tensor_scan(incl[:], c.ones[:, 0:NE], nov[:], 0.0, ALU.mult, ALU.add))
                ch.sync()
                jj = iota[:, 0:OVB].rearrange("p (j o) -> p j o", o=1).broadcast_to([P, OVB, NE])

                def per_j(ap):
                    return ap.rearrange("p (a n) -> p a n", a=1).broadcast_to([P, OVB, NE])

                ch.do(nc.vector.tensor_tensor(ind[:], per_j(incl[:]), jj, ALU.is_le))
                ch.sync()
                ch.do(nc.vector.tensor_reduce(ovf[:, 0], ind[:], AX.X, ALU.add))
                ch.sync()
                ch.do(nc.vector.tensor_tensor(ind[:], ind[:], per_j(nov[:]), ALU.mult))
                ch.do(nc.vector.tensor_scalar(ovi[0:1, 0:OVB], ovf[0:1, 0], float(NE - 1), None, ALU.min))
                ch.sync()
                ch.do(nc.vector.tensor_reduce(ovf[:, 1], ind[:], AX.X, ALU.add))
                ch.sync()
                ch.do(nc.vector.tensor_tensor(ovf[:, 1], iota[:, 0:OVB], ovf[:, 1], ALU.subtract))
                ch.sync()
                ch.do(nc.vector.tensor_scalar(ovf[:, 1], ovf[:, 1], float(CAP), float(CAP), ALU.mult, ALU.add))
                ch.sync()
                nc.vector.tensor_copy(ovi[0:1, OVB:OVB + 1], incl[0:1, NE - 1:NE]).then_inc(route_ready, 1)
                dve.wait_ge(route_ready, 1)

            for_all_steps(dve, step)
            total = dve.value_load(ovi[0:1, OVB:OVB + 1], min_val=0, max_val=OVB)
            dve.wait_ge(xg_in[0], 16 * (NE // 2))
            dve.wait_ge(xg_in[1], 16 * (NE // 2))
            for b in range(2):
                dve.wait_ge(y_out[b], 16 * (NE // 2))
            with dve.Fori(0, OVB) as j:
                with dve.If(j < total):
                    e = dve.value_load(ovi[0:1, bass.ds(j, 1)], min_val=0, max_val=NE - 1)
                    nc.vector.tensor_scalar(pcol[:], pos[:, :, bass.ds(e, 1)].rearrange("p t a -> p (t a)"),
                                            ovf[:, 1, bass.ds(j, 1)], None, ALU.subtract).then_inc(ov["pcol"], 1)
                    dve.wait_ge(ov["pcol"], j + 1)
                    one_hot(pcol[:].rearrange("p (t o) -> p t o", o=1), 0).then_inc(ov["hot"], 1)
                    dve.wait_ge(ov["idxp"], j + 1)
                    with nc.allow_low_precision(reason="sums of small integers"):
                        nc.vector.tensor_reduce(idx[:, 0:1], pi[:, 0:2], AX.X, ALU.add).then_inc(ov["idx"], 1)
                        nc.vector.tensor_reduce(yidx[:, 0:1], pi[:, 2:5], AX.X, ALU.add).then_inc(ov["idx"], 1)
                    dve.wait_ge(ov["tx"], 2 * j + 2)
                    nc.vector.tensor_copy(xT[:, 0, 4:8], tx[1][:]).then_inc(ov["xTd"], 1)
                    dve.wait_ge(ov["silu"], j + 1)
                    nc.vector.tensor_tensor(hh[:, 0], act_s[:, 0, 0:ED], ph[0][:, ED:F2], ALU.mult).then_inc(ov["hh"], 1)
                    dve.wait_ge(ov["out"], 16 * j + 16)
                    dve.sem_inc(ov["turn"], 1)
            dve.wait_ge(sh_acc, 2 * TT)
            for t in range(TT):
                for k in range(TOPK):
                    n, m = t * TOPK + k, (t * TOPK + k) // YG
                    dve.wait_ge(yg_in[m % NYG], 16 * (m // NYG + 1))
                    nc.vector.scalar_tensor_tensor(out=acc[:, t], in0=yg[:, m % NYG, k % YG], scalar=gate[:, t, k:k + 1],
                                                   in1=acc[:, t], op0=ALU.mult, op1=ALU.add).then_inc(yg_used, 1)
                    dve.wait_ge(yg_used, n + 1)
                ch.do(nc.vector.scalar_tensor_tensor(out=acc[:, t], in0=c.ada[:, 2], scalar=1.0, in1=acc[:, t],
                                                     op0=ALU.add, op1=ALU.mult))
                ch.sync()
                ch.do(nc.vector.scalar_tensor_tensor(out=c.x[:, t], in0=c.x[:, t], scalar=ALPHA, in1=acc[:, t],
                                                     op0=ALU.mult, op1=ALU.add))
            ch.sync()

        @block.tensor
        def _(pe):
            def up(out, xt, ws, done):
                for k in range(KT):
                    last = nc.tensor.matmul(out[:], xt(k), w13[:, ws, :, k], start=k == 0, stop=k == KT - 1)
                last.then_inc(done, 1)

            def turn_h(b, done):
                for k in range(2):
                    last = nc.tensor.transpose(th[:, k], hh[:, b, k::2], c.ident[:])
                last.then_inc(done, 1)

            def down(b, wb, done):
                for n in range(2):
                    for k in range(2):
                        last = nc.tensor.matmul(py[n][:], hT2[:, b, k], w2[:, wb, k, n * 512:(n + 1) * 512],
                                                start=k == 0, stop=k == 1)
                last.then_inc(done, 1)

            def turn_x(b, done):
                for n in range(2):
                    for k in range(4):
                        last = nc.tensor.transpose(tx[n][:, k], xg[:, b, 4 * n + k::KT], c.ident[:])
                    last.then_inc(done, 1)

            def rows(b, at, done):
                nc.tensor.matmul(pi[:, 0:5], onesb[:], offs[:], start=True, stop=False)
                for t in range(TT):
                    last = nc.tensor.matmul(pi[:, 0:5], onehot[:, b, t], at(t), start=False, stop=t == TT - 1)
                last.then_inc(done, 1)

            pe.wait_ge(small_in, 32)
            for k in range(KT):
                last = nc.tensor.matmul(pr[0:NE, :], rw[:, k], c.hT[:, k], start=k == 0, stop=k == KT - 1)
            last.then_inc(lg_done, 1)
            pe.wait_ge(lg_ready, 1)
            for t in range(TT):
                last = nc.tensor.transpose(pi[:, t * NE:(t + 1) * NE], lgT[:, t * P:(t + 1) * P], c.ident[0:NE, 0:NE])
            last.then_inc(lg_turned, 1)
            pe.wait_ge(sh_in, 48)
            for t in range(TT):
                if t:
                    pe.wait_ge(sh_silu, 2 * t)
                up(ph[0], lambda k: c.hT[:, k, t * P:(t + 1) * P], 3, sh_h)
                if t == 2:
                    pe.wait_ge(sel_ready, 1)
                    pe.wait_ge(consts, 4)
                    for tt in range(TT):
                        for s in range(tt + 1):
                            nc.tensor.matmul(pr[:, tt * NE:(tt + 1) * NE], before[:] if s == tt else onesb[:], sel[:, s],
                                             start=s == 0, stop=s == tt)
                    for s in range(TT):
                        last = nc.tensor.matmul(pr[:, TT * NE:(TT + 1) * NE], onesb[:], sel[:, s], start=s == 0, stop=s == TT - 1)
                    last.then_inc(pos_done, 1)
                pe.wait_ge(sh_hh, t + 1)
                if t:
                    pe.wait_ge(sh_hT, t)
                turn_h(t % 2, sh_th)
                pe.wait_ge(sh_hT, t + 1)
                if t:
                    pe.wait_ge(sh_acc, 2 * t)
                down(t % 2, 1, sh_y)
            for e in range(3):
                pe.wait_ge(sg_ready, 1)
                pe.wait_ge(consts, 5)
                pe.wait_ge(hot_ready, e + 2)
                if e:
                    pe.wait_ge(idx_ready, 2 * e)
                rows(e % 2, lambda t: num[:, t, e], idx_done)
            pe.wait_ge(xg_in[0], 16)
            turn_x(0, tx_done)
            pe.sem_inc(h_done, 2)
            pe.sem_inc(y_done, 2)
            pe.wait_ge(sh_silu, 2 * TT)
            pe.wait_ge(sh_acc, 2 * TT)
            pe.wait_ge(idx_ready, 6)
            pe.wait_ge(w13_in[0], 32)
            pe.wait_ge(xT_act, 1)
            pe.wait_ge(xT_dve, 1)
            up(ph[0], lambda k: xT[:, 0, k], 0, h_done)
            pe.wait_ge(xg_in[1], 16)
            turn_x(1, tx_done)

            def step(i, u, where):
                e, b = 4 * i + u, u % 2
                if where != LAST or u < 1:
                    pe.wait_ge(hot_ready, e + 5)
                    pe.wait_ge(idx_ready, 2 * e + 6)
                    at = (lambda t: num[:, t, bass.ds(e + 3, 1)].rearrange("p a n -> p (a n)")) if where is None else \
                        (lambda t: num[:, t, e + 3])
                    rows(1 - b, at, idx_done)
                if where != LAST or u < 3:
                    pe.wait_ge(w13_in[(u + 1) % 4], 32 * i + 32 + 32 * (u // 3))
                    pe.wait_ge(xT_act, e + 2)
                    pe.wait_ge(xT_dve, e + 2)
                    up(ph[1 - b], lambda k: xT[:, 1 - b, k], (u + 1) % 4, h_done)
                pe.wait_ge(hh_ready, e + 1)
                turn_h(b, th_done)
                if where != LAST or u < 2:
                    pe.wait_ge(xg_in[b], 32 * i + 16 * (u // 2) + 32)
                    turn_x(b, tx_done)
                pe.wait_ge(hT_ready, e + 1)
                pe.wait_ge(w2_in[b], 32 * i + 16 * (u // 2) + 16)
                pe.wait_ge(y_ready, 2 * e + 1)
                down(b, b, y_done)

            for_all_steps(pe, step)
            total = pe.value_load(ovi[0:1, OVB:OVB + 1], min_val=0, max_val=OVB)
            with pe.Fori(0, OVB) as j:
                with pe.If(j < total):
                    ex = pe.value_load(ovi[0:1, bass.ds(j, 1)], min_val=0, max_val=NE - 1)
                    pe.wait_ge(ov["hot"], j + 1)
                    rows(0, lambda t: num[:, t, bass.ds(ex, 1)].rearrange("p a n -> p (a n)"), ov["idxp"])
                    pe.wait_ge(ov_xg_in, 16 * j + 16)
                    turn_x(0, ov["tx"])
                    pe.wait_ge(ov["w"], 48 * j + 48)
                    pe.wait_ge(ov["xTa"], j + 1)
                    pe.wait_ge(ov["xTd"], j + 1)
                    up(ph[0], lambda k: xT[:, 0, k], 0, ov["h"])
                    pe.wait_ge(ov["hh"], j + 1)
                    turn_h(0, ov["th"])
                    pe.wait_ge(ov["hT"], j + 1)
                    down(0, 0, ov["y"])
                    pe.wait_ge(ov["out"], 16 * j + 16)
                    pe.sem_inc(ov["turn"], 1)
    st.close(gathers=True)


def delta_stage(nc, c, A, ada_rows):
    st = Stage(nc, "gdn")
    HP = 2
    TURNS = GH // HP
    PF = HP * GD
    KINDS = 4
    K_, Q_, V_, Z_ = 1, 0, 2, 3
    NCONV = 3 * HP
    W = GH * GD
    TH = TT * GH
    BASE = 16
    LEVELS = (16, 32, 64)

    w = st.sb("w", [P, 2, KT, PF])
    raw = st.sb("raw", [P, 2, CONV - 1 + SEQ])
    acc = st.sb("acc", [P, 2, SEQ])
    oT = st.sb("oT", [P, GH, SEQ])
    wab = st.sb("wab", [P, KT, 2 * GH])
    abT = st.sb("abT", [2 * GH, SEQ])
    convw = st.sb("convw", [CONV * 3 * GH, P])
    convT = st.sb("convT", [P, CONV, 3, GH])
    cw = st.sb("cw", [P, CONV, 3, HP])
    nw = st.sb("nw", [P, 1])
    eps = st.sb("eps", [P, 1])
    dtb = st.sb("dtb", [P, GH])
    alog = st.sb("alog", [P, GH])
    soft = st.sb("soft", [P, 5, TT, GH])
    tab = st.sb("tab", [P, 7, TT, GH])
    G_, NGC, NBEG, KD, BE, NBE, GL = range(7)
    cur = st.sb("cur", [P, 7, TT, HP])
    masks = st.sb("masks", [P, 6, P])

    def tiles(name):
        return [st.sb(f"{name}{h}", [P, TT, P]) for h in range(HP)]

    kT, qT, vT, zs, qg, dT, vn, kbe, kdec, vb, M, P0, P1, Q0, Q1, E0, E1, qkT = [
        tiles(x) for x in "kT qT vT zs qg dT vn kbe kdec vb M P0 P1 Q0 Q1 E0 E1 qkT".split()]
    wT = vT
    S = st.sb("S", [P, HP, 2, P])
    ada = AdaRows(nc, c, st, A, (3,), ada_rows, 4)
    pj = [st.ps(f"pj{n}", [P, 512]) for n in range(2)]
    ps = [[st.ps(f"ps{h}{n}", [P, TT, P]) for n in range(3)] for h in range(HP)]

    r, q = np.arange(P)[:, None], np.arange(P)[None, :]
    below = (q < r) & (q // BASE == r // BASE)
    links = [(r // (2 * b) == q // (2 * b)) & (r // b % 2 == 1) & (q // b % 2 == 0) for b in LEVELS]
    side = [pj[n][:, 0:ada.QA // 2] for n in range(2)]
    table = np.stack([below, below.T] + links + [np.where(r <= q, 0.0, NEG)], 1).astype(np.float32)
    BELOW, ABOVE, LINK, CAUSAL = 0, 1, 2, 5
    mask_dram = nc.inline_tensor(table.reshape(P, -1), "delta_masks")

    sem = st.sem
    small_in, abw_in, conv_in = sem("small_in"), sem("abw_in"), sem("conv_in")
    w_in = [sem(f"w_in{n}") for n in range(2)]
    proj_done, proj_free, silu_ready, conv_ready = sem("proj_done"), sem("proj_free"), sem("silu_ready"), sem("conv_ready")
    ab_done, ab_copied, ab_turned, conv_turned = sem("ab_done"), sem("ab_copied"), sem("ab_turned"), sem("conv_turned")
    x_ready, act_small, g_ready, gc_done, kd_arg, tab_ready = (sem("x_ready"), sem("act_small"), sem("g_ready"), sem("gc_done"),
                                                               sem("kd_arg"), sem("tab_ready"))
    k_ln, q_ln, o_ln = sem("k_ln"), sem("q_ln"), sem("o_ln")
    dve_step, conv_step, cur_ready, gb_ready = sem("dve_step"), sem("conv_step"), sem("cur_ready"), sem("gb_ready")
    w_asked = sem("w_asked")
    (gc_row, eg_row, masked, dT_ready, kk_sq, kk_norm, k_rs, kT_ready, q_sq, q_norm, q_rs, qT_ready, k_turned, kbe_ready,
     kdec_ready, kk_done, G_ready, G_turned, M_ready, M_turned, Q_ready, P_ready, E_first, v_turned, vb_ready, qk_done,
     qk_ready, qg_ready) = [sem(x) for x in (
        "gc_row eg_row masked dT_ready k_sq k_norm k_rs kT_ready q_sq q_norm q_rs qT_ready k_turned kbe_ready "
        "kdec_ready kk_done G_ready G_turned M_ready M_turned Q_ready P_ready E_first v_turned vb_ready qk_done "
        "qk_ready qg_ready").split()]
    pw_done = [sem(f"pw_done{n}") for n in range(3)]
    pw_ready = [sem(f"pw_ready{n}") for n in range(3)]
    e_done = [sem(f"e_done{n}") for n in range(6)]
    e_ready = [sem(f"e_ready{n}") for n in range(6)]
    d_done = [sem(f"d_done{n}") for n in range(3)]
    d_ready = [sem(f"d_ready{n}") for n in range(3)]
    n_ready = [sem(f"n_ready{n}") for n in range(3)]
    y_done_ = [sem(f"y_done{n}") for n in range(3)]
    y_ready_ = [sem(f"y_ready{n}") for n in range(3)]
    w_done, w_ready = sem("w_done"), sem("w_ready")
    vn_done, vn_ready, s_done, s_ready, o_done = sem("vn_done"), sem("vn_ready"), sem("s_done"), sem("s_ready"), sem("o_done")
    o_sq, o_norm, o_rs, o_scaled, o_ready = sem("o_sq"), sem("o_norm"), sem("o_rs"), sem("o_scaled"), sem("o_ready")
    out_done, out_used = sem("out_done"), sem("out_used")

    w_dram = A["gdn_w_in"][0].rearrange("(p k) n -> p k n", k=KT)
    wo_dram = A["gdn_w_out"][0].rearrange("(k p) n -> p k n", p=P)
    order = [K_, Q_, V_, Z_]

    def rowp(ap):
        return ap.rearrange("(a n) -> a n", a=1).partition_broadcast(P)

    def flat(t):
        return t[:].rearrange("p t n -> p (t n)")

    def over_t(m):
        return m.rearrange("p (a n) -> p a n", a=1).broadcast_to([P, TT, P])

    def col(kind, h):
        return cur[:, kind, :, h:h + 1].broadcast_to([P, TT, P])

    with nc.Block() as block:
        @block.sync
        def _(sp):
            sp.dma_start(wab[:], w_dram[:, :, 4 * W:4 * W + 2 * GH]).then_inc(abw_in, 16)
            sp.sem_inc(ada.stored, 16)
            with sp.Fori(0, TURNS) as i:
                ada.load_bias(sp, i)
                for n, kind in enumerate(order):
                    sp.wait_ge(proj_done, 2 * KINDS * i + 2 * n + 2)
                    sp.sem_inc(w_asked, 1)
                    sp.dma_start(w[:, n % 2], w_dram[:, :, bass.ds(i * PF + kind * W, PF)]).then_inc(w_in[n % 2], 16)
                ada.store(sp, i)
            for n in range(4):
                if n < 2:
                    sp.wait_ge(proj_done, 2 * KINDS * TURNS + 2 * n + 2)
                else:
                    sp.wait_ge(out_done, TT * (n - 1))
                sp.dma_start(w[:, n % 2], wo_dram[:, :, n * PF:(n + 1) * PF]).then_inc(w_in[n % 2], 16)
            sp.wait_ge(ada.stored, 16 * TURNS + 16)

        @block.scalar
        def _(act):
            act.dma_start(convw[:], A["gdn_conv_w"][0].rearrange("j (m p) -> (j m) p", p=P)).then_inc(conv_in, 16)
            act.dma_start(nw[:], A["gdn_norm_w"][0].rearrange("(p a) -> p a", a=1)).then_inc(small_in, 16)
            act.dma_start(dtb[:], rowp(A["gdn_dt_bias"][0])).then_inc(small_in, 16)
            act.dma_start(alog[:], rowp(A["gdn_a_log"][0])).then_inc(small_in, 16)
            act.dma_start(masks[:], mask_dram.ap().rearrange("p (m n) -> p m n", n=P)).then_inc(small_in, 16)
            act.wait_ge(ab_done, 1)
            nc.scalar.copy(abT[:], pj[0][0:2 * GH, :]).then_inc(ab_copied, 1)
            act.wait_ge(ab_turned, 1)
            abv = pj[1][:, 0:2 * TH].rearrange("p (t n) -> p t n", t=TT)
            nc.scalar.activation(tab[:, BE], abv[:, :, GH:2 * GH], ACT.Sigmoid).then_inc(act_small, 1)
            act.wait_ge(small_in, 64)
            nc.scalar.activation(alog[:], alog[:], ACT.Exp).then_inc(act_small, 1)
            act.wait_ge(x_ready, 1)
            nc.scalar.activation(soft[:, 1], soft[:, 1], ACT.Exp, scale=-1.0).then_inc(act_small, 1)
            act.wait_ge(x_ready, 2)
            nc.scalar.activation(soft[:, 3], soft[:, 2], ACT.Ln).then_inc(act_small, 1)
            act.wait_ge(gc_done, 1)
            gcv = pj[1][:, 0:2 * TH].rearrange("p (s t n) -> p s t n", s=2, t=TT)
            nc.scalar.activation(soft[:, 0], gcv[:, 0], ACT.Exp).then_inc(act_small, 1)
            nc.scalar.activation(tab[:, GL], gcv[:, 1], ACT.Exp).then_inc(act_small, 1)
            act.wait_ge(kd_arg, 1)
            nc.scalar.activation(tab[:, KD], soft[:, 1], ACT.Exp).then_inc(act_small, 1)
            act.sem_inc(silu_ready, 2)
            act.sem_inc(proj_free, 2)

            with act.Fori(0, TURNS) as i:
                def copy_raw(m):
                    act.wait_ge(proj_done, 2 * KINDS * i + m + 5)
                    act.wait_ge(conv_ready, NCONV * i + m + 1)
                    nc.scalar.copy(raw[:, m % 2, CONV - 1:], pj[m % 2][:]).then_inc(proj_free, 1)

                def silu(m, dst):
                    act.wait_ge(conv_ready, NCONV * i + m + 3)
                    nc.scalar.activation(flat(dst), acc[:, m % 2], ACT.Silu).then_inc(silu_ready, 1)

                copy_raw(0), copy_raw(1), silu(0, kT[0]), silu(1, kT[1])
                copy_raw(2), silu(2, qT[0]), copy_raw(3), silu(3, qT[1])
                for h in range(HP):
                    act.wait_ge(kk_norm, 2 * i + h + 1)
                    nc.scalar.activation(E1[h][:], ps[h][1][:], ACT.Ln, bias=eps[:]).then_inc(k_ln, 1)
                copy_raw(4)
                for h in range(HP):
                    act.wait_ge(q_norm, 2 * i + h + 1)
                    nc.scalar.activation(E0[h][:], ps[h][2][:], ACT.Ln, bias=eps[:]).then_inc(q_ln, 1)
                for h in range(HP):
                    act.wait_ge(k_ln, 2 * i + h + 1)
                    nc.scalar.activation(E1[h][:], E1[h][:], ACT.Exp, scale=-0.5).then_inc(k_rs, 1)
                for h in range(HP):
                    act.wait_ge(q_ln, 2 * i + h + 1)
                    nc.scalar.activation(E0[h][:], E0[h][:], ACT.Exp, scale=-0.5).then_inc(q_rs, 1)
                for h in range(HP):
                    n = 2 * i + h + 1
                    act.wait_ge(masked, n)
                    nc.scalar.activation(qg[h][:], ps[h][0][:], ACT.Exp).then_inc(eg_row, 1)
                    for t in range(TT):
                        last = nc.scalar.activation(dT[h][:, t], P1[h][:, t], ACT.Exp, bias=cur[:, NGC, t, h:h + 1])
                    last.then_inc(dT_ready, 1)
                silu(4, vT[0]), copy_raw(5), silu(5, vT[1])
                for h in range(HP):
                    act.wait_ge(proj_done, 2 * KINDS * i + 6 + h + 5)
                    nc.scalar.activation(flat(zs[h]), pj[h][:], ACT.Silu).then_inc(proj_free, 1)
                for s, (pd, qd) in enumerate(((P1, Q1), (P0, Q0), (P1, None))):
                    for h in range(HP):
                        act.wait_ge(pw_done[s], 2 * i + h + 1)
                        if s == 1:
                            act.wait_ge(E_first, 2 * i + h + 1)
                        last = nc.scalar.copy(pd[h][:], ps[h][1][:])
                        if qd is not None:
                            last = nc.scalar.copy(qd[h][:], ps[h][2][:])
                        last.then_inc(pw_ready[s], 1)
                for s in range(3):
                    for h in range(HP):
                        act.wait_ge(d_done[s], 2 * i + h + 1)
                        nc.scalar.copy(Q0[h][:], ps[h][1][:]).then_inc(d_ready[s], 1)
                        act.wait_ge(y_done_[s], 2 * i + h + 1)
                        nc.scalar.copy(Q1[h][:], ps[h][2][:]).then_inc(y_ready_[s], 1)
                for h in range(HP):
                    act.wait_ge(w_done, 2 * i + h + 1)
                    nc.scalar.copy(wT[h][:], ps[h][2][:]).then_inc(w_ready, 1)
                for t in range(TT):
                    for h in range(HP):
                        act.wait_ge(vn_done, 2 * TT * i + 2 * t + h + 1)
                        nc.scalar.copy(vn[h][:, t], ps[h][1][:, t]).then_inc(vn_ready, 1)
                for h in range(HP):
                    act.wait_ge(o_done, 2 * i + h + 1)
                    nc.scalar.activation(P1[h][:], ps[h][0][:], ACT.Square, scale=GD ** -0.5).then_inc(o_sq, 1)
                for h in range(HP):
                    act.wait_ge(o_norm, 2 * i + h + 1)
                    nc.scalar.activation(Q1[h][:], ps[h][1][:], ACT.Ln, bias=eps[:]).then_inc(o_ln, 1)
                for h in range(HP):
                    act.wait_ge(o_ln, 2 * i + h + 1)
                    nc.scalar.activation(Q1[h][:], Q1[h][:], ACT.Exp, scale=-0.5).then_inc(o_rs, 1)

        @block.gpsimd
        def _(pool):
            pool.wait_ge(tab_ready, 1)
            with pool.Fori(0, TURNS) as i:
                for j in range(4):
                    ada.load(pool, i, j)
                for h in range(HP):
                    pool.wait_ge(cur_ready, 2 * i + 2)
                    pool.tensor_tensor(Q1[h][:], over_t(c.ones[:]), col(G_, h), ALU.mult).then_inc(gb_ready, 1)
                for h in range(HP):
                    pool.wait_ge(silu_ready, NCONV * i + h + 3)
                    pool.tensor_tensor(E1[h][:], kT[h][:], kT[h][:], ALU.mult).then_inc(kk_sq, 1)
                for h in range(HP):
                    pool.wait_ge(silu_ready, NCONV * i + h + 5)
                    pool.tensor_tensor(E0[h][:], qT[h][:], qT[h][:], ALU.mult).then_inc(q_sq, 1)
                for j in range(4, 8):
                    ada.load(pool, i, j)
                for h in range(HP):
                    pool.wait_ge(qT_ready, 2 * i + h + 1)
                    pool.wait_ge(eg_row, 2 * i + h + 1)
                    pool.tensor_tensor(qg[h][:], qT[h][:], qg[h][:], ALU.mult).then_inc(qg_ready, 1)
                for h in range(HP):
                    pool.wait_ge(M_ready, 2 * i + h + 1)
                    pool.tensor_tensor(P0[h][:], M[h][:], over_t(masks[:, BELOW]), ALU.mult).then_inc(P_ready, 1)
                for s, dst in enumerate((P0, P1, P0)):
                    for h in range(HP):
                        pool.wait_ge((e_done[1], e_done[2], y_done_[0])[s], 2 * i + h + 1)
                        if s == 0:
                            pool.wait_ge(pw_done[2], 2 * i + h + 1)
                        pool.tensor_tensor(dst[h][:], M[h][:], over_t(masks[:, LINK + s]), ALU.mult).then_inc(n_ready[s], 1)

        @block.vector
        def _(dve):
            ch = Chain(dve, dve_step)
            dve.sem_inc(conv_ready, 2)
            dve.sem_inc(o_ready, 2)
            ada.credits(dve)
            ch.do(nc.vector.memset(raw[:, :, 0:CONV - 1], 0.0))
            ch.do(nc.vector.memset(eps[:], RMS_EPS))
            dve.wait_ge(small_in, 64)
            dve.wait_ge(conv_turned, 1)
            ch.do(nc.vector.tensor_copy(convT[:].rearrange("p a b c -> p (a b c)"), pj[0][:, 0:CONV * 3 * GH]))
            dve.wait_ge(act_small, 1)
            abv = pj[1][:, 0:2 * TH].rearrange("p (t n) -> p t n", t=TT)
            x, e, u, ln, fix = [soft[:, n] for n in range(5)]
            ch.do(nc.vector.tensor_tensor(x, abv[:, :, 0:GH], dtb[:].rearrange("p (a n) -> p a n", a=1).broadcast_to([P, TT, GH]), ALU.add))
            ch.sync()
            nc.vector.scalar_tensor_tensor(out=e, in0=x, scalar=-1.0, in1=x, op0=ALU.mult, op1=ALU.max).then_inc(x_ready, 1)
            dve.wait_ge(act_small, 3)
            nc.vector.tensor_scalar(u, e, 1.0, None, ALU.add).then_inc(x_ready, 1)
            dve.wait_ge(x_ready, 2)
            ch.do(nc.vector.tensor_scalar(fix, u, -1.0, None, ALU.add))
            ch.sync()
            ch.do(nc.vector.tensor_tensor(fix, e, fix, ALU.subtract))
            dve.wait_ge(act_small, 4)
            ch.do(nc.vector.reciprocal(u, u))
            ch.sync()
            ch.do(nc.vector.tensor_tensor(fix, fix, u, ALU.mult))
            ch.sync()
            ch.do(nc.vector.tensor_tensor(fix, fix, ln, ALU.add))
            ch.sync()
            ch.do(nc.vector.scalar_tensor_tensor(out=fix, in0=x, scalar=0.0, in1=fix, op0=ALU.max, op1=ALU.add))
            ch.sync()
            nc.vector.scalar_tensor_tensor(out=tab[:, G_], in0=fix, scalar=-1.0,
                                           in1=alog[:].rearrange("p (a n) -> p a n", a=1).broadcast_to([P, TT, GH]),
                                           op0=ALU.mult, op1=ALU.mult).then_inc(g_ready, 1)
            dve.wait_ge(act_small, 6)
            gcv = pj[1][:, 0:2 * TH].rearrange("p (s t n) -> p s t n", s=2, t=TT)
            ch.do(nc.vector.tensor_scalar(tab[:, NGC], gcv[:, 0], -1.0, None, ALU.mult))
            ch.sync()
            nc.vector.tensor_tensor(e, gcv[:, 1], tab[:, NGC], ALU.add).then_inc(kd_arg, 1)
            ch.do(nc.vector.tensor_scalar(tab[:, NBE], tab[:, BE], -1.0, None, ALU.mult))
            ch.sync()
            dve.wait_ge(act_small, 7)
            nc.vector.tensor_tensor(tab[:, NBEG], tab[:, NBE], x, ALU.mult).then_inc(tab_ready, 1)
            dve.wait_ge(tab_ready, 1)
            first = ch.n

            with dve.Fori(0, TURNS) as i:
                nc.vector.tensor_scalar(cur[:], tab[:, :, :, bass.ds(HP * i, HP)], 1.0, None, ALU.mult).then_inc(cur_ready, 1)
                nc.vector.tensor_scalar(cw[:], convT[:, :, :, bass.ds(HP * i, HP)], 1.0, None, ALU.mult).then_inc(cur_ready, 1)
                dve.wait_ge(cur_ready, 2 * i + 2)

                def conv(m, kind):
                    dve.wait_ge(proj_free, 2 * KINDS * i + m + 3)
                    dve.wait_ge(silu_ready, NCONV * i + m + 1)
                    for j in range(CONV):
                        src, to = raw[:, m % 2, j:j + SEQ], acc[:, m % 2]
                        wj = cw[:, j, kind, m % 2:m % 2 + 1]
                        if j == 0:
                            last = nc.vector.tensor_scalar(to, src, wj, None, ALU.mult)
                        else:
                            last = nc.vector.scalar_tensor_tensor(out=to, in0=src, scalar=wj, in1=to, op0=ALU.mult, op1=ALU.add)
                        if j < CONV - 1:
                            last.then_inc(conv_step, 1)
                            dve.wait_ge(conv_step, 3 * NCONV * i + 3 * m + j + 1)
                    last.then_inc(conv_ready, 1)

                def with_column(out, in_, kind, h, done):
                    nc.vector.tensor_tensor(out[:], in_[:], col(kind, h), ALU.mult).then_inc(done, 1)

                def mask_causal(h):
                    dve.wait_ge(gc_row, 2 * i + h + 1)
                    nc.vector.tensor_tensor(P1[h][:], ps[h][0][:], over_t(masks[:, CAUSAL]), ALU.add).then_inc(masked, 1)

                def norm_k(h):
                    dve.wait_ge(k_rs, 2 * i + h + 1)
                    nc.vector.tensor_tensor(kT[h][:], kT[h][:], E1[h][:], ALU.mult).then_inc(kT_ready, 1)

                def norm_q(h):
                    dve.wait_ge(q_rs, 2 * i + h + 1)
                    nc.vector.scalar_tensor_tensor(out=qT[h][:], in0=qT[h][:], scalar=GD ** -0.5, in1=E0[h][:],
                                                   op0=ALU.mult, op1=ALU.mult).then_inc(qT_ready, 1)

                def keys(h):
                    dve.wait_ge(k_turned, 2 * i + h + 1)
                    with_column(kbe[h], ps[h][2], NBEG, h, kbe_ready)
                    with_column(kdec[h], ps[h][2], KD, h, kdec_ready)
                    dve.wait_ge(kk_done, 2 * i + h + 1)
                    dve.wait_ge(dT_ready, 2 * i + h + 1)
                    nc.vector.tensor_tensor(Q1[h][:], ps[h][1][:], dT[h][:], ALU.mult).then_inc(G_ready, 1)

                conv(0, K_), conv(1, K_), mask_causal(0), mask_causal(1)
                for m, kind in ((2, Q_), (3, Q_), (4, V_)):
                    ada.add(dve, i, 2 * m - 4), ada.add(dve, i, 2 * m - 3)
                    conv(m, kind)
                ada.add(dve, i, 6), ada.add(dve, i, 7)
                norm_k(0), norm_k(1), norm_q(0), norm_q(1), keys(0), keys(1), conv(5, V_)
                for h in range(HP):
                    dve.wait_ge(G_turned, 2 * i + h + 1)
                    with_column(M[h], ps[h][1], NBE, h, M_ready)
                for h in range(HP):
                    n = 2 * i + h + 1
                    dve.wait_ge(v_turned, n)
                    with_column(vb[h], ps[h][2], BE, h, vb_ready)
                    dve.wait_ge(M_turned, n)
                    nc.vector.tensor_tensor(Q0[h][:], ps[h][1][:], over_t(masks[:, ABOVE]), ALU.mult).then_inc(Q_ready, 1)
                    dve.wait_ge(qk_done, n)
                    nc.vector.tensor_tensor(qkT[h][:], ps[h][0][:], dT[h][:], ALU.mult).then_inc(qk_ready, 1)
                    dve.wait_ge(Q_ready, n)
                    nc.vector.tensor_tensor(E0[h][:], Q0[h][:], over_t(c.ident[:]), ALU.add).then_inc(E_first, 1)
                ada.finish(dve, i, 0, side)
                for s in range(6):
                    src, dst = (E0, E1) if s % 2 == 0 else (E1, E0)
                    for h in range(HP):
                        dve.wait_ge(e_done[s], 2 * i + h + 1)
                        dve.wait_ge(E_first if s == 0 else e_ready[s - 1], 2 * i + h + 1)
                        nc.vector.tensor_tensor(dst[h][:], ps[h][0][:], src[h][:], ALU.add).then_inc(e_ready[s], 1)
                for t in range(TT - 1):
                    for h in range(HP):
                        dve.wait_ge(s_done, 2 * (TT - 1) * i + 2 * t + h + 1)
                        if t == 0:
                            last = nc.vector.tensor_copy(S[:, h, 0], ps[h][2][:, t])
                        else:
                            dve.wait_ge(s_ready, 2 * (TT - 1) * i + 2 * (t - 1) + h + 1)
                            last = nc.vector.scalar_tensor_tensor(out=S[:, h, t % 2], in0=S[:, h, (t - 1) % 2],
                                                                  scalar=cur[:, GL, t, h:h + 1], in1=ps[h][2][:, t],
                                                                  op0=ALU.mult, op1=ALU.add)
                        last.then_inc(s_ready, 1)
                for h in range(HP):
                    n = 2 * i + h + 1
                    dve.wait_ge(o_rs, n)
                    nc.vector.scalar_tensor_tensor(out=kT[h][:], in0=ps[h][0][:], scalar=nw[:], in1=Q1[h][:],
                                                   op0=ALU.mult, op1=ALU.mult).then_inc(o_scaled, 1)
                    dve.wait_ge(o_scaled, n)
                    nc.vector.tensor_tensor(oT[:, bass.ds(2 * i + h, 1)].rearrange("p a n -> p (a n)"), flat(kT[h]), flat(zs[h]),
                                            ALU.mult).then_inc(o_ready, 1)
            out = Chain(dve, dve_step, first)
            for n in range(4):
                for t in range(TT):
                    j = n * TT + t
                    cols = slice(n * PF, (n + 1) * PF)
                    dve.wait_ge(out_done, j + 1)
                    nc.vector.scalar_tensor_tensor(out=acc[:, j % 2, 0:PF], in0=c.ada[:, 2, cols], scalar=1.0,
                                                   in1=pj[j % 2][:, 0:PF], op0=ALU.add, op1=ALU.mult).then_inc(out_used, 1)
                    dve.wait_ge(out_used, j + 1)
                    out.do(nc.vector.scalar_tensor_tensor(out=c.x[:, t, cols], in0=c.x[:, t, cols], scalar=ALPHA,
                                                          in1=acc[:, j % 2, 0:PF], op0=ALU.mult, op1=ALU.add))
                    out.sync()

        @block.tensor
        def _(pe):
            def each(out, lhsT, rhs):
                for t in range(TT):
                    last = nc.tensor.matmul(out[:, t], lhsT(t), rhs(t), start=True, stop=True)
                return last

            def turn(out, src, done):
                for t in range(TT):
                    last = nc.tensor.transpose(out[:, t], src[:, t], c.ident[:])
                last.then_inc(done, 1)

            pe.wait_ge(abw_in, 16)
            for k in range(KT):
                last = nc.tensor.matmul(pj[0][0:2 * GH, :], wab[:, k], c.hT[:, k], start=k == 0, stop=k == KT - 1)
            last.then_inc(ab_done, 1)
            pe.wait_ge(ab_copied, 1)
            for t in range(TT):
                last = nc.tensor.transpose(pj[1][:, t * 2 * GH:(t + 1) * 2 * GH], abT[:, t * P:(t + 1) * P],
                                           c.ident[0:2 * GH, 0:2 * GH])
            last.then_inc(ab_turned, 1)
            NW = CONV * 3 * GH
            pe.wait_ge(conv_in, 16)
            nc.tensor.transpose(pj[0][:, 0:NW], convw[:], c.ident[0:NW, 0:NW]).then_inc(conv_turned, 1)
            pe.wait_ge(g_ready, 1)
            pe.wait_ge(act_small, 1)
            gflat = tab[:, G_].rearrange("p t n -> p (t n)")
            nc.tensor.matmul(pj[1][:, 0:TH], c.upper[:], gflat, start=True, stop=True)
            nc.tensor.matmul(pj[1][:, TH:2 * TH], c.ones[:], gflat, start=True, stop=True).then_inc(gc_done, 1)
            pe.wait_ge(tab_ready, 1)
            pe.sem_inc(proj_done, 4)

            with pe.Fori(0, TURNS) as i:
                def proj(m):
                    n, h = m // 2, m % 2
                    if h == 0:
                        pe.wait_ge(w_in[n % 2], 32 * i + 16 * (n // 2) + 16)
                    pe.wait_ge(proj_free, 2 * KINDS * i + m + 1)
                    for k in range(KT):
                        last = nc.tensor.matmul(pj[h][:], w[:, n % 2, k, h * P:(h + 1) * P], c.hT[:, k], start=k == 0, stop=k == KT - 1)
                    last.then_inc(proj_done, 1)

                def sum_squares(bank, sq, ready, h, done):
                    pe.wait_ge(ready, 2 * i + h + 1)
                    nc.tensor.matmul(bank[:].rearrange("p t n -> p (t n)"), c.ones[:], flat(sq), start=True, stop=True).then_inc(done, 1)

                def keys(h):
                    pe.wait_ge(kT_ready, 2 * i + h + 1)
                    turn(ps[h][2], kT[h], k_turned)
                    each(ps[h][1], lambda t: kT[h][:, t], lambda t: kT[h][:, t]).then_inc(kk_done, 1)

                def turn_g(h):
                    pe.wait_ge(G_ready, 2 * i + h + 1)
                    turn(ps[h][1], Q1[h], G_turned)

                def late(h):
                    n = 2 * i + h + 1
                    pe.wait_ge(silu_ready, NCONV * i + 4 + h + 3)
                    pe.wait_ge(qT_ready, n)
                    pe.wait_ge(kdec_ready, n)
                    turn(ps[h][2], vT[h], v_turned)
                    pe.wait_ge(M_ready, n)
                    turn(ps[h][1], M[h], M_turned)
                    each(ps[h][0], lambda t: kT[h][:, t], lambda t: qT[h][:, t]).then_inc(qk_done, 1)

                pe.wait_ge(o_ready, 2 * i + 2)
                proj(0)
                for h in range(HP):
                    pe.wait_ge(gb_ready, 2 * i + h + 1)
                    each(ps[h][0], lambda t: Q1[h][:, t], lambda t: c.upper[:]).then_inc(gc_row, 1)
                proj(1)
                proj(2), sum_squares(ps[0][1], E1[0], kk_sq, 0, kk_norm)
                proj(3), sum_squares(ps[1][1], E1[1], kk_sq, 1, kk_norm)
                sum_squares(ps[0][2], E0[0], q_sq, 0, q_norm)
                proj(4), sum_squares(ps[1][2], E0[1], q_sq, 1, q_norm)
                proj(5), keys(0), keys(1)
                proj(6), turn_g(0), turn_g(1)
                proj(7), late(0), late(1)
                pe.wait_ge(proj_free, 2 * KINDS * i + 10)
                ada.total(pe, i, 0, side)
                for h in range(HP):
                    n = 2 * i + h + 1
                    pe.wait_ge(P_ready, n)
                    pe.wait_ge(Q_ready, n)
                    each(ps[h][1], lambda t: Q0[h][:, t], lambda t: P0[h][:, t])
                    each(ps[h][2], lambda t: P0[h][:, t], lambda t: Q0[h][:, t]).then_inc(pw_done[0], 1)
                for s, (p, q, e, ready) in enumerate(((P1, Q1, E0, E_first), (P0, Q0, E1, e_ready[0]), (P1, None, E0, e_ready[1]))):
                    for h in range(HP):
                        n = 2 * i + h + 1
                        pe.wait_ge(pw_ready[s], n)
                        if s < 2:
                            last = each(ps[h][1], lambda t: q[h][:, t], lambda t: p[h][:, t])
                            if s == 1:
                                last.then_inc(pw_done[2], 1)
                        if s == 0:
                            each(ps[h][2], lambda t: p[h][:, t], lambda t: q[h][:, t]).then_inc(pw_done[1], 1)
                            pe.wait_ge(qk_ready, n)
                        pe.wait_ge(ready, n)
                        each(ps[h][0], lambda t: p[h][:, t], lambda t: e[h][:, t]).then_inc(e_done[s], 1)
                for s in range(3):
                    link, e = (P0, P1, P0)[s], (E1, E0, E1)[s]
                    for h in range(HP):
                        n = 2 * i + h + 1
                        pe.wait_ge(e_ready[s + 2], n)
                        turn(ps[h][1], e[h], d_done[s])
                        pe.wait_ge(n_ready[s], n)
                        each(ps[h][2], lambda t: link[h][:, t], lambda t: e[h][:, t]).then_inc(y_done_[s], 1)
                    for h in range(HP):
                        n = 2 * i + h + 1
                        pe.wait_ge(d_ready[s], n)
                        pe.wait_ge(y_ready_[s], n)
                        each(ps[h][0], lambda t: Q0[h][:, t], lambda t: Q1[h][:, t]).then_inc(e_done[s + 3], 1)
                for h in range(HP):
                    n = 2 * i + h + 1
                    pe.wait_ge(e_ready[5], n)
                    pe.wait_ge(kbe_ready, n)
                    each(ps[h][2], lambda t: kbe[h][:, t], lambda t: E0[h][:, t]).then_inc(w_done, 1)
                for t in range(TT):
                    for h in range(HP):
                        n = 2 * i + h + 1
                        if t == 0:
                            pe.wait_ge(vb_ready, n)
                            pe.wait_ge(w_ready, n)
                        last = nc.tensor.matmul(ps[h][1][:, t], E0[h][:, t], vb[h][:, t], start=True, stop=t == 0)
                        if t:
                            pe.wait_ge(s_ready, 2 * (TT - 1) * i + 2 * (t - 1) + h + 1)
                            last = nc.tensor.matmul(ps[h][1][:, t], wT[h][:, t], S[:, h, (t - 1) % 2], start=False, stop=True)
                        last.then_inc(vn_done, 1)
                        if t:
                            if t == 1:
                                pe.wait_ge(qg_ready, n)
                            nc.tensor.matmul(ps[h][0][:, t], S[:, h, (t - 1) % 2], qg[h][:, t], start=True, stop=False)
                    for h in range(HP):
                        pe.wait_ge(vn_ready, 2 * TT * i + 2 * t + h + 1)
                        if t < TT - 1:
                            nc.tensor.matmul(ps[h][2][:, t], kdec[h][:, t], vn[h][:, t], start=True, stop=True).then_inc(s_done, 1)
                        last = nc.tensor.matmul(ps[h][0][:, t], vn[h][:, t], qkT[h][:, t], start=t == 0, stop=True)
                        if t == TT - 1:
                            last.then_inc(o_done, 1)
                for h in range(HP):
                    sum_squares(ps[h][1], P1[h], o_sq, h, o_norm)
                pe.wait_ge(ada.ready, 2 * i + 2)
                pe.sem_inc(ada.asked, 1)
            pe.wait_ge(o_ready, 2 * TURNS + 2)
            for n in range(4):
                pe.wait_ge(w_in[n % 2], 32 * TURNS + 16 * (n // 2) + 16)
                for t in range(TT):
                    j = n * TT + t
                    if j >= 2:
                        pe.wait_ge(out_used, j - 1)
                    else:
                        pe.wait_ge(proj_free, 2 * KINDS * TURNS + 2)
                    for k in range(KT):
                        last = nc.tensor.matmul(pj[j % 2][:, 0:PF], oT[:, k, t * P:(t + 1) * P], w[:, n % 2, k],
                                                start=k == 0, stop=k == KT - 1)
                    last.then_inc(out_done, 1)
    st.close(gathers=True)


def build(nc, A, out):
    h_rows = nc.dram_tensor("h_rows", (SEQ, D), F32).ap()
    y_rows = nc.dram_tensor("y_rows", (SEQ * TOPK, D), F32).ap()
    ada_rows = nc.dram_tensor("ada_rows", (2 * DEPTH, 3 * D), F32).ap()
    with ExitStack() as ctx:
        c = alloc_core(nc, ctx)
        setup_stage(nc, c, A)
        norm_stage(nc, c, A, None, 0)
        attention_stage(nc, c, A, ada_rows)
        norm_stage(nc, c, A, 0, 1, ada_rows, h_rows=h_rows)
        moe_stage(nc, c, A, 0, h_rows, y_rows)
        norm_stage(nc, c, A, 1, 2, ada_rows)
        delta_stage(nc, c, A, ada_rows)
        norm_stage(nc, c, A, 2, 3, ada_rows, h_rows=h_rows)
        moe_stage(nc, c, A, 1, h_rows, y_rows)
        norm_stage(nc, c, A, 3, None, out=out)


_INS = ("x", "c", "positions", "ada_w", "ada_b", "ln_g", "ln_b", "attn_w_in", "attn_w_out", "gdn_w_in", "gdn_conv_w",
        "gdn_a_log", "gdn_dt_bias", "gdn_norm_w", "gdn_w_out", "router_w", "router_bias", "expert_w1", "expert_w3",
        "expert_w2", "shared_w1", "shared_w3", "shared_w2")


def kernel(**inputs):
    import concourse.bacc as _bacc
    from concourse.bass_utils import run_bass_kernel_spmd as _run

    nc = _bacc.Bacc("TRN2", target_bir_lowering=False, num_devices=1)
    arrays, A = {}, {}
    for name in _INS:
        a = np.ascontiguousarray(inputs[name])
        arrays[f"in_{name}_dram"] = a
        A[name] = nc.dram_tensor(f"in_{name}_dram", a.shape, mybir.dt.from_np(a.dtype), kind="ExternalInput").ap()
    out = nc.dram_tensor("out_dram", (1, SEQ, D), F32, kind="ExternalOutput").ap()
    build(nc, A, out)
    r = _run(nc, [arrays], core_ids=[0])
    return r.results[0]["out_dram"]
```

```python
from contextlib import ExitStack

import numpy as np
import concourse.bass as bass
from concourse import mybir

F32 = mybir.dt.float32
BF16 = mybir.dt.bfloat16
I32 = mybir.dt.int32
U32 = mybir.dt.uint32
ALU = mybir.AluOpType
ACT = mybir.ActivationFunctionType
AX = mybir.AxisListType

P = 128
SEQ, D = 512, 1024
TT = SEQ // P
KT = D // P
DEPTH = 2
ALPHA = (2 * DEPTH) ** 0.25
LN_EPS, RMS_EPS = 1e-5, 1e-6
NEG = -1e30

HEADS, HD = 16, 64
GROUPS = 3
WINDOW0 = 128
QUADS = HEADS // 4
QF = 4 * HD
RES = 4
ROPE_THETA = 10000.0

GH, GD = 8, 128
CONV = 4

NE, TOPK, NG, TOPG = 64, 8, 8, 4
ED = 256
CAP = P
OVB = SEQ * TOPK // (CAP + 1)
ROUTED_SCALE = 2.5


class Stage:

    def __init__(self, nc, tag):
        self.nc, self.tag, self.ctx, self.sems = nc, tag, ExitStack(), []

    def sb(self, name, shape, dt=F32):
        return self.ctx.enter_context(self.nc.sbuf_tensor(f"{self.tag}_{name}", shape, dt))

    def ps(self, name, shape, dt=F32):
        return self.ctx.enter_context(self.nc.psum_tensor(f"{self.tag}_{name}", shape, dt))

    def sem(self, name):
        s = self.ctx.enter_context(self.nc.semaphore(f"{self.tag}_{name}"))
        self.sems.append(s)
        return s

    def close(self, gathers=False, beside=None):
        if gathers:
            self.nc.gpsimd.dma_reset()
        if beside is not None:
            self.sems += beside.sems
        numbers = sorted(s.num for s in self.sems)
        first = 0
        for n in range(1, len(numbers) + 1):
            if n == len(numbers) or numbers[n] != numbers[n - 1] + 1:
                self.nc.gpsimd.sem_clear(range(numbers[first], numbers[n - 1] + 1))
                first = n
        self.nc.all_engine_barrier()
        self.ctx.close()
        if beside is not None:
            beside.ctx.close()


class Chain:

    def __init__(self, eng, sem, base=0):
        self.eng, self.sem, self.base, self.n = eng, sem, base, 0

    def do(self, ins):
        ins.then_inc(self.sem, 1)
        self.n += 1
        return ins

    def sync(self):
        self.eng.wait_ge(self.sem, self.base + self.n)


class Ring:

    def __init__(self, nc, tag, slots, shape, chunk):
        self.st = Stage(nc, tag)
        self.w = self.st.sb("w", [P, slots] + shape)
        self.w_in = [self.st.sem(f"w_in{n}") for n in range(slots)]
        self.slots, self.chunk = slots, chunk

    def load_early(self, sp):
        for n in range(self.slots):
            sp.dma_start(self.w[:, n], self.chunk(n)).then_inc(self.w_in[n], 16)


class Core:
    pass


def alloc_core(nc, ctx):
    c = Core()

    def sb(name, shape, dt=F32):
        return ctx.enter_context(nc.sbuf_tensor(f"core_{name}", shape, dt))

    c.x = sb("x", [P, TT, D])
    c.hT = sb("hT", [P, KT, SEQ])
    c.ada = sb("ada", [P, 3, D])
    c.c = sb("c", [P, KT])
    c.ident = sb("ident", [P, P])
    c.ones = sb("ones", [P, P])
    c.upper = sb("upper", [P, P])
    return c


def setup_stage(nc, c, A):
    st = Stage(nc, "setup")
    loaded, filled, selected = st.sem("loaded"), st.sem("filled"), st.sem("selected")
    with nc.Block() as block:
        @block.sync
        def _(sp):
            sp.dma_start(c.c[:], A["c"].rearrange("a (p k) -> p (a k)", k=KT)).then_inc(loaded, 16)

        @block.vector
        def _(dve):
            nc.vector.memset(c.ident[:], 0.0).then_inc(filled, 1)
            nc.vector.memset(c.upper[:], 1.0).then_inc(filled, 1)
            nc.vector.memset(c.ones[:], 1.0).then_inc(filled, 1)
            dve.wait_ge(loaded, 16)

        @block.gpsimd
        def _(pool):
            pool.wait_ge(filled, 3)
            pool.affine_select(out=c.ident[:], in_=c.ident[:], compare_op=ALU.not_equal, fill=1.0, base=0,
                               pattern=[[-1, P]], channel_multiplier=1).then_inc(selected, 1)
            pool.affine_select(out=c.upper[:], in_=c.upper[:], compare_op=ALU.is_ge, fill=0.0, base=0,
                               pattern=[[1, P]], channel_multiplier=-1).then_inc(selected, 1)
            pool.wait_ge(selected, 2)
    st.close()


class AdaRows:
    TURNS = 4
    QA = 3 * D // TURNS

    def __init__(self, nc, c, st, A, mods, rows, slots):
        self.nc, self.c, self.slots, self.n = nc, c, slots, len(mods)
        self.first, self.rows = mods[0], rows
        self.steps = self.n * KT
        self.w = st.sb("ada_w", [P, slots, self.QA])
        self.acc = st.sb("ada_acc", [P, self.n, self.QA])
        self.row = st.sb("ada_row", [1, self.n, self.QA])
        self.w_in = [st.sem(f"ada_w_in{s}") for s in range(slots)]
        (self.asked, self.used, self.summed, self.ready, self.bias_in, self.stored) = [
            st.sem("ada_" + x) for x in "asked used summed ready bias_in stored".split()]
        self.aw = [A["ada_w"][m // 2, m % 2].rearrange("(p k) n -> p k n", k=KT) for m in mods]
        self.bias = A["ada_b"].rearrange("l s n -> (l s) n")

    def load(self, pool, i, j):
        pool.wait_ge(self.used, self.steps * i + j + 1)
        pool.sem_inc(self.asked, 1)
        pool.dma_start(self.w[:, j % self.slots], self.aw[j // KT][:, j % KT, bass.ds(i * self.QA, self.QA)])\
            .then_inc(self.w_in[j % self.slots], 16)

    def credits(self, dve):
        dve.sem_inc(self.used, self.slots)
        dve.sem_inc(self.summed, self.n)

    def add(self, dve, i, j):
        m, k, s = j // KT, j % KT, j % self.slots
        dve.wait_ge(self.w_in[s], 16 * (self.steps // self.slots) * i + 16 * (j // self.slots + 1))
        if k == 0:
            dve.wait_ge(self.summed, self.n * i + m + 1)
            ins = self.nc.vector.tensor_scalar(self.acc[:, m], self.w[:, s], self.c.c[:, k:k + 1], None, ALU.mult)
        else:
            dve.wait_ge(self.used, self.steps * i + j + self.slots)
            ins = self.nc.vector.scalar_tensor_tensor(out=self.acc[:, m], in0=self.w[:, s], scalar=self.c.c[:, k:k + 1],
                                                      in1=self.acc[:, m], op0=ALU.mult, op1=ALU.add)
        ins.then_inc(self.used, 1)

    def total(self, pe, i, m, outs):
        half = self.QA // 2
        pe.wait_ge(self.used, self.steps * i + KT * (m + 1) + self.slots)
        for n, out in enumerate(outs):
            last = self.nc.tensor.matmul(out, self.c.ones[:], self.acc[:, m, n * half:(n + 1) * half], start=True, stop=True)
        last.then_inc(self.summed, 1)

    def finish(self, dve, i, m, outs):
        half = self.QA // 2
        dve.wait_ge(self.bias_in, 16 * i + 16)
        dve.wait_ge(self.summed, self.n * i + m + 1 + self.n)
        for n, out in enumerate(outs):
            r = self.row[:, m, n * half:(n + 1) * half]
            self.nc.vector.tensor_tensor(r, out[0:1], r, ALU.add).then_inc(self.ready, 1)

    def cols(self, t, i):
        return t[self.first:self.first + self.n, bass.ds(i * self.QA, self.QA)].rearrange("(a m) n -> a m n", a=1)

    def load_bias(self, sp, i):
        sp.wait_ge(self.stored, 16 * i + 16)
        sp.sem_inc(self.asked, 1)
        sp.dma_start(self.row[:], self.cols(self.bias, i)).then_inc(self.bias_in, 16)

    def store(self, sp, i):
        sp.wait_ge(self.ready, 2 * self.n * i + 2 * self.n)
        sp.sem_inc(self.asked, 1)
        sp.dma_start(self.cols(self.rows, i), self.row[:]).then_inc(self.stored, 16)


def norm_stage(nc, c, A, norm, mod, ada_rows=None, h_rows=None, out=None, weights=None, ring=None):
    direct = mod is not None and ada_rows is None
    st = Stage(nc, f"norm{norm}")
    SLOTS = 2
    sem = st.sem
    rows_in, x_out = sem("rows_in"), sem("x_out")
    bias_in = sem("bias_in")
    w_in = [sem(f"w_in{i}") for i in range(SLOTS)]
    spread, x_in = sem("spread"), sem("x_in")
    w_used, ada_sum, ada_ready = sem("w_used"), sem("ada_sum"), sem("ada_ready")
    dve_step, var_ready, std_ready = sem("dve_step"), sem("var_ready"), sem("std_ready")
    h_ready, turned, laid = sem("h_ready"), sem("turned"), sem("laid")
    less_ready, xn_ready, pool_step = sem("less_ready"), sem("xn_ready"), sem("pool_step")
    x_ready = [sem(f"x_ready{t}") for t in range(TT)]
    if norm is not None:
        g = st.sb("g", [P, D])
        b = st.sb("b", [P, D])
        gh = st.sb("gh", [P, D])
        bh = st.sb("bh", [P, D])
        stats = st.sb("stats", [P, TT, 2, 6])
        mv = st.sb("mv", [P, TT, 2])
        std = st.sb("std", [P, TT])
        less = st.sb("less", [P, TT])
        eps = st.sb("eps", [P, 1])
        xn = st.sb("xn", [P, TT, D])
        on_pool = (0, 1) if mod is not None else (1,)
    if direct:
        w = st.sb("w", [P, SLOTS, 3 * D])
        bias = st.sb("bias", [P, 3 * D])
        cb = st.sb("cb", [P, KT, P])
        ada_ps = [st.ps(f"ada{n}", [P, 512]) for n in range(6)]
    if mod is not None:
        h = st.sb("h", [P, TT, D]) if weights is None else weights.h
        tp = [st.ps(f"tp{n}", [P, 4, P]) for n in range(2)]
        aw = A["ada_w"][mod // 2, mod % 2].rearrange("(p k) n -> p k n", k=KT)

    def row(t, i):
        return t[i // 2, i % 2].rearrange("(a n) -> a n", a=1).partition_broadcast(P)

    with nc.Block() as block:
        @block.sync
        def _(sp):
            if weights is not None:
                if norm is not None:
                    sp.wait_ge(rows_in, 32)
                sp.wait_ge(bias_in, 16)
                weights.load_early(sp)
            if direct:
                for k in range(KT):
                    if k >= SLOTS:
                        sp.wait_ge(w_used, k - SLOTS + 1)
                    sp.dma_start(w[:, k % SLOTS], aw[:, k]).then_inc(w_in[k % SLOTS], 16)
            if ring is not None:
                if norm is not None:
                    sp.wait_ge(rows_in, 32)
                    sp.wait_ge(bias_in, 16)
                ring.load_early(sp)
            for t in range(TT):
                if h_rows is not None:
                    sp.wait_ge(h_ready, t + 1)
                    sp.dma_start(h_rows[t * P:(t + 1) * P, :], h[:, t]).then_inc(weights.h_out, 16)
                if out is not None:
                    sp.wait_ge(x_ready[t], 1)
                    sp.dma_start(out[0, t * P:(t + 1) * P, :], c.x[:, t]).then_inc(x_out, 16)
            if out is not None:
                sp.wait_ge(x_out, 16 * TT)

        @block.scalar
        def _(act):
            if norm is not None:
                act.dma_start(g[:], row(A["ln_g"], norm)).then_inc(rows_in, 16)
                act.dma_start(b[:], row(A["ln_b"], norm)).then_inc(rows_in, 16)
            if norm is None:
                act.dma_start(c.x[:], A["x"][0].rearrange("(t p) d -> p t d", p=P)).then_inc(x_in, 16)
            if direct:
                act.dma_start(bias[:], row(A["ada_b"], mod)).then_inc(bias_in, 16)
            elif mod is not None:
                act.dma_start(c.ada[:].rearrange("p a n -> p (a n)"),
                              ada_rows[mod].rearrange("(a n) -> a n", a=1).partition_broadcast(P)).then_inc(bias_in, 16)
            if norm is not None:
                act.wait_ge(var_ready, TT)
                nc.scalar.activation(std[:], mv[:, :, 1], ACT.Sqrt, bias=eps[:]).then_inc(std_ready, 1)
                act.wait_ge(less_ready, 1)
                for t in range(TT):
                    nc.scalar.activation(xn[:, t], c.x[:, t], ACT.Identity, scale=std[:, t:t + 1], bias=less[:, t:t + 1])\
                        .then_inc(xn_ready, 1)
            if mod is not None:
                for t in range(TT):
                    for q in range(2):
                        act.wait_ge(turned, 2 * t + q + 1)
                        nc.scalar.copy(c.hT[:, 4 * q:4 * q + 4, t * P:(t + 1) * P], tp[q][:]).then_inc(laid, 1)
                act.wait_ge(laid, 2 * TT)

        @block.vector
        def _(dve):
            ch = Chain(dve, dve_step)
            if direct:
                nc.vector.tensor_copy(cb[:], c.c[:].rearrange("p (k o) -> p k o", o=1).broadcast_to([P, KT, P])).then_inc(spread, 1)
            if norm is not None:
                ch.do(nc.vector.memset(eps[:], LN_EPS))
                for t in range(TT):
                    for q in range(2):
                        ch.do(nc.vector.bn_stats(stats[:, t, q], c.x[:, t, q * 512:(q + 1) * 512]))
                ch.sync()
                for t in range(TT):
                    nc.vector.bn_aggr(mv[:, t], stats[:, t]).then_inc(var_ready, 1)
                dve.wait_ge(std_ready, 1)
                ch.do(nc.vector.reciprocal(std[:], std[:]))
                ch.sync()
                nc.vector.scalar_tensor_tensor(out=less[:], in0=mv[:, :, 0], scalar=-1.0, in1=std[:], op0=ALU.mult,
                                               op1=ALU.mult).then_inc(less_ready, 1)
                dve.wait_ge(rows_in, 32)
            if mod is not None:
                dve.wait_ge(bias_in, 16)
            if norm is not None and mod is not None:
                ch.do(nc.vector.scalar_tensor_tensor(out=gh[:], in0=c.ada[:, 1], scalar=1.0, in1=g[:], op0=ALU.add, op1=ALU.mult))
                ch.do(nc.vector.scalar_tensor_tensor(out=bh[:], in0=c.ada[:, 1], scalar=1.0, in1=b[:], op0=ALU.add, op1=ALU.mult))
                ch.sync()
                ch.do(nc.vector.tensor_tensor(bh[:], bh[:], c.ada[:, 0], ALU.add))
                ch.sync()
                for t in range(TT):
                    dve.wait_ge(xn_ready, t + 1)
                    ch.do(nc.vector.tensor_tensor(h[:, t], xn[:, t], gh[:], ALU.mult))
                    ch.sync()
                    nc.vector.tensor_tensor(h[:, t], h[:, t], bh[:], ALU.add).then_inc(h_ready, 1)
            elif mod is not None:
                dve.wait_ge(x_in, 16)
                dve.wait_ge(ada_sum, 1)
                for n in range(6):
                    nc.vector.tensor_tensor(c.ada[:, n // 2, n % 2 * 512:(n % 2 + 1) * 512], ada_ps[n][:],
                                            bias[:, n * 512:(n + 1) * 512], ALU.add).then_inc(ada_ready, 1)
                dve.wait_ge(ada_ready, 6)
                for t in range(TT):
                    ch.do(nc.vector.scalar_tensor_tensor(out=h[:, t], in0=c.ada[:, 1], scalar=1.0, in1=c.x[:, t],
                                                         op0=ALU.add, op1=ALU.mult))
                    ch.sync()
                    nc.vector.tensor_tensor(h[:, t], h[:, t], c.ada[:, 0], ALU.add).then_inc(h_ready, 1)
            if norm is not None:
                for t in range(TT):
                    if t not in on_pool:
                        dve.wait_ge(xn_ready, t + 1)
                        ch.do(nc.vector.tensor_tensor(xn[:, t], xn[:, t], g[:], ALU.mult))
                        ch.sync()
                        nc.vector.tensor_tensor(c.x[:, t], xn[:, t], b[:], ALU.add).then_inc(x_ready[t], 1)
                        dve.wait_ge(x_ready[t], 1)
            if mod is not None:
                dve.wait_ge(h_ready, TT)

        if norm is not None:
            @block.gpsimd
            def _(pool):
                pool.wait_ge(rows_in, 32)
                for n, t in enumerate(on_pool):
                    pool.wait_ge(xn_ready, t + 1)
                    if mod is not None:
                        pool.wait_ge(h_ready, t + 1)
                    pool.tensor_tensor(xn[:, t], xn[:, t], g[:], ALU.mult).then_inc(pool_step, 1)
                    pool.wait_ge(pool_step, n + 1)
                    pool.tensor_tensor(c.x[:, t], xn[:, t], b[:], ALU.add).then_inc(x_ready[t], 1)
                for t in on_pool:
                    pool.wait_ge(x_ready[t], 1)

        @block.tensor
        def _(pe):
            if direct:
                pe.wait_ge(spread, 1)
                for k in range(KT):
                    pe.wait_ge(w_in[k % SLOTS], 16 * (k // SLOTS + 1))
                    for n in range(6):
                        last = nc.tensor.matmul(ada_ps[n][:], cb[:, k], w[:, k % SLOTS, n * 512:(n + 1) * 512],
                                                start=k == 0, stop=k == KT - 1)
                    last.then_inc(w_used if k < KT - 1 else ada_sum, 1)
            if mod is not None:
                for t in range(TT):
                    pe.wait_ge(h_ready, t + 1)
                    for q in range(2):
                        if t:
                            pe.wait_ge(laid, 2 * t - 1 + q)
                        for k in range(4):
                            last = nc.tensor.transpose(tp[q][:, k], h[:, t, 4 * q + k::KT], c.ident[:])
                        last.then_inc(turned, 1)
    st.close()


def attention_weights(A):
    return A["attn_w_in"][0].rearrange("(p k) (g s n) -> p k g s n", k=KT, g=GROUPS, s=3)


def attention_ring(nc, A):
    return Ring(nc, "attn_w", 3, [KT, QF], lambda n: attention_weights(A)[:, :, n // 3, n % 3, 0:QF])


def attention_stage(nc, c, A, ada_rows, ring):
    st = Stage(nc, "attn")
    SLOTS = ring.slots
    CH = 3 * GROUPS
    NPROJ = 2 * CH
    PC = 2 * SLOTS
    NROT = 4 * GROUPS
    UNITS = 4 * RES
    KEYS = SEQ + 2 * P
    C1, C2 = 6.28125, float(np.float32(0.0019350051879882812))
    C3 = float(2 * np.pi - C1 - C2)
    ROUND = 12582912.0

    w, w_in = ring.w, ring.w_in
    v = st.sb("v", [P, GROUPS, TT, QF])
    q = st.sb("q", [P, GROUPS, 2, 2, SEQ])
    k = st.sb("k", [P, GROUPS, 2, SEQ])
    raw = st.sb("raw", [P, 2, SEQ])
    swp = st.sb("swp", [P, 2, SEQ])
    rot = st.sb("rot", [P, 2, SEQ])
    cos = st.sb("cos", [P, SEQ])
    sin = st.sb("sin", [P, SEQ])
    mask = st.sb("mask", [P, RES, KEYS])
    sm = st.sb("sm", [P, 2, KEYS])
    prob = st.sb("prob", [P, 2, KEYS])
    probT = st.sb("probT", [P, 2, KEYS])
    o = st.sb("o", [P, 2, P])
    oT = st.sb("oT", [P, KT, SEQ])
    small = st.sb("small", [P, 12])
    top = small[:, 0:2]
    bias = small[:, 2:4]
    den = small[:, 4:8]
    rden = small[:, 8:12]
    freq = st.sb("freq", [P, 2])
    halfpi = st.sb("halfpi", [P, 1])
    pos = st.sb("pos", [P, SEQ], I32)
    diff = st.sb("diff", [P, P], I32)
    ada = AdaRows(nc, c, st, A, (1, 2), ada_rows, 2)

    proj = [st.ps(f"proj{n}", [P, 512]) for n in range(2)]
    sc = st.ps("sc", [P, 1024])
    tp = st.ps("tp", [P, 8, P])
    pv = st.ps("pv", [P, 512])
    po = st.ps("po", [P, 512])

    sem = st.sem
    proj_done, proj_free = sem("proj_done"), sem("proj_free")
    raw_ready, rot_done = sem("raw_ready"), sem("rot_done")
    swp_in = [sem(f"swp_in{n}") for n in range(2)]
    sc_done, sm_ready, bias_ready, p_ready = sem("sc_done"), sem("sm_ready"), sem("bias_ready"), sem("p_ready")
    tp_done, pT_ready, pv_done, o_ready = sem("tp_done"), sem("pT_ready"), sem("pv_done"), sem("o_ready")
    oT_done, oT_ready = sem("oT_done"), sem("oT_ready")
    dve_step, pool_step, tables_in, angle_ready = sem("dve_step"), sem("pool_step"), sem("tables_in"), sem("angle_ready")
    sin_ready, diff_ready, parity_ready, mask_ready = sem("sin_ready"), sem("diff_ready"), sem("parity_ready"), sem("mask_ready")
    turn_seen = sem("turn_seen")
    y_done, y_used = sem("y_done"), sem("y_used")
    DVE_T = NROT // 2 + 2 * NROT + UNITS

    half = HD // 2
    f = np.arange(P)
    table = np.stack([ROPE_THETA ** (-(f % half).astype(np.float32) / np.float32(half)),
                      np.where(f % HD < half, -1.0, 1.0)], 1).astype(np.float32)
    table_dram = nc.inline_tensor(table, "rope_table")
    w_dram = attention_weights(A)
    wo_dram = A["attn_w_out"][0].rearrange("(k p) n -> p k n", p=P)
    side = [pv[:, P:P + ada.QA // 2], po[:, P:P + ada.QA // 2]]
    chunks = [(g, s) for g in range(GROUPS) for s in range(3)]

    with nc.Block() as block:
        @block.sync
        def _(sp):
            sp.sem_inc(ada.stored, 16)
            def turn(i, first):
                ada.load_bias(sp, i)
                for n, (g, s) in enumerate(chunks):
                    if first and n < SLOTS:
                        continue
                    sp.wait_ge(proj_done, NPROJ * i + 2 * n + 2)
                    sp.sem_inc(turn_seen, 1)
                    sp.dma_start(w[:, n % SLOTS], w_dram[:, :, g, s, bass.ds(i * QF, QF)]).then_inc(w_in[n % SLOTS], 16)
                ada.store(sp, i)

            turn(0, True)
            with sp.Fori(1, QUADS) as i:
                turn(i, False)
            for n in range(4):
                if n < SLOTS:
                    sp.wait_ge(proj_done, NPROJ * QUADS + 2 * n + 2)
                else:
                    sp.wait_ge(y_done, TT * (n - SLOTS + 1))
                sp.dma_start(w[:, n % SLOTS], wo_dram[:, :, n * QF:(n + 1) * QF]).then_inc(w_in[n % SLOTS], 16)
            sp.wait_ge(ada.stored, 16 * QUADS + 16)

        @block.scalar
        def _(act):
            act.sem_inc(proj_free, 2)
            act.sem_inc(pT_ready, 1)
            act.dma_start(pos[:], A["positions"][0].rearrange("(a n) -> a n", a=1).partition_broadcast(P)).then_inc(tables_in, 16)
            act.dma_start(freq[:], table_dram.ap()).then_inc(tables_in, 16)
            act.wait_ge(angle_ready, 2)
            nc.scalar.activation(sin[:], raw[:, 0], ACT.Sin).then_inc(sin_ready, 1)
            nc.scalar.activation(cos[:], raw[:, 1], ACT.Sin, scale=-1.0, bias=halfpi[:]).then_inc(sin_ready, 1)
            act.wait_ge(sin_ready, 2)
            with act.Fori(0, QUADS) as i:
                n = m = 0
                for g, s in chunks:
                    for half_ in range(2):
                        act.wait_ge(proj_done, NPROJ * i + n + 1 + PC)
                        if s == 2:
                            nc.scalar.copy(v[:, g, 2 * half_:2 * half_ + 2, :],
                                           proj[n % 2][:].rearrange("p (t f) -> p t f", f=QF)).then_inc(proj_free, 1)
                        else:
                            act.wait_ge(rot_done, NROT * i + m + 1)
                            nc.scalar.copy(raw[:, m % 2], proj[n % 2][:]).then_inc(proj_free, 1)
                            act.wait_ge(proj_free, NPROJ * i + n + 3)
                            for d in range(4):
                                e = d ^ 1
                                act.dma_start(swp[32 * d:32 * d + 32, m % 2], raw[32 * e:32 * e + 32, m % 2])\
                                   .then_inc(swp_in[m % 2], 16)
                            m += 1
                        n += 1
                for step in range(UNITS + 1):
                    u = step - 1
                    if u >= 0:
                        act.wait_ge(tp_done, UNITS * i + u + 3)
                        act.wait_ge(pv_done, UNITS * i + u + 1)
                        nc.scalar.copy(probT[:, u % 2], tp[:, 0:6].rearrange("p b q -> p (b q)")).then_inc(pT_ready, 1)
                    u = step
                    if u < UNITS:
                        act.wait_ge(bias_ready, UNITS * i + u + 1)
                        act.wait_ge(tp_done, UNITS * i + u + 1)
                        nc.scalar.activation(prob[:, u % 2], sm[:, u % 2], ACT.Exp, bias=bias[:, u % 2:u % 2 + 1],
                                             scale=HD ** -0.5, accum_out=den[:, u % 4:u % 4 + 1]).then_inc(p_ready, 1)

        @block.gpsimd
        def _(pool):
            ch = Chain(pool, pool_step)
            ch.do(pool.iota(diff[:], pattern=[[-1, P]], base=P, channel_multiplier=1))
            ch.do(pool.memset(mask[:, :, 0:SEQ + P], 0.0))
            ch.sync()
            pool.sem_inc(diff_ready, 1)
            pool.wait_ge(parity_ready, 1)
            for t in range(2):
                m = mask[:, 0, SEQ + t * P:SEQ + (t + 1) * P]
                ch.do(pool.affine_select(out=m, in_=m, compare_op=ALU.is_ge, fill=NEG, base=0,
                                         pattern=[[-1, P]], channel_multiplier=1))
            ch.sync()
            for r in range(RES):
                m = mask[:, r, 0:SEQ]
                if r:
                    ch.do(pool.tensor_copy(mask[:, r, SEQ:KEYS], mask[:, 0, SEQ:KEYS]))
                ch.do(pool.affine_select(out=m, in_=m, compare_op=ALU.is_ge, fill=NEG, base=r,
                                         pattern=[[-1, SEQ]], channel_multiplier=RES))
                ch.sync()
                pool.affine_select(out=m, in_=m, compare_op=ALU.is_ge, fill=NEG, base=WINDOW0 - r,
                                   pattern=[[1, SEQ]], channel_multiplier=-RES).then_inc(mask_ready, 1)
            pool.wait_ge(mask_ready, RES)
            with pool.Fori(0, QUADS) as i:
                for j in range(ada.steps):
                    ada.load(pool, i, j)

        @block.vector
        def _(dve):
            dve.sem_inc(rot_done, 2)
            dve.sem_inc(sm_ready, 1)
            dve.sem_inc(o_ready, 1)
            ada.credits(dve)
            ch = Chain(dve, dve_step)
            ch.do(nc.vector.memset(q[:], 0.0))
            ch.do(nc.vector.memset(halfpi[:], float(np.pi / 2)))
            dve.wait_ge(pool_step, 2)
            ch.do(nc.vector.tensor_single_scalar(diff[:], diff[:], 3, ALU.bitwise_and))
            ch.sync()
            nc.vector.tensor_scalar(mask[:, 0, SEQ + P:KEYS], diff[:], 0.0, NEG, ALU.not_equal, ALU.mult).then_inc(parity_ready, 1)
            dve.wait_ge(tables_in, 32)
            ang, turns, rest = raw[:, 1], swp[:, 0], raw[:, 0]
            ch.do(nc.vector.tensor_scalar(ang, pos[:], freq[:, 0:1], None, ALU.mult))
            ch.sync()
            ch.do(nc.vector.tensor_scalar(turns, ang, float(1 / (2 * np.pi)), ROUND, ALU.mult, ALU.add))
            ch.sync()
            ch.do(nc.vector.tensor_scalar(turns, turns, ROUND, None, ALU.subtract))
            ch.sync()
            for part, src in ((C1, ang), (C2, rest), (C3, rest)):
                ch.do(nc.vector.scalar_tensor_tensor(out=rest, in0=turns, scalar=-part, in1=src, op0=ALU.mult, op1=ALU.add))
                ch.sync()
            lim = 3.1415925
            nc.vector.tensor_scalar(rest, rest, lim, -lim, ALU.min, ALU.max).then_inc(angle_ready, 1)
            dve.wait_ge(angle_ready, 1)
            nc.vector.scalar_tensor_tensor(out=ang, in0=rest, scalar=-1.0, in1=rest, op0=ALU.mult, op1=ALU.max).then_inc(angle_ready, 1)
            dve.wait_ge(sin_ready, 2)
            ch.do(nc.vector.tensor_scalar(sin[:], sin[:], freq[:, 1:2], None, ALU.mult))
            dve.wait_ge(mask_ready, RES)
            ch.sync()
            first = ch.n

            with dve.Fori(0, QUADS) as i:
                ch = Chain(dve, dve_step, DVE_T * i + first)
                m = 0
                for g in range(GROUPS):
                    for s in range(2):
                        for pair in range(2):
                            dve.wait_ge(proj_free, NPROJ * i + 2 * (3 * g + s) + pair + 3)
                            ch.do(nc.vector.tensor_tensor(rot[:, 0], raw[:, m % 2], cos[:], ALU.mult))
                            dve.wait_ge(swp_in[m % 2], 64 * (NROT // 2) * i + 64 * (m // 2 + 1))
                            ch.do(nc.vector.tensor_tensor(rot[:, 1], swp[:, m % 2], sin[:], ALU.mult))
                            ch.sync()
                            a = rot[:, 0].rearrange("p (j r) -> p j r", r=RES)
                            b = rot[:, 1].rearrange("p (j r) -> p j r", r=RES)
                            if s == 0:
                                for hh in range(2):
                                    rows = slice(HD * hh, HD * hh + HD)
                                    to = q[rows, g, pair, hh].rearrange("p (r j) -> p j r", r=RES)
                                    ins = nc.vector.tensor_tensor(to, a[rows], b[rows], ALU.add)
                                    if hh == 0:
                                        ch.do(ins)
                            else:
                                to = k[:, g, pair]
                                if g == 0:
                                    ins = nc.vector.tensor_tensor(to, rot[:, 0], rot[:, 1], ALU.add)
                                else:
                                    ins = nc.vector.tensor_tensor(to.rearrange("p (r j) -> p j r", r=RES), a, b, ALU.add)
                            ins.then_inc(rot_done, 1)
                            dve.wait_ge(rot_done, NROT * i + m + 3)
                            m += 1
                            if m <= 8:
                                ada.add(dve, i, 2 * m - 2)
                                ada.add(dve, i, 2 * m - 1)
                            if m in (8, 12):
                                ada.finish(dve, i, m // 4 - 2, side)
                for step in range(UNITS + 4):
                    u = step
                    if u < UNITS:
                        r = u // 2 % RES
                        if u:
                            dve.wait_ge(mask_ready, RES)
                        dve.wait_ge(sc_done, UNITS * i + u + 1)
                        dve.wait_ge(p_ready, UNITS * i + u + 1)
                        if u == 0:
                            dve.sem_inc(turn_seen, 1)
                        nc.vector.tensor_tensor_reduce(sm[:, u % 2], sc[:, 0:KEYS], mask[:, r], 1.0, -3e38,
                                                       ALU.add, ALU.max, top[:, u % 2:u % 2 + 1]).then_inc(sm_ready, 1)
                        dve.wait_ge(sm_ready, UNITS * i + u + 2)
                        nc.vector.tensor_scalar(bias[:, u % 2:u % 2 + 1], top[:, u % 2:u % 2 + 1], -HD ** -0.5, None,
                                                ALU.mult).then_inc(bias_ready, 1)
                    u = step - 2
                    if 0 <= u < UNITS:
                        hh, slot = u % 2, u // 2 % 2
                        dve.wait_ge(p_ready, UNITS * i + u + 3)
                        ch.do(nc.vector.reciprocal(rden[:, u % 4:u % 4 + 1], den[:, u % 4:u % 4 + 1]))
                        dve.wait_ge(pv_done, UNITS * i + u + 3)
                        ch.sync()
                        nc.vector.tensor_scalar(o[:, slot, HD * hh:HD * hh + HD], pv[:, HD * hh:HD * hh + HD],
                                                rden[:, u % 4:u % 4 + 1], None, ALU.mult).then_inc(o_ready, 1)
                    u = step - 3
                    if u >= 0 and u % 2:
                        pair, r = u // 8, u // 2 % RES
                        dve.wait_ge(oT_done, UNITS // 2 * i + u // 2 + 1)
                        nc.vector.tensor_scalar(oT[:, bass.ds(2 * i + pair, 1), r::RES].rearrange("p a q -> p (a q)"),
                                                po[:, 0:P], 1.0, None, ALU.mult).then_inc(oT_ready, 1)
                assert DVE_T == ch.n, ch.n
            out = Chain(dve, dve_step, DVE_T * QUADS + first)
            for n in range(4):
                for t in range(TT):
                    j = n * TT + t
                    cols = slice(n * QF, (n + 1) * QF)
                    dve.wait_ge(y_done, j + 1)
                    nc.vector.scalar_tensor_tensor(out=rot[:, j % 2, 0:QF], in0=c.ada[:, 2, cols], scalar=1.0,
                                                   in1=proj[j % 2][:, 0:QF], op0=ALU.add, op1=ALU.mult).then_inc(y_used, 1)
                    dve.wait_ge(y_used, j + 1)
                    out.do(nc.vector.scalar_tensor_tensor(out=c.x[:, t, cols], in0=c.x[:, t, cols], scalar=ALPHA,
                                                          in1=rot[:, j % 2, 0:QF], op0=ALU.mult, op1=ALU.add))
                    out.sync()

        @block.tensor
        def _(pe):
            pe.sem_inc(proj_done, PC)
            pe.sem_inc(tp_done, 2)
            pe.sem_inc(pv_done, 2)
            pe.sem_inc(p_ready, 2)
            with pe.Fori(0, QUADS) as i:
                n = 0
                for j, (g, s) in enumerate(chunks):
                    pe.wait_ge(w_in[j % SLOTS], 16 * (CH // SLOTS) * i + 16 * (j // SLOTS + 1))
                    for half_ in range(2):
                        pe.wait_ge(proj_free, NPROJ * i + n + 1)
                        if s == 2:
                            for t in range(2 * half_, 2 * half_ + 2):
                                toks = slice(t * P, (t + 1) * P) if g == 0 else slice(t, SEQ, RES)
                                for kk in range(KT):
                                    last = nc.tensor.matmul(proj[n % 2][:, t % 2 * QF:(t % 2 + 1) * QF],
                                                            c.hT[:, kk, toks], w[:, j % SLOTS, kk], start=kk == 0, stop=kk == KT - 1)
                        else:
                            for kk in range(KT):
                                last = nc.tensor.matmul(proj[n % 2][:], w[:, j % SLOTS, kk, half_ * P:(half_ + 1) * P],
                                                        c.hT[:, kk, :], start=kk == 0, stop=kk == KT - 1)
                        last.then_inc(proj_done, 1)
                        n += 1
                        if n == 2 * 6:
                            ada.total(pe, i, 0, side)
                pe.wait_ge(ada.ready, 4 * i + 2)
                ada.total(pe, i, 1, side)
                for step in range(UNITS + 4):
                    u = step
                    if u < UNITS:
                        pair, r, hh = u // 8, u // 2 % RES, u % 2
                        if u == 0:
                            pe.wait_ge(rot_done, NROT * (i + 1) + 2)
                        pe.wait_ge(sm_ready, UNITS * i + u + 1)
                        qs = [q[:, g, pair, hh, r * P:(r + 1) * P] for g in range(GROUPS)]
                        nc.tensor.matmul(sc[:, 0:SEQ], qs[0], k[:, 0, pair], start=True, stop=True)
                        for g in (1, 2):
                            last = nc.tensor.matmul(sc[:, SEQ + (g - 1) * P:SEQ + g * P], qs[g],
                                                    k[:, g, pair, r * P:(r + 1) * P], start=True, stop=True)
                        last.then_inc(sc_done, 1)
                    u = step - 1
                    if 0 <= u < UNITS:
                        pe.wait_ge(p_ready, UNITS * i + u + 3)
                        pe.wait_ge(pT_ready, UNITS * i + u + 1)
                        for b in range(6):
                            last = nc.tensor.transpose(tp[:, b], prob[:, u % 2, b * P:(b + 1) * P], c.ident[:])
                        last.then_inc(tp_done, 1)
                    u = step - 2
                    if 0 <= u < UNITS:
                        pair, r = u // 8, u // 2 % RES
                        pe.wait_ge(pT_ready, UNITS * i + u + 2)
                        pe.wait_ge(o_ready, UNITS * i + u + 1)
                        if u == 0:
                            pe.wait_ge(proj_free, NPROJ * (i + 1) + 2)
                            pe.wait_ge(ada.ready, 4 * i + 4)
                        for b in range(6):
                            g, t = (0, b) if b < 4 else (b - 3, r)
                            last = nc.tensor.matmul(pv[:, 0:P], probT[:, u % 2, b * P:(b + 1) * P],
                                                    v[:, g, t, pair * P:(pair + 1) * P], start=b == 0, stop=b == 5)
                        last.then_inc(pv_done, 1)
                    u = step - 3
                    if u >= 0 and u % 2:
                        pe.wait_ge(o_ready, UNITS * i + u + 2)
                        if u > 1:
                            pe.wait_ge(oT_ready, UNITS // 2 * i + u // 2)
                        nc.tensor.transpose(po[:, 0:P], o[:, u // 2 % 2], c.ident[:]).then_inc(oT_done, 1)
                pe.wait_ge(oT_ready, UNITS // 2 * (i + 1))
            for n in range(4):
                pe.wait_ge(w_in[n % SLOTS], 16 * (CH // SLOTS) * QUADS + 16 * (n // SLOTS + 1))
                for t in range(TT):
                    j = n * TT + t
                    if j >= 2:
                        pe.wait_ge(y_used, j - 1)
                    for kk in range(KT):
                        last = nc.tensor.matmul(proj[j % 2][:, 0:QF], oT[:, kk, t * P:(t + 1) * P], w[:, n % SLOTS, kk],
                                                start=kk == 0, stop=kk == KT - 1)
                    last.then_inc(y_done, 1)
    st.close(gathers=True, beside=ring.st)


class ExpertWeights:
    EARLY = 3

    def __init__(self, nc, A, l):
        self.nc, self.A, self.l = nc, A, l
        self.st = st = Stage(nc, f"weights{l}")
        self.w13 = st.sb("w13", [P, 4, 2, KT, ED])
        self.w2 = st.sb("w2", [P, 2, 2, D])
        self.rw = st.sb("rw", [P, KT, NE])
        self.rb = st.sb("rb", [P, NE])
        self.w13_in = [st.sem(f"w13_in{n}") for n in range(4)]
        self.w2_in = [st.sem(f"w2_in{n}") for n in range(2)]
        self.router_in = st.sem("router_in")
        self.h_out = st.sem("h_out")
        self.h = self.w13[:, 3].rearrange("p a k n -> p (a k n)").rearrange("p (t d) -> p t d", d=D)
        self.up_dram = [A[n][l].rearrange("e (p k) n -> p e (k n)", k=KT) for n in ("expert_w1", "expert_w3")]
        self.down_dram = A["expert_w2"][l].rearrange("e (p k) n -> p e (k n)", k=2)

    def up_slot(self, slot, a):
        return self.w13[:, slot, a].rearrange("p k n -> p (k n)")

    def down_slot(self, slot):
        return self.w2[:, slot].rearrange("p k n -> p (k n)")

    def load_up(self, sp, e, slot, done):
        for a, src in enumerate(self.up_dram):
            sp.dma_start(self.up_slot(slot, a), src[:, bass.ds(e, 1)].rearrange("p a n -> p (a n)")).then_inc(done, 16)

    def load_down(self, sp, e, slot, done):
        sp.dma_start(self.down_slot(slot), self.down_dram[:, bass.ds(e, 1)].rearrange("p a n -> p (a n)")).then_inc(done, 16)

    def load_early(self, sp):
        sp.dma_start(self.rw[:], self.A["router_w"][self.l].rearrange("(p k) n -> p k n", k=KT)).then_inc(self.router_in, 16)
        sp.dma_start(self.rb[:], self.A["router_bias"][self.l].rearrange("(a n) -> a n", a=1).partition_broadcast(P))\
            .then_inc(self.router_in, 16)
        for e in range(self.EARLY):
            self.load_up(sp, e, e, self.w13_in[e])
            if e < 2:
                self.load_down(sp, e, e, self.w2_in[e])


def moe_stage(nc, c, A, l, h_rows, y_rows, ew):
    st = Stage(nc, f"moe{l}")
    BIG = 1e5
    PICKED = 1e30
    F2 = 2 * ED

    w13, w2, rw, rb, w13_in, w2_in, router_in = ew.w13, ew.w2, ew.rw, ew.rb, ew.w13_in, ew.w2_in, ew.router_in
    xg = st.sb("xg", [P, 2, D])
    xT = st.sb("xT", [P, 2, KT, P])
    act_s = st.sb("act_s", [P, 2, F2])
    hh = st.sb("hh", [P, 2, ED])
    hT2 = st.sb("hT2", [P, 2, 2, P])
    ysb = st.sb("ysb", [P, 2, D])
    acc = st.sb("acc", [P, 2, D])
    lgT = st.sb("lgT", [NE, SEQ])
    sg = st.sb("sg", [P, TT, NE])
    biased = st.sb("biased", [P, TT, NE])
    g8 = st.sb("g8", [P, TT, NG, 8])
    gpad = st.sb("gpad", [P, TT, 16])
    grep = st.sb("grep", [P, TT, 8])
    gm = st.sb("gm", [P, TT, 16])
    v8 = st.sb("v8", [P, TT, 8])
    left = st.sb("left", [P, TT, NE])
    sel = st.sb("sel", [P, TT, NE], BF16)
    self32 = st.sb("self32", [P, TT, NE])
    kth = st.sb("kth", [P, TT, NE])
    hot = st.sb("hot", [P, TOPK, NE])
    gate = st.sb("gate", [P, TT, TOPK])
    gsum = st.sb("gsum", [P, TT])
    pos = st.sb("pos", [P, TT, NE])
    cnt = st.sb("cnt", [P, NE])
    nov = st.sb("nov", [P, NE])
    incl = st.sb("incl", [P, NE])
    ind = st.sb("ind", [P, OVB, NE])
    ovf = st.sb("ovf", [P, 2, OVB])
    ovi = st.sb("ovi", [1, OVB + 1], I32)
    ii = st.sb("ii", [P, P], I32)
    iota = st.sb("iota", [P, P])
    pidx = st.sb("pidx", [P, TT, 2], I32)
    tokf = st.sb("tokf", [P, TT, 2])
    num = st.sb("num", [P, TT, NE, 5], BF16)
    offs = st.sb("offs", [P, 5], BF16)
    onesb = st.sb("onesb", [P, P], BF16)
    before = st.sb("before", [P, P], BF16)
    onehot = st.sb("onehot", [P, 2, TT, P], BF16)
    pcol = st.sb("pcol", [P, TT])
    idx = st.sb("idx", [P, 2], U32)
    yidx = st.sb("yidx", [P, 4], U32)

    tx = [st.ps(f"tx{n}", [P, 4, P]) for n in range(2)]
    th = st.ps("th", [P, 2, P])
    py = [st.ps(f"py{n}", [P, 512]) for n in range(2)]
    pr = st.ps("pr", [P, 512])
    ph = [st.ps("ph", [P, 512]), pr]
    pi = st.ps("pi", [P, 512])

    sem = st.sem
    turns_over = sem("turns_over")
    consts = sem("consts")
    sh_in, sh_h, sh_silu, sh_hh, sh_th, sh_hT, sh_y, sh_acc = [sem("sh_" + x) for x in "in h silu hh th hT y acc".split()]
    lg_done, lg_ready, lg_turned, sg_ready = sem("lg_done"), sem("lg_ready"), sem("lg_turned"), sem("sg_ready")
    dve_step, iota_ready, sel_ready, pos_done, route_ready = (sem("dve_step"), sem("iota_ready"), sem("sel_ready"),
                                                              sem("pos_done"), sem("route_ready"))
    xg_in, ov_xg_in = [sem(f"xg_in{n}") for n in range(2)], sem("ov_xg_in")
    y_out = [sem(f"y_out{n}") for n in range(2)]
    hot_ready, idx_done, idx_ready, gathering = sem("hot_ready"), sem("idx_done"), sem("idx_ready"), sem("gathering")
    tx_done, xT_act, xT_dve = sem("tx_done"), sem("xT_act"), sem("xT_dve")
    h_done, silu_ready, hh_ready, th_done, hT_ready = (sem("h_done"), sem("silu_ready"), sem("hh_ready"), sem("th_done"),
                                                       sem("hT_ready"))
    y_done, y_ready = sem("y_done"), sem("y_ready")
    ov = {x: sem("ov_" + x) for x in
          "w pcol hot idxp idx tx xTa xTd h silu hh th hT y ysb out turn".split()}
    YG = 2
    NYG = 4
    yg_in = [sem(f"yg_in{n}") for n in range(NYG)]
    yg_used = sem("yg_used")
    yg = w13[:, 0:2].rearrange("p s a k e -> p (s a k e)").rearrange("p (n k d) -> p n k d", k=YG, d=D)

    def half(n):
        return slice(n * 512, (n + 1) * 512)

    FIRST, LAST = "first", "last"

    def for_all_steps(eng, step):
        for u in range(4):
            step(0, u, FIRST)
        with eng.Fori(1, NE // 4 - 1) as i:
            for u in range(4):
                step(i, u, None)
        for u in range(4):
            step(NE // 4 - 1, u, LAST)

    def further(eng, block):
        total = eng.value_load(ovi[0:1, OVB:OVB + 1], min_val=0, max_val=OVB)
        for lo, hi in ((0, 2), (2, OVB)):
            with eng.If(lo < total):
                with eng.Fori(lo, hi) as j:
                    with eng.If(j < total):
                        block(j)
                eng.sem_inc(turns_over, 1)

    def column(t, e, where):
        return t[:, :, bass.ds(e, 1)] if where is None else t[:, :, e:e + 1]

    with nc.Block() as block:
        @block.sync
        def _(sp):
            sp.wait_ge(ew.h_out, 16 * TT)
            for e in range(ew.EARLY, 4):
                ew.load_up(sp, e, e, w13_in[e])
            with sp.Fori(0, NE // 4 - 1) as i:
                for u in range(4):
                    e = 4 * i + u
                    sp.wait_ge(h_done, e + 3)
                    sp.sem_inc(gathering, 1)
                    ew.load_up(sp, e + 4, u, w13_in[u])
                    sp.wait_ge(y_done, e + 3)
                    sp.sem_inc(gathering, 1)
                    ew.load_down(sp, e + 2, u % 2, w2_in[u % 2])
            for e in range(NE - 4, NE - 2):
                sp.wait_ge(y_done, e + 3)
                ew.load_down(sp, e + 2, e % 2, w2_in[e % 2])
            sp.wait_ge(h_done, NE + 1)
            for a, name in enumerate(("shared_w1", "shared_w3")):
                sp.dma_start(ew.up_slot(2, a), A[name][l].rearrange("(p k) n -> p (k n)", k=KT)).then_inc(sh_in, 16)
            sp.wait_ge(y_done, NE + 1)
            sp.dma_start(ew.down_slot(0), A["shared_w2"][l].rearrange("(p k) n -> p (k n)", k=2)).then_inc(sh_in, 16)
            sp.wait_ge(y_done, NE + 2)
            sp.wait_ge(route_ready, 1)

            def block(j):
                e = sp.value_load(ovi[0:1, bass.ds(j, 1)], min_val=0, max_val=NE - 1)
                ew.load_up(sp, e, 0, ov["w"])
                ew.load_down(sp, e, 1, ov["w"])
                sp.wait_ge(ov["out"], 16 * j + 16)
                sp.sem_inc(ov["turn"], 1)

            further(sp, block)
            for b in range(2):
                sp.wait_ge(y_out[b], 16 * (NE // 2))
            for m in range(TT * TOPK // YG):
                t, k = m * YG // TOPK, m * YG % TOPK
                if m >= NYG:
                    sp.wait_ge(yg_used, YG * (m - NYG + 1))
                sp.dma_start(yg[:, m % NYG], y_rows.rearrange("(t p k) d -> p t k d", p=P, k=TOPK)[:, t, k:k + YG])\
                  .then_inc(yg_in[m % NYG], 16)

        @block.scalar
        def _(act):
            act.wait_ge(lg_done, 1)
            nc.scalar.copy(lgT[:], pr[0:NE, :]).then_inc(lg_ready, 1)
            act.wait_ge(lg_turned, 1)
            nc.scalar.activation(sg[:], pi[:, 0:TT * NE].rearrange("p (t e) -> p t e", e=NE), ACT.Sigmoid).then_inc(sg_ready, 1)
            def turned(k, slot):
                act.wait_ge(tx_done, 2 * k + 2)
                nc.scalar.copy(xT[:, slot, 0:4], tx[0][:]).then_inc(xT_act, 1)

            def silu(k, slot):
                act.wait_ge(h_done, k + 3)
                nc.scalar.activation(act_s[:, slot, 0:ED], ph[slot][:, 0:ED], ACT.Silu).then_inc(silu_ready, 1)

            def step(i, u, where):
                e, b = 4 * i + u, u % 2
                act.wait_ge(th_done, e + 1)
                nc.scalar.copy(hT2[:, b], th[:]).then_inc(hT_ready, 1)
                if where != LAST or u < 2:
                    turned(e + 2, b)
                if where != LAST or u < 3:
                    silu(e + 1, 1 - b)
                if where != FIRST or u >= 2:
                    act.wait_ge(y_out[b], 32 * i + 16 * (u // 2))
                act.wait_ge(y_done, e + 3)
                for n in range(2):
                    nc.scalar.copy(ysb[:, b, half(n)], py[n][:]).then_inc(y_ready, 1)

            act.sem_inc(y_ready, 1)
            turned(0, 0), silu(0, 0), turned(1, 1)
            for_all_steps(act, step)
            act.wait_ge(y_out[0], 16 * (NE // 2))
            act.wait_ge(y_out[1], 16 * (NE // 2))

            def block(j):
                act.wait_ge(ov["tx"], 2 * j + 2)
                nc.scalar.copy(xT[:, 0, 0:4], tx[0][:]).then_inc(ov["xTa"], 1)
                act.wait_ge(ov["h"], j + 1)
                nc.scalar.activation(act_s[:, 0, 0:ED], ph[0][:, 0:ED], ACT.Silu).then_inc(ov["silu"], 1)
                act.wait_ge(ov["th"], j + 1)
                nc.scalar.copy(hT2[:, 0], th[:]).then_inc(ov["hT"], 1)
                act.wait_ge(ov["y"], j + 1)
                for n in range(2):
                    nc.scalar.copy(ysb[:, 0, n * 512:(n + 1) * 512], py[n][:]).then_inc(ov["ysb"], 1)
                act.wait_ge(ov["out"], 16 * j + 16)
                act.sem_inc(ov["turn"], 1)

            further(act, block)
            for t in range(TT):
                act.wait_ge(sh_h, t + 1)
                if t >= 2:
                    act.wait_ge(sh_hh, t - 1)
                nc.scalar.activation(act_s[:, t % 2, 0:ED], ph[t % 2][:, 0:ED], ACT.Silu).then_inc(sh_silu, 1)
                nc.scalar.copy(act_s[:, t % 2, ED:F2], ph[t % 2][:, ED:F2]).then_inc(sh_silu, 1)
                act.wait_ge(sh_th, t + 1)
                nc.scalar.copy(hT2[:, t % 2], th[:]).then_inc(sh_hT, 1)

        @block.gpsimd
        def _(pool):
            pool.iota(ii[:], pattern=[[1, P]], base=0, channel_multiplier=0).then_inc(iota_ready, 1)
            pool.iota(pidx[:, :, 0], pattern=[[P, TT]], base=-SEQ, channel_multiplier=0).then_inc(iota_ready, 1)
            pool.iota(pidx[:, :, 1], pattern=[[0, TT]], base=0, channel_multiplier=1).then_inc(iota_ready, 1)
            pool.memset(before[:], 1.0).then_inc(iota_ready, 1)
            pool.memset(xg[:], 0.0).then_inc(iota_ready, 1)
            pool.wait_ge(iota_ready, 5)
            pool.affine_select(out=before[:], in_=before[:], compare_op=ALU.is_gt, fill=0.0, base=0,
                               pattern=[[1, P]], channel_multiplier=-1).then_inc(iota_ready, 1)
            def gather(b, done):
                pool.indirect_dma_start(xg[:, b], None, h_rows, bass.IndirectOffsetOnAxis(ap=idx[:, b:b + 1], axis=0),
                                        bounds_check=SEQ - 1, oob_is_err=False).then_inc(done, 16)

            def scatter(b, s, done):
                pool.indirect_dma_start(y_rows, bass.IndirectOffsetOnAxis(ap=yidx[:, s:s + 1], axis=0), ysb[:, b], None,
                                        bounds_check=SEQ * TOPK - 1, oob_is_err=False).then_inc(done, 16)

            pool.wait_ge(ew.h_out, 16 * TT)
            for b in range(2):
                pool.wait_ge(idx_ready, 2 * b + 1)
                gather(b, xg_in[b])
            pool.wait_ge(idx_ready, 5)
            pool.wait_ge(tx_done, 2)
            gather(0, xg_in[0])

            def step(i, u, where):
                e, b = 4 * i + u, u % 2
                if where != LAST or u < 1:
                    pool.wait_ge(idx_ready, 2 * e + 7)
                    pool.wait_ge(tx_done, 2 * e + 4)
                    pool.sem_inc(gathering, 1)
                    gather(1 - b, xg_in[1 - b])
                pool.wait_ge(y_ready, 2 * e + 3)
                pool.sem_inc(gathering, 1)
                scatter(b, u, y_out[b])

            for_all_steps(pool, step)
            for b in range(2):
                pool.wait_ge(xg_in[b], 16 * (NE // 2))
                pool.wait_ge(y_out[b], 16 * (NE // 2))

            def block(j):
                pool.wait_ge(ov["idx"], 2 * j + 2)
                pool.sem_inc(gathering, 1)
                gather(0, ov_xg_in)
                pool.wait_ge(ov["ysb"], 2 * j + 2)
                pool.sem_inc(gathering, 1)
                scatter(0, 0, ov["out"])
                pool.wait_ge(ov["out"], 16 * j + 16)
                pool.sem_inc(ov["turn"], 1)

            further(pool, block)
            for t in range(TT):
                pool.wait_ge(sh_silu, 2 * t + 2)
                if t >= 2:
                    pool.wait_ge(sh_th, t - 1)
                pool.tensor_tensor(hh[:, t % 2], act_s[:, t % 2, 0:ED], act_s[:, t % 2, ED:F2], ALU.mult).then_inc(sh_hh, 1)

        @block.vector
        def _(dve):
            ch = Chain(dve, dve_step)
            dve.wait_ge(iota_ready, 6)
            ch.do(nc.vector.tensor_copy(iota[:], ii[:]))
            ch.do(nc.vector.tensor_copy(tokf[:], pidx[:]))
            for a in range(2):
                ch.do(nc.vector.memset(offs[:, 2 * a:2 * a + 1], float(SEQ * (1, TOPK)[a] // P)))
                ch.do(nc.vector.memset(offs[:, 2 * a + 1:2 * a + 2 + a], 0.0))
            ch.sync()
            for a in range(2):
                v = tokf[:].rearrange("p t (o a) -> p t o a", o=1).broadcast_to([P, TT, NE, 2])
                nc.vector.tensor_scalar(num[:, :, :, 2 * a:2 * a + 2], v, float((1, TOPK)[a]), None, ALU.mult).then_inc(consts, 1)
            nc.vector.memset(num[:, :, :, 4], 0.0).then_inc(consts, 1)
            nc.vector.memset(onesb[:], 1.0).then_inc(consts, 1)
            ch.do(nc.vector.memset(gpad[:], NEG))
            ch.do(nc.vector.memset(grep[:], NEG))
            dve.wait_ge(router_in, 32)
            dve.wait_ge(sg_ready, 1)
            rbb = rb[:].rearrange("p (a n) -> p a n", a=1).broadcast_to([P, TT, NE])
            ch.do(nc.vector.tensor_tensor(biased[:], sg[:], rbb, ALU.add))
            ch.sync()
            for t in range(TT):
                for g in range(NG):
                    ch.do(nc.vector.max(g8[:, t, g], biased[:, t, g * 8:(g + 1) * 8]))
            ch.sync()
            ch.do(nc.vector.tensor_tensor(gpad[:, :, 0:NG], g8[:, :, :, 0], g8[:, :, :, 1], ALU.add))
            ch.sync()
            for t in range(TT):
                ch.do(nc.vector.max(v8[:, t], gpad[:, t, 0:NG]))
            ch.sync()
            ch.do(nc.vector.tensor_copy(grep[:, :, 0:TOPG], v8[:, :, 0:TOPG]))
            ch.sync()
            for t in range(TT):
                ch.do(nc.vector.match_replace(gm[:, t], grep[:, t], gpad[:, t], PICKED))
            ch.sync()
            ch.do(nc.vector.tensor_scalar(gm[:], gm[:], PICKED, NEG, ALU.not_equal, ALU.mult))
            ch.sync()
            gmb = gm[:, :, 0:NG].rearrange("p t (g o) -> p t g o", o=1).broadcast_to([P, TT, NG, 8])
            ch.do(nc.vector.tensor_tensor(biased[:].rearrange("p t (g e) -> p t g e", e=8),
                                          biased[:].rearrange("p t (g e) -> p t g e", e=8), gmb, ALU.add))
            ch.sync()
            for t in range(TT):
                ch.do(nc.vector.max(v8[:, t], biased[:, t]))
            ch.sync()
            for t in range(TT):
                ch.do(nc.vector.match_replace(left[:, t], v8[:, t], biased[:, t], PICKED))
            ch.sync()
            nc.vector.tensor_scalar(sel[:], left[:], PICKED, None, ALU.is_equal).then_inc(sel_ready, 1)
            ch.do(nc.vector.tensor_scalar(self32[:], left[:], PICKED, None, ALU.is_equal))
            ch.sync()
            for t in range(TT):
                ch.do(nc.vector.tensor_tensor_scan(kth[:, t], c.ones[:, 0:NE], self32[:, t], 0.0, ALU.mult, ALU.add))
            ch.do(nc.vector.tensor_scalar(left[:], self32[:], -BIG, BIG, ALU.mult, ALU.add))
            ch.sync()
            ch.do(nc.vector.tensor_tensor(kth[:], kth[:], self32[:], ALU.subtract))
            ch.sync()
            dve.wait_ge(consts, 4)
            nc.vector.tensor_copy(num[:, :, 0:NE, 4], kth[:]).then_inc(consts, 1)
            dve.wait_ge(pos_done, 1)
            prt = pr[:, 0:TT * NE].rearrange("p (t e) -> p t e", e=NE)
            ch.do(nc.vector.tensor_copy(cnt[:], pr[:, TT * NE:(TT + 1) * NE]))
            nc.vector.tensor_tensor(pos[:, :, 0:NE], left[:], prt, ALU.add).then_inc(hot_ready, 1)
            dve.wait_ge(hot_ready, 1)
            dve.wait_ge(sel_ready, 1)
            def one_hot(col, b):
                return nc.vector.tensor_tensor(onehot[:, b], iota[:].rearrange("p (a n) -> p a n", a=1).broadcast_to([P, TT, P]),
                                               col.broadcast_to([P, TT, P]), ALU.is_equal)

            def to_gather(b):
                with nc.allow_low_precision(reason="sums of small integers"):
                    return nc.vector.tensor_reduce(idx[:, b:b + 1], pi[:, 0:2], AX.X, ALU.add)

            def to_write(s):
                with nc.allow_low_precision(reason="sums of small integers"):
                    return nc.vector.tensor_reduce(yidx[:, s:s + 1], pi[:, 2:5], AX.X, ALU.add)

            def turned(k, slot):
                dve.wait_ge(tx_done, 2 * k + 2)
                nc.vector.tensor_copy(xT[:, slot, 4:8], tx[1][:]).then_inc(xT_dve, 1)

            def product(k, slot):
                dve.wait_ge(silu_ready, k + 1)
                nc.vector.tensor_tensor(hh[:, slot], act_s[:, slot, 0:ED], ph[slot][:, ED:F2], ALU.mult).then_inc(hh_ready, 1)

            for e in range(3):
                one_hot(pos[:, :, e:e + 1], e % 2).then_inc(hot_ready, 1)
                dve.wait_ge(idx_done, e + 1)
                if e == 2:
                    dve.wait_ge(xg_in[0], 16)
                to_gather(e % 2).then_inc(idx_ready, 1)
                to_write(e).then_inc(idx_ready, 1)
            one_hot(pos[:, :, 3:4], 1).then_inc(hot_ready, 1)
            turned(0, 0), turned(1, 1), product(0, 0)

            def step(i, u, where):
                e, b = 4 * i + u, u % 2
                if where != LAST or u < 1:
                    dve.wait_ge(idx_done, e + 4)
                    to_gather(1 - b).then_inc(idx_ready, 1)
                if where != LAST:
                    one_hot(column(pos, e + 4, where), b).then_inc(hot_ready, 1)
                if where != LAST or u < 2:
                    turned(e + 2, b)
                if where != LAST or u < 3:
                    product(e + 1, 1 - b)
                if where == FIRST:
                    gates(u)
                if where != LAST or u < 1:
                    if where != FIRST or u:
                        dve.wait_ge(y_out[1 - b], 32 * i + 16 * ((u + 1) // 2))
                    to_write((u + 3) % 4).then_inc(idx_ready, 1)
                if where == FIRST and u == 3:
                    further_blocks()

            def gates(t):
                ch.do(nc.vector.tensor_tensor(kth[:, t], kth[:, t], left[:, t], ALU.add))
                ch.sync()
                ks = iota[:, 0:TOPK].rearrange("p (k o) -> p k o", o=1).broadcast_to([P, TOPK, NE])

                def per_k(ap):
                    return ap.rearrange("p (a n) -> p a n", a=1).broadcast_to([P, TOPK, NE])

                ch.do(nc.vector.tensor_tensor(hot[:], per_k(kth[:, t]), ks, ALU.is_equal))
                ch.sync()
                ch.do(nc.vector.tensor_tensor(hot[:], hot[:], per_k(sg[:, t]), ALU.mult))
                ch.sync()
                ch.do(nc.vector.tensor_reduce(gate[:, t], hot[:], AX.X, ALU.add))
                ch.sync()

            def further_blocks():
                ch.do(nc.vector.tensor_reduce(gsum[:], gate[:], AX.X, ALU.add))
                ch.sync()
                ch.do(nc.vector.reciprocal(gsum[:], gsum[:]))
                ch.sync()
                ch.do(nc.vector.scalar_tensor_tensor(out=gate[:], in0=gate[:], scalar=ROUTED_SCALE,
                                                     in1=gsum[:].rearrange("p (t o) -> p t o", o=1).broadcast_to([P, TT, TOPK]),
                                                     op0=ALU.mult, op1=ALU.mult))
                ch.sync()
                ch.do(nc.vector.tensor_scalar(nov[:], cnt[:], float(CAP), None, ALU.is_gt))
                ch.sync()
                for n in range(2, SEQ // CAP):
                    ch.do(nc.vector.scalar_tensor_tensor(out=nov[:], in0=cnt[:], scalar=float(n * CAP), in1=nov[:],
                                                         op0=ALU.is_gt, op1=ALU.add))
                    ch.sync()
                ch.do(nc.vector.tensor_tensor_scan(incl[:], c.ones[:, 0:NE], nov[:], 0.0, ALU.mult, ALU.add))
                ch.sync()
                jj = iota[:, 0:OVB].rearrange("p (j o) -> p j o", o=1).broadcast_to([P, OVB, NE])

                def per_j(ap):
                    return ap.rearrange("p (a n) -> p a n", a=1).broadcast_to([P, OVB, NE])

                ch.do(nc.vector.tensor_tensor(ind[:], per_j(incl[:]), jj, ALU.is_le))
                ch.sync()
                ch.do(nc.vector.tensor_reduce(ovf[:, 0], ind[:], AX.X, ALU.add))
                ch.sync()
                ch.do(nc.vector.tensor_tensor(ind[:], ind[:], per_j(nov[:]), ALU.mult))
                ch.do(nc.vector.tensor_scalar(ovi[0:1, 0:OVB], ovf[0:1, 0], float(NE - 1), None, ALU.min))
                ch.sync()
                ch.do(nc.vector.tensor_reduce(ovf[:, 1], ind[:], AX.X, ALU.add))
                ch.sync()
                ch.do(nc.vector.tensor_tensor(ovf[:, 1], iota[:, 0:OVB], ovf[:, 1], ALU.subtract))
                ch.sync()
                ch.do(nc.vector.tensor_scalar(ovf[:, 1], ovf[:, 1], float(CAP), float(CAP), ALU.mult, ALU.add))
                ch.sync()
                nc.vector.tensor_copy(ovi[0:1, OVB:OVB + 1], incl[0:1, NE - 1:NE]).then_inc(route_ready, 1)
                dve.wait_ge(route_ready, 1)

            for_all_steps(dve, step)
            dve.wait_ge(xg_in[0], 16 * (NE // 2))
            dve.wait_ge(xg_in[1], 16 * (NE // 2))
            for b in range(2):
                dve.wait_ge(y_out[b], 16 * (NE // 2))

            def block(j):
                e = dve.value_load(ovi[0:1, bass.ds(j, 1)], min_val=0, max_val=NE - 1)
                nc.vector.tensor_scalar(pcol[:], pos[:, :, bass.ds(e, 1)].rearrange("p t a -> p (t a)"),
                                        ovf[:, 1, bass.ds(j, 1)], None, ALU.subtract).then_inc(ov["pcol"], 1)
                dve.wait_ge(ov["pcol"], j + 1)
                one_hot(pcol[:].rearrange("p (t o) -> p t o", o=1), 0).then_inc(ov["hot"], 1)
                dve.wait_ge(ov["idxp"], j + 1)
                with nc.allow_low_precision(reason="sums of small integers"):
                    nc.vector.tensor_reduce(idx[:, 0:1], pi[:, 0:2], AX.X, ALU.add).then_inc(ov["idx"], 1)
                    nc.vector.tensor_reduce(yidx[:, 0:1], pi[:, 2:5], AX.X, ALU.add).then_inc(ov["idx"], 1)
                dve.wait_ge(ov["tx"], 2 * j + 2)
                nc.vector.tensor_copy(xT[:, 0, 4:8], tx[1][:]).then_inc(ov["xTd"], 1)
                dve.wait_ge(ov["silu"], j + 1)
                nc.vector.tensor_tensor(hh[:, 0], act_s[:, 0, 0:ED], ph[0][:, ED:F2], ALU.mult).then_inc(ov["hh"], 1)
                dve.wait_ge(ov["out"], 16 * j + 16)
                dve.sem_inc(ov["turn"], 1)

            further(dve, block)
            for t in range(TT):
                a = acc[:, t % 2]
                for k in range(TOPK):
                    n, m = t * TOPK + k, (t * TOPK + k) // YG
                    dve.wait_ge(yg_in[m % NYG], 16 * (m // NYG + 1))
                    src, by = yg[:, m % NYG, k % YG], gate[:, t, k:k + 1]
                    if k == 0:
                        nc.vector.tensor_scalar(a, src, by, None, ALU.mult).then_inc(yg_used, 1)
                    else:
                        nc.vector.scalar_tensor_tensor(out=a, in0=src, scalar=by, in1=a, op0=ALU.mult, op1=ALU.add).then_inc(yg_used, 1)
                    dve.wait_ge(yg_used, n + 1)
                dve.wait_ge(sh_y, t + 1)
                for n in range(2):
                    nc.vector.tensor_tensor(a[:, half(n)], a[:, half(n)], py[n][:], ALU.add).then_inc(sh_acc, 1)
                dve.wait_ge(sh_acc, 2 * t + 2)
                ch.do(nc.vector.scalar_tensor_tensor(out=a, in0=c.ada[:, 2], scalar=1.0, in1=a, op0=ALU.add, op1=ALU.mult))
                ch.sync()
                ch.do(nc.vector.scalar_tensor_tensor(out=c.x[:, t], in0=c.x[:, t], scalar=ALPHA, in1=a, op0=ALU.mult, op1=ALU.add))
            ch.sync()

        @block.tensor
        def _(pe):
            def up(out, xt, ws, done):
                for k in range(KT):
                    last = nc.tensor.matmul(out[:], xt(k), w13[:, ws, :, k], start=k == 0, stop=k == KT - 1)
                last.then_inc(done, 1)

            def turn_h(b, done):
                for k in range(2):
                    last = nc.tensor.transpose(th[:, k], hh[:, b, k::2], c.ident[:])
                last.then_inc(done, 1)

            def down(b, wb, done):
                for n in range(2):
                    for k in range(2):
                        last = nc.tensor.matmul(py[n][:], hT2[:, b, k], w2[:, wb, k, n * 512:(n + 1) * 512],
                                                start=k == 0, stop=k == 1)
                last.then_inc(done, 1)

            def turn_x(b, done):
                for n in range(2):
                    for k in range(4):
                        last = nc.tensor.transpose(tx[n][:, k], xg[:, b, 4 * n + k::KT], c.ident[:])
                    last.then_inc(done, 1)

            def rows(b, at, done):
                nc.tensor.matmul(pi[:, 0:5], onesb[:], offs[:], start=True, stop=False)
                for t in range(TT):
                    last = nc.tensor.matmul(pi[:, 0:5], onehot[:, b, t], at(t), start=False, stop=t == TT - 1)
                last.then_inc(done, 1)

            pe.wait_ge(router_in, 32)
            for k in range(KT):
                last = nc.tensor.matmul(pr[0:NE, :], rw[:, k], c.hT[:, k], start=k == 0, stop=k == KT - 1)
            last.then_inc(lg_done, 1)
            pe.wait_ge(lg_ready, 1)
            for t in range(TT):
                last = nc.tensor.transpose(pi[:, t * NE:(t + 1) * NE], lgT[:, t * P:(t + 1) * P], c.ident[0:NE, 0:NE])
            last.then_inc(lg_turned, 1)
            pe.wait_ge(sel_ready, 1)
            pe.wait_ge(consts, 4)
            for tt in range(TT):
                for s in range(tt + 1):
                    nc.tensor.matmul(pr[:, tt * NE:(tt + 1) * NE], before[:] if s == tt else onesb[:], sel[:, s],
                                     start=s == 0, stop=s == tt)
            for s in range(TT):
                last = nc.tensor.matmul(pr[:, TT * NE:(TT + 1) * NE], onesb[:], sel[:, s], start=s == 0, stop=s == TT - 1)
            last.then_inc(pos_done, 1)
            for e in range(3):
                pe.wait_ge(sg_ready, 1)
                pe.wait_ge(consts, 5)
                pe.wait_ge(hot_ready, e + 2)
                if e:
                    pe.wait_ge(idx_ready, 2 * e)
                rows(e % 2, lambda t: num[:, t, e], idx_done)
            pe.wait_ge(xg_in[0], 16)
            turn_x(0, tx_done)
            pe.sem_inc(h_done, 2)
            pe.sem_inc(y_done, 2)
            pe.wait_ge(idx_ready, 6)
            pe.wait_ge(w13_in[0], 32)
            pe.wait_ge(xT_act, 1)
            pe.wait_ge(xT_dve, 1)
            up(ph[0], lambda k: xT[:, 0, k], 0, h_done)
            pe.wait_ge(xg_in[1], 16)
            turn_x(1, tx_done)

            def step(i, u, where):
                e, b = 4 * i + u, u % 2
                if where != LAST or u < 1:
                    pe.wait_ge(hot_ready, e + 5)
                    pe.wait_ge(idx_ready, 2 * e + 6)
                    at = (lambda t: num[:, t, bass.ds(e + 3, 1)].rearrange("p a n -> p (a n)")) if where is None else \
                        (lambda t: num[:, t, e + 3])
                    rows(1 - b, at, idx_done)
                if where != LAST or u < 3:
                    pe.wait_ge(w13_in[(u + 1) % 4], 32 * i + 32 + 32 * (u // 3))
                    pe.wait_ge(xT_act, e + 2)
                    pe.wait_ge(xT_dve, e + 2)
                    up(ph[1 - b], lambda k: xT[:, 1 - b, k], (u + 1) % 4, h_done)
                pe.wait_ge(hh_ready, e + 1)
                turn_h(b, th_done)
                if where != LAST or u < 2:
                    pe.wait_ge(xg_in[b], 32 * i + 16 * (u // 2) + 32)
                    turn_x(b, tx_done)
                pe.wait_ge(hT_ready, e + 1)
                pe.wait_ge(w2_in[b], 32 * i + 16 * (u // 2) + 16)
                pe.wait_ge(y_ready, 2 * e + 1)
                down(b, b, y_done)

            for_all_steps(pe, step)

            def block(j):
                ex = pe.value_load(ovi[0:1, bass.ds(j, 1)], min_val=0, max_val=NE - 1)
                pe.wait_ge(ov["hot"], j + 1)
                rows(0, lambda t: num[:, t, bass.ds(ex, 1)].rearrange("p a n -> p (a n)"), ov["idxp"])
                pe.wait_ge(ov_xg_in, 16 * j + 16)
                turn_x(0, ov["tx"])
                pe.wait_ge(ov["w"], 48 * j + 48)
                pe.wait_ge(ov["xTa"], j + 1)
                pe.wait_ge(ov["xTd"], j + 1)
                up(ph[0], lambda k: xT[:, 0, k], 0, ov["h"])
                pe.wait_ge(ov["hh"], j + 1)
                turn_h(0, ov["th"])
                pe.wait_ge(ov["hT"], j + 1)
                down(0, 1, ov["y"])
                pe.wait_ge(ov["out"], 16 * j + 16)
                pe.sem_inc(ov["turn"], 1)

            further(pe, block)
            pe.wait_ge(sh_in, 48)
            pe.wait_ge(y_ready, 2 * NE + 1)
            up(ph[0], lambda k: c.hT[:, k, 0:P], 2, sh_h)
            for t in range(TT):
                if t + 1 < TT:
                    if t:
                        pe.wait_ge(sh_silu, 2 * t)
                    up(ph[(t + 1) % 2], lambda k: c.hT[:, k, (t + 1) * P:(t + 2) * P], 2, sh_h)
                pe.wait_ge(sh_hh, t + 1)
                turn_h(t % 2, sh_th)
                pe.wait_ge(sh_hT, t + 1)
                if t:
                    pe.wait_ge(sh_acc, 2 * t)
                down(t % 2, 0, sh_y)
    st.close(gathers=True, beside=ew.st)


def delta_weights(A):
    return A["gdn_w_in"][0].rearrange("(p k) n -> p k n", k=KT)


DELTA_KINDS = (1, 0, 2, 3)


def delta_ring(nc, A):
    at = [kind * GH * GD for kind in DELTA_KINDS]
    return Ring(nc, "gdn_w", 2, [KT, 2 * GD], lambda n: delta_weights(A)[:, :, at[n]:at[n] + 2 * GD])


def delta_stage(nc, c, A, ada_rows, ring):
    st = Stage(nc, "gdn")
    HP = 2
    TURNS = GH // HP
    PF = HP * GD
    KINDS = 4
    K_, Q_, V_, Z_ = DELTA_KINDS
    NCONV = 3 * HP
    W = GH * GD
    TH = TT * GH
    BASE = 16
    LEVELS = (16, 32, 64)

    w, w_in = ring.w, ring.w_in
    raw = st.sb("raw", [P, 2, CONV - 1 + SEQ])
    acc = st.sb("acc", [P, 2, SEQ])
    oT = st.sb("oT", [P, GH, SEQ])
    wab = st.sb("wab", [P, KT, 2 * GH])
    abT = acc[0:2 * GH, 0]
    convw = st.sb("convw", [CONV * 3 * GH, P])
    convT = st.sb("convT", [P, CONV, 3, GH])
    cw = st.sb("cw", [P, CONV, 3, HP])
    nw = st.sb("nw", [P, 1])
    eps = st.sb("eps", [P, 1])
    dtb = st.sb("dtb", [P, GH])
    alog = st.sb("alog", [P, GH])
    soft = st.sb("soft", [P, 5, TT, GH])
    tab = st.sb("tab", [P, 7, TT, GH])
    G_, NGC, NBEG, KD, BE, NBE, GL = range(7)
    cur = st.sb("cur", [P, 7, TT, HP])
    masks = st.sb("masks", [P, 6, P])

    def tiles(name):
        return [st.sb(f"{name}{h}", [P, TT, P]) for h in range(HP)]

    kT, qT, vT, zs, qg, dT, vn, kbe, kdec, vb, M, P0, P1, Q0, Q1, E0, E1, qkT = [
        tiles(x) for x in "kT qT vT zs qg dT vn kbe kdec vb M P0 P1 Q0 Q1 E0 E1 qkT".split()]
    wT = vT
    S = st.sb("S", [P, HP, 2, P])
    ada = AdaRows(nc, c, st, A, (3,), ada_rows, 2)
    pj = [st.ps(f"pj{n}", [P, 512]) for n in range(2)]
    ps = [[st.ps(f"ps{h}{n}", [P, TT, P]) for n in range(3)] for h in range(HP)]

    r, q = np.arange(P)[:, None], np.arange(P)[None, :]
    below = (q < r) & (q // BASE == r // BASE)
    links = [(r // (2 * b) == q // (2 * b)) & (r // b % 2 == 1) & (q // b % 2 == 0) for b in LEVELS]
    pre = [ps[0][n][:].rearrange("p t n -> p (t n)") for n in (1, 2)]
    side = [pj[n][:, 0:ada.QA // 2] for n in range(2)]
    table = np.stack([below, below.T] + links + [np.where(r <= q, 0.0, NEG)], 1).astype(np.float32)
    BELOW, ABOVE, LINK, CAUSAL = 0, 1, 2, 5
    mask_dram = nc.inline_tensor(table.reshape(P, -1), "delta_masks")

    sem = st.sem
    small_in, abw_in, conv_in = sem("small_in"), sem("abw_in"), sem("conv_in")
    proj_done, proj_free, silu_ready, conv_ready = sem("proj_done"), sem("proj_free"), sem("silu_ready"), sem("conv_ready")
    ab_done, ab_copied, ab_turned, conv_turned = sem("ab_done"), sem("ab_copied"), sem("ab_turned"), sem("conv_turned")
    x_ready, act_small, g_ready, gc_done, kd_arg, tab_ready = (sem("x_ready"), sem("act_small"), sem("g_ready"), sem("gc_done"),
                                                               sem("kd_arg"), sem("tab_ready"))
    k_ln, q_ln, o_ln = sem("k_ln"), sem("q_ln"), sem("o_ln")
    dve_step, conv_step, cur_ready, gb_ready = sem("dve_step"), sem("conv_step"), sem("cur_ready"), sem("gb_ready")
    w_asked = sem("w_asked")
    (gc_row, eg_row, masked, dT_ready, kk_sq, kk_norm, k_rs, kT_ready, q_sq, q_norm, q_rs, qT_ready, k_turned, kbe_ready,
     kdec_ready, kk_done, G_ready, G_turned, M_ready, M_turned, Q_ready, P_ready, E_first, v_turned, vb_ready, qk_done,
     qk_ready, qg_ready) = [sem(x) for x in (
        "gc_row eg_row masked dT_ready k_sq k_norm k_rs kT_ready q_sq q_norm q_rs qT_ready k_turned kbe_ready "
        "kdec_ready kk_done G_ready G_turned M_ready M_turned Q_ready P_ready E_first v_turned vb_ready qk_done "
        "qk_ready qg_ready").split()]
    pw_done = [sem(f"pw_done{n}") for n in range(3)]
    pw_ready = [sem(f"pw_ready{n}") for n in range(3)]
    e_done = [sem(f"e_done{n}") for n in range(6)]
    e_ready = [sem(f"e_ready{n}") for n in range(6)]
    d_done = [sem(f"d_done{n}") for n in range(3)]
    d_ready = [sem(f"d_ready{n}") for n in range(3)]
    n_ready = [sem(f"n_ready{n}") for n in range(3)]
    y_done_ = [sem(f"y_done{n}") for n in range(3)]
    y_ready_ = [sem(f"y_ready{n}") for n in range(3)]
    w_done, w_ready = sem("w_done"), sem("w_ready")
    vn_done, vn_ready, s_done, s_ready, o_done = sem("vn_done"), sem("vn_ready"), sem("s_done"), sem("s_ready"), sem("o_done")
    o_sq, o_norm, o_rs, o_scaled, o_ready = sem("o_sq"), sem("o_norm"), sem("o_rs"), sem("o_scaled"), sem("o_ready")
    out_done, out_used = sem("out_done"), sem("out_used")

    w_dram = delta_weights(A)
    wo_dram = A["gdn_w_out"][0].rearrange("(k p) n -> p k n", p=P)
    order = [K_, Q_, V_, Z_]

    def rowp(ap):
        return ap.rearrange("(a n) -> a n", a=1).partition_broadcast(P)

    def flat(t):
        return t[:].rearrange("p t n -> p (t n)")

    def over_t(m):
        return m.rearrange("p (a n) -> p a n", a=1).broadcast_to([P, TT, P])

    def col(kind, h):
        return cur[:, kind, :, h:h + 1].broadcast_to([P, TT, P])

    with nc.Block() as block:
        @block.sync
        def _(sp):
            sp.dma_start(wab[:], w_dram[:, :, 4 * W:4 * W + 2 * GH]).then_inc(abw_in, 16)
            sp.sem_inc(ada.stored, 16)
            def turn(i, first):
                ada.load_bias(sp, i)
                for n, kind in enumerate(order):
                    if first and n < ring.slots:
                        continue
                    sp.wait_ge(proj_done, 2 * KINDS * i + 2 * n + 2)
                    sp.sem_inc(w_asked, 1)
                    sp.dma_start(w[:, n % 2], w_dram[:, :, bass.ds(i * PF + kind * W, PF)]).then_inc(w_in[n % 2], 16)
                ada.store(sp, i)

            turn(0, True)
            with sp.Fori(1, TURNS) as i:
                turn(i, False)
            for n in range(4):
                if n < 2:
                    sp.wait_ge(proj_done, 2 * KINDS * TURNS + 2 * n + 2)
                else:
                    sp.wait_ge(out_done, TT * (n - 1))
                sp.dma_start(w[:, n % 2], wo_dram[:, :, n * PF:(n + 1) * PF]).then_inc(w_in[n % 2], 16)
            sp.wait_ge(ada.stored, 16 * TURNS + 16)

        @block.scalar
        def _(act):
            act.dma_start(convw[:], A["gdn_conv_w"][0].rearrange("j (m p) -> (j m) p", p=P)).then_inc(conv_in, 16)
            act.dma_start(nw[:], A["gdn_norm_w"][0].rearrange("(p a) -> p a", a=1)).then_inc(small_in, 16)
            act.dma_start(dtb[:], rowp(A["gdn_dt_bias"][0])).then_inc(small_in, 16)
            act.dma_start(alog[:], rowp(A["gdn_a_log"][0])).then_inc(small_in, 16)
            act.dma_start(masks[:], mask_dram.ap().rearrange("p (m n) -> p m n", n=P)).then_inc(small_in, 16)
            act.sem_inc(proj_free, 2)
            act.wait_ge(ab_done, 1)
            nc.scalar.copy(abT, pre[0][0:2 * GH, :]).then_inc(ab_copied, 1)
            act.wait_ge(ab_turned, 1)
            abv = pre[1][:, 0:2 * TH].rearrange("p (t n) -> p t n", t=TT)
            nc.scalar.activation(tab[:, BE], abv[:, :, GH:2 * GH], ACT.Sigmoid).then_inc(act_small, 1)
            act.wait_ge(small_in, 64)
            nc.scalar.activation(alog[:], alog[:], ACT.Exp).then_inc(act_small, 1)
            act.wait_ge(x_ready, 1)
            nc.scalar.activation(soft[:, 1], soft[:, 1], ACT.Exp, scale=-1.0).then_inc(act_small, 1)
            act.wait_ge(x_ready, 2)
            nc.scalar.activation(soft[:, 3], soft[:, 2], ACT.Ln).then_inc(act_small, 1)
            act.wait_ge(gc_done, 1)
            gcv = pre[1][:, 0:2 * TH].rearrange("p (s t n) -> p s t n", s=2, t=TT)
            nc.scalar.activation(soft[:, 0], gcv[:, 0], ACT.Exp).then_inc(act_small, 1)
            nc.scalar.activation(tab[:, GL], gcv[:, 1], ACT.Exp).then_inc(act_small, 1)
            act.wait_ge(kd_arg, 1)
            nc.scalar.activation(tab[:, KD], soft[:, 1], ACT.Exp).then_inc(act_small, 1)
            act.sem_inc(silu_ready, 2)

            with act.Fori(0, TURNS) as i:
                def copy_raw(m):
                    act.wait_ge(proj_done, 2 * KINDS * i + m + 5)
                    act.wait_ge(conv_ready, NCONV * i + m + 1)
                    nc.scalar.copy(raw[:, m % 2, CONV - 1:], pj[m % 2][:]).then_inc(proj_free, 1)

                def silu(m, dst):
                    act.wait_ge(conv_ready, NCONV * i + m + 3)
                    nc.scalar.activation(flat(dst), acc[:, m % 2], ACT.Silu).then_inc(silu_ready, 1)

                copy_raw(0), copy_raw(1), silu(0, kT[0]), silu(1, kT[1])
                copy_raw(2), silu(2, qT[0]), copy_raw(3), silu(3, qT[1])
                for h in range(HP):
                    act.wait_ge(kk_norm, 2 * i + h + 1)
                    nc.scalar.activation(E1[h][:], ps[h][1][:], ACT.Ln, bias=eps[:]).then_inc(k_ln, 1)
                copy_raw(4)
                for h in range(HP):
                    act.wait_ge(q_norm, 2 * i + h + 1)
                    nc.scalar.activation(E0[h][:], ps[h][2][:], ACT.Ln, bias=eps[:]).then_inc(q_ln, 1)
                for h in range(HP):
                    act.wait_ge(k_ln, 2 * i + h + 1)
                    nc.scalar.activation(E1[h][:], E1[h][:], ACT.Exp, scale=-0.5).then_inc(k_rs, 1)
                for h in range(HP):
                    act.wait_ge(q_ln, 2 * i + h + 1)
                    nc.scalar.activation(E0[h][:], E0[h][:], ACT.Exp, scale=-0.5).then_inc(q_rs, 1)
                for h in range(HP):
                    n = 2 * i + h + 1
                    act.wait_ge(masked, n)
                    nc.scalar.activation(qg[h][:], ps[h][0][:], ACT.Exp).then_inc(eg_row, 1)
                    for t in range(TT):
                        last = nc.scalar.activation(dT[h][:, t], P1[h][:, t], ACT.Exp, bias=cur[:, NGC, t, h:h + 1])
                    last.then_inc(dT_ready, 1)
                silu(4, vT[0]), copy_raw(5), silu(5, vT[1])
                for h in range(HP):
                    act.wait_ge(proj_done, 2 * KINDS * i + 6 + h + 5)
                    nc.scalar.activation(flat(zs[h]), pj[h][:], ACT.Silu).then_inc(proj_free, 1)
                for s, (pd, qd) in enumerate(((P1, Q1), (P0, Q0), (P1, None))):
                    for h in range(HP):
                        act.wait_ge(pw_done[s], 2 * i + h + 1)
                        if s == 1:
                            act.wait_ge(E_first, 2 * i + h + 1)
                        last = nc.scalar.copy(pd[h][:], ps[h][1][:])
                        if qd is not None:
                            last = nc.scalar.copy(qd[h][:], ps[h][2][:])
                        last.then_inc(pw_ready[s], 1)
                for s in range(3):
                    for h in range(HP):
                        act.wait_ge(d_done[s], 2 * i + h + 1)
                        nc.scalar.copy(Q0[h][:], ps[h][1][:]).then_inc(d_ready[s], 1)
                        act.wait_ge(y_done_[s], 2 * i + h + 1)
                        nc.scalar.copy(Q1[h][:], ps[h][2][:]).then_inc(y_ready_[s], 1)
                for h in range(HP):
                    act.wait_ge(w_done, 2 * i + h + 1)
                    nc.scalar.copy(wT[h][:], ps[h][2][:]).then_inc(w_ready, 1)
                for t in range(TT):
                    for h in range(HP):
                        act.wait_ge(vn_done, 2 * TT * i + 2 * t + h + 1)
                        nc.scalar.copy(vn[h][:, t], ps[h][1][:, t]).then_inc(vn_ready, 1)
                for h in range(HP):
                    act.wait_ge(o_done, 2 * i + h + 1)
                    nc.scalar.activation(P1[h][:], ps[h][0][:], ACT.Square, scale=GD ** -0.5).then_inc(o_sq, 1)
                for h in range(HP):
                    act.wait_ge(o_norm, 2 * i + h + 1)
                    nc.scalar.activation(Q1[h][:], ps[h][1][:], ACT.Ln, bias=eps[:]).then_inc(o_ln, 1)
                for h in range(HP):
                    act.wait_ge(o_ln, 2 * i + h + 1)
                    nc.scalar.activation(Q1[h][:], Q1[h][:], ACT.Exp, scale=-0.5).then_inc(o_rs, 1)

        @block.gpsimd
        def _(pool):
            pool.wait_ge(tab_ready, 1)
            with pool.Fori(0, TURNS) as i:
                for j in range(2):
                    ada.load(pool, i, j)
                for h in range(HP):
                    pool.wait_ge(cur_ready, 2 * i + 2)
                    pool.tensor_tensor(Q1[h][:], over_t(c.ones[:]), col(G_, h), ALU.mult).then_inc(gb_ready, 1)
                for h in range(HP):
                    pool.wait_ge(silu_ready, NCONV * i + h + 3)
                    pool.tensor_tensor(E1[h][:], kT[h][:], kT[h][:], ALU.mult).then_inc(kk_sq, 1)
                for h in range(HP):
                    pool.wait_ge(silu_ready, NCONV * i + h + 5)
                    pool.tensor_tensor(E0[h][:], qT[h][:], qT[h][:], ALU.mult).then_inc(q_sq, 1)
                for h in range(HP):
                    pool.wait_ge(qT_ready, 2 * i + h + 1)
                    pool.wait_ge(eg_row, 2 * i + h + 1)
                    pool.tensor_tensor(qg[h][:], qT[h][:], qg[h][:], ALU.mult).then_inc(qg_ready, 1)
                for h in range(HP):
                    pool.wait_ge(M_ready, 2 * i + h + 1)
                    pool.tensor_tensor(P0[h][:], M[h][:], over_t(masks[:, BELOW]), ALU.mult).then_inc(P_ready, 1)
                for j in range(2, 6):
                    ada.load(pool, i, j)
                for s, dst in enumerate((P0, P1, P0)):
                    for h in range(HP):
                        pool.wait_ge((e_done[1], e_done[2], y_done_[0])[s], 2 * i + h + 1)
                        if s == 0:
                            pool.wait_ge(pw_done[2], 2 * i + h + 1)
                        pool.tensor_tensor(dst[h][:], M[h][:], over_t(masks[:, LINK + s]), ALU.mult).then_inc(n_ready[s], 1)
                    if s == 0:
                        ada.load(pool, i, 6), ada.load(pool, i, 7)

        @block.vector
        def _(dve):
            ch = Chain(dve, dve_step)
            dve.sem_inc(conv_ready, 2)
            dve.sem_inc(o_ready, 2)
            ada.credits(dve)
            ch.do(nc.vector.memset(raw[:, :, 0:CONV - 1], 0.0))
            ch.do(nc.vector.memset(eps[:], RMS_EPS))
            dve.wait_ge(small_in, 64)
            dve.wait_ge(conv_turned, 1)
            ch.do(nc.vector.tensor_copy(convT[:].rearrange("p a b c -> p (a b c)"), pre[0][:, 0:CONV * 3 * GH]))
            dve.wait_ge(act_small, 1)
            abv = pre[1][:, 0:2 * TH].rearrange("p (t n) -> p t n", t=TT)
            x, e, u, ln, fix = [soft[:, n] for n in range(5)]
            ch.do(nc.vector.tensor_tensor(x, abv[:, :, 0:GH], dtb[:].rearrange("p (a n) -> p a n", a=1).broadcast_to([P, TT, GH]), ALU.add))
            ch.sync()
            nc.vector.scalar_tensor_tensor(out=e, in0=x, scalar=-1.0, in1=x, op0=ALU.mult, op1=ALU.max).then_inc(x_ready, 1)
            dve.wait_ge(act_small, 3)
            nc.vector.tensor_scalar(u, e, 1.0, None, ALU.add).then_inc(x_ready, 1)
            dve.wait_ge(x_ready, 2)
            ch.do(nc.vector.tensor_scalar(fix, u, -1.0, None, ALU.add))
            ch.sync()
            ch.do(nc.vector.tensor_tensor(fix, e, fix, ALU.subtract))
            dve.wait_ge(act_small, 4)
            ch.do(nc.vector.reciprocal(u, u))
            ch.sync()
            ch.do(nc.vector.tensor_tensor(fix, fix, u, ALU.mult))
            ch.sync()
            ch.do(nc.vector.tensor_tensor(fix, fix, ln, ALU.add))
            ch.sync()
            ch.do(nc.vector.scalar_tensor_tensor(out=fix, in0=x, scalar=0.0, in1=fix, op0=ALU.max, op1=ALU.add))
            ch.sync()
            nc.vector.scalar_tensor_tensor(out=tab[:, G_], in0=fix, scalar=-1.0,
                                           in1=alog[:].rearrange("p (a n) -> p a n", a=1).broadcast_to([P, TT, GH]),
                                           op0=ALU.mult, op1=ALU.mult).then_inc(g_ready, 1)
            dve.wait_ge(act_small, 6)
            gcv = pre[1][:, 0:2 * TH].rearrange("p (s t n) -> p s t n", s=2, t=TT)
            ch.do(nc.vector.tensor_scalar(tab[:, NGC], gcv[:, 0], -1.0, None, ALU.mult))
            ch.sync()
            nc.vector.tensor_tensor(e, gcv[:, 1], tab[:, NGC], ALU.add).then_inc(kd_arg, 1)
            ch.do(nc.vector.tensor_scalar(tab[:, NBE], tab[:, BE], -1.0, None, ALU.mult))
            ch.sync()
            dve.wait_ge(act_small, 7)
            nc.vector.tensor_tensor(tab[:, NBEG], tab[:, NBE], x, ALU.mult).then_inc(tab_ready, 1)
            dve.wait_ge(tab_ready, 1)
            first = ch.n

            with dve.Fori(0, TURNS) as i:
                def conv(m, kind):
                    dve.wait_ge(proj_free, 2 * KINDS * i + m + 3)
                    dve.wait_ge(silu_ready, NCONV * i + m + 1)
                    for j in range(CONV):
                        src, to = raw[:, m % 2, j:j + SEQ], acc[:, m % 2]
                        wj = cw[:, j, kind, m % 2:m % 2 + 1]
                        if j == 0:
                            last = nc.vector.tensor_scalar(to, src, wj, None, ALU.mult)
                        else:
                            last = nc.vector.scalar_tensor_tensor(out=to, in0=src, scalar=wj, in1=to, op0=ALU.mult, op1=ALU.add)
                        if j < CONV - 1:
                            last.then_inc(conv_step, 1)
                            dve.wait_ge(conv_step, 3 * NCONV * i + 3 * m + j + 1)
                    last.then_inc(conv_ready, 1)

                def with_column(out, in_, kind, h, done):
                    nc.vector.tensor_tensor(out[:], in_[:], col(kind, h), ALU.mult).then_inc(done, 1)

                def mask_causal(h):
                    dve.wait_ge(gc_row, 2 * i + h + 1)
                    nc.vector.tensor_tensor(P1[h][:], ps[h][0][:], over_t(masks[:, CAUSAL]), ALU.add).then_inc(masked, 1)

                def norm_k(h):
                    dve.wait_ge(k_rs, 2 * i + h + 1)
                    nc.vector.tensor_tensor(kT[h][:], kT[h][:], E1[h][:], ALU.mult).then_inc(kT_ready, 1)

                def norm_q(h):
                    dve.wait_ge(q_rs, 2 * i + h + 1)
                    nc.vector.scalar_tensor_tensor(out=qT[h][:], in0=qT[h][:], scalar=GD ** -0.5, in1=E0[h][:],
                                                   op0=ALU.mult, op1=ALU.mult).then_inc(qT_ready, 1)

                def keys(h):
                    dve.wait_ge(k_turned, 2 * i + h + 1)
                    with_column(kbe[h], ps[h][2], NBEG, h, kbe_ready)
                    with_column(kdec[h], ps[h][2], KD, h, kdec_ready)
                    dve.wait_ge(kk_done, 2 * i + h + 1)
                    dve.wait_ge(dT_ready, 2 * i + h + 1)
                    nc.vector.tensor_tensor(Q1[h][:], ps[h][1][:], dT[h][:], ALU.mult).then_inc(G_ready, 1)

                nc.vector.tensor_scalar(cur[:], tab[:, :, :, bass.ds(HP * i, HP)], 1.0, None, ALU.mult).then_inc(cur_ready, 1)
                nc.vector.tensor_scalar(cw[:], convT[:, :, :, bass.ds(HP * i, HP)], 1.0, None, ALU.mult).then_inc(cur_ready, 1)
                dve.wait_ge(cur_ready, 2 * i + 2)
                conv(0, K_), conv(1, K_), mask_causal(0), mask_causal(1)
                conv(2, Q_), conv(3, Q_), conv(4, V_)
                norm_k(0), norm_k(1), norm_q(0), norm_q(1)
                keys(0), keys(1), conv(5, V_)
                for h in range(HP):
                    dve.wait_ge(G_turned, 2 * i + h + 1)
                    with_column(M[h], ps[h][1], NBE, h, M_ready)
                for h in range(HP):
                    n = 2 * i + h + 1
                    dve.wait_ge(v_turned, n)
                    with_column(vb[h], ps[h][2], BE, h, vb_ready)
                    dve.wait_ge(M_turned, n)
                    nc.vector.tensor_tensor(Q0[h][:], ps[h][1][:], over_t(masks[:, ABOVE]), ALU.mult).then_inc(Q_ready, 1)
                    dve.wait_ge(qk_done, n)
                    nc.vector.tensor_tensor(qkT[h][:], ps[h][0][:], dT[h][:], ALU.mult).then_inc(qk_ready, 1)
                    dve.wait_ge(Q_ready, n)
                    nc.vector.tensor_tensor(E0[h][:], Q0[h][:], over_t(c.ident[:]), ALU.add).then_inc(E_first, 1)
                for s in range(6):
                    src, dst = (E0, E1) if s % 2 == 0 else (E1, E0)
                    for h in range(HP):
                        dve.wait_ge(e_done[s], 2 * i + h + 1)
                        dve.wait_ge(E_first if s == 0 else e_ready[s - 1], 2 * i + h + 1)
                        nc.vector.tensor_tensor(dst[h][:], ps[h][0][:], src[h][:], ALU.add).then_inc(e_ready[s], 1)
                    if s < 4:
                        ada.add(dve, i, 2 * s), ada.add(dve, i, 2 * s + 1)
                ada.finish(dve, i, 0, side)
                for t in range(TT - 1):
                    for h in range(HP):
                        dve.wait_ge(s_done, 2 * (TT - 1) * i + 2 * t + h + 1)
                        if t == 0:
                            last = nc.vector.tensor_copy(S[:, h, 0], ps[h][2][:, t])
                        else:
                            dve.wait_ge(s_ready, 2 * (TT - 1) * i + 2 * (t - 1) + h + 1)
                            last = nc.vector.scalar_tensor_tensor(out=S[:, h, t % 2], in0=S[:, h, (t - 1) % 2],
                                                                  scalar=cur[:, GL, t, h:h + 1], in1=ps[h][2][:, t],
                                                                  op0=ALU.mult, op1=ALU.add)
                        last.then_inc(s_ready, 1)
                for h in range(HP):
                    n = 2 * i + h + 1
                    dve.wait_ge(o_rs, n)
                    nc.vector.scalar_tensor_tensor(out=kT[h][:], in0=ps[h][0][:], scalar=nw[:], in1=Q1[h][:],
                                                   op0=ALU.mult, op1=ALU.mult).then_inc(o_scaled, 1)
                    dve.wait_ge(o_scaled, n)
                    nc.vector.tensor_tensor(oT[:, bass.ds(2 * i + h, 1)].rearrange("p a n -> p (a n)"), flat(kT[h]), flat(zs[h]),
                                            ALU.mult).then_inc(o_ready, 1)
            out = Chain(dve, dve_step, first)
            for n in range(4):
                for t in range(TT):
                    j = n * TT + t
                    cols = slice(n * PF, (n + 1) * PF)
                    dve.wait_ge(out_done, j + 1)
                    nc.vector.scalar_tensor_tensor(out=acc[:, j % 2, 0:PF], in0=c.ada[:, 2, cols], scalar=1.0,
                                                   in1=pj[j % 2][:, 0:PF], op0=ALU.add, op1=ALU.mult).then_inc(out_used, 1)
                    dve.wait_ge(out_used, j + 1)
                    out.do(nc.vector.scalar_tensor_tensor(out=c.x[:, t, cols], in0=c.x[:, t, cols], scalar=ALPHA,
                                                          in1=acc[:, j % 2, 0:PF], op0=ALU.mult, op1=ALU.add))
                    out.sync()

        @block.tensor
        def _(pe):
            def each(out, lhsT, rhs):
                for t in range(TT):
                    last = nc.tensor.matmul(out[:, t], lhsT(t), rhs(t), start=True, stop=True)
                return last

            def turn(out, src, done):
                for t in range(TT):
                    last = nc.tensor.transpose(out[:, t], src[:, t], c.ident[:])
                last.then_inc(done, 1)

            pe.wait_ge(abw_in, 16)
            for k in range(KT):
                last = nc.tensor.matmul(pre[0][0:2 * GH, :], wab[:, k], c.hT[:, k], start=k == 0, stop=k == KT - 1)
            last.then_inc(ab_done, 1)
            pe.wait_ge(ab_copied, 1)
            for t in range(TT):
                last = nc.tensor.transpose(pre[1][:, t * 2 * GH:(t + 1) * 2 * GH], abT[:, t * P:(t + 1) * P],
                                           c.ident[0:2 * GH, 0:2 * GH])
            last.then_inc(ab_turned, 1)
            NW = CONV * 3 * GH
            pe.wait_ge(conv_in, 16)
            nc.tensor.transpose(pre[0][:, 0:NW], convw[:], c.ident[0:NW, 0:NW]).then_inc(conv_turned, 1)
            pe.wait_ge(g_ready, 1)
            pe.wait_ge(act_small, 1)
            gflat = tab[:, G_].rearrange("p t n -> p (t n)")
            nc.tensor.matmul(pre[1][:, 0:TH], c.upper[:], gflat, start=True, stop=True)
            nc.tensor.matmul(pre[1][:, TH:2 * TH], c.ones[:], gflat, start=True, stop=True).then_inc(gc_done, 1)
            pe.sem_inc(proj_done, 4)

            with pe.Fori(0, TURNS) as i:
                def proj(m):
                    n, h = m // 2, m % 2
                    if h == 0:
                        pe.wait_ge(w_in[n % 2], 32 * i + 16 * (n // 2) + 16)
                    pe.wait_ge(proj_free, 2 * KINDS * i + m + 1)
                    for k in range(KT):
                        last = nc.tensor.matmul(pj[h][:], w[:, n % 2, k, h * P:(h + 1) * P], c.hT[:, k], start=k == 0, stop=k == KT - 1)
                    last.then_inc(proj_done, 1)

                def sum_squares(bank, sq, ready, h, done):
                    pe.wait_ge(ready, 2 * i + h + 1)
                    nc.tensor.matmul(bank[:].rearrange("p t n -> p (t n)"), c.ones[:], flat(sq), start=True, stop=True).then_inc(done, 1)

                def keys(h):
                    pe.wait_ge(kT_ready, 2 * i + h + 1)
                    turn(ps[h][2], kT[h], k_turned)
                    each(ps[h][1], lambda t: kT[h][:, t], lambda t: kT[h][:, t]).then_inc(kk_done, 1)

                def turn_g(h):
                    pe.wait_ge(G_ready, 2 * i + h + 1)
                    turn(ps[h][1], Q1[h], G_turned)

                def late(h):
                    n = 2 * i + h + 1
                    pe.wait_ge(silu_ready, NCONV * i + 4 + h + 3)
                    pe.wait_ge(qT_ready, n)
                    pe.wait_ge(kdec_ready, n)
                    turn(ps[h][2], vT[h], v_turned)
                    pe.wait_ge(M_ready, n)
                    turn(ps[h][1], M[h], M_turned)
                    each(ps[h][0], lambda t: kT[h][:, t], lambda t: qT[h][:, t]).then_inc(qk_done, 1)

                proj(0), proj(1)
                pe.wait_ge(o_ready, 2 * i + 2)
                for h in range(HP):
                    pe.wait_ge(gb_ready, 2 * i + h + 1)
                    each(ps[h][0], lambda t: Q1[h][:, t], lambda t: c.upper[:]).then_inc(gc_row, 1)
                proj(2), sum_squares(ps[0][1], E1[0], kk_sq, 0, kk_norm)
                proj(3), sum_squares(ps[1][1], E1[1], kk_sq, 1, kk_norm)
                sum_squares(ps[0][2], E0[0], q_sq, 0, q_norm)
                proj(4), sum_squares(ps[1][2], E0[1], q_sq, 1, q_norm)
                proj(5), keys(0), keys(1)
                proj(6), turn_g(0), turn_g(1)
                proj(7), late(0), late(1)
                for h in range(HP):
                    n = 2 * i + h + 1
                    pe.wait_ge(P_ready, n)
                    pe.wait_ge(Q_ready, n)
                    each(ps[h][1], lambda t: Q0[h][:, t], lambda t: P0[h][:, t])
                    each(ps[h][2], lambda t: P0[h][:, t], lambda t: Q0[h][:, t]).then_inc(pw_done[0], 1)
                for s, (p, q, e, ready) in enumerate(((P1, Q1, E0, E_first), (P0, Q0, E1, e_ready[0]), (P1, None, E0, e_ready[1]))):
                    for h in range(HP):
                        n = 2 * i + h + 1
                        pe.wait_ge(pw_ready[s], n)
                        if s < 2:
                            last = each(ps[h][1], lambda t: q[h][:, t], lambda t: p[h][:, t])
                            if s == 1:
                                last.then_inc(pw_done[2], 1)
                        if s == 0:
                            each(ps[h][2], lambda t: p[h][:, t], lambda t: q[h][:, t]).then_inc(pw_done[1], 1)
                            pe.wait_ge(qk_ready, n)
                        pe.wait_ge(ready, n)
                        each(ps[h][0], lambda t: p[h][:, t], lambda t: e[h][:, t]).then_inc(e_done[s], 1)
                for s in range(3):
                    link, e = (P0, P1, P0)[s], (E1, E0, E1)[s]
                    for h in range(HP):
                        n = 2 * i + h + 1
                        pe.wait_ge(e_ready[s + 2], n)
                        turn(ps[h][1], e[h], d_done[s])
                        pe.wait_ge(n_ready[s], n)
                        each(ps[h][2], lambda t: link[h][:, t], lambda t: e[h][:, t]).then_inc(y_done_[s], 1)
                    for h in range(HP):
                        n = 2 * i + h + 1
                        pe.wait_ge(d_ready[s], n)
                        pe.wait_ge(y_ready_[s], n)
                        each(ps[h][0], lambda t: Q0[h][:, t], lambda t: Q1[h][:, t]).then_inc(e_done[s + 3], 1)
                for h in range(HP):
                    n = 2 * i + h + 1
                    pe.wait_ge(e_ready[5], n)
                    pe.wait_ge(kbe_ready, n)
                    each(ps[h][2], lambda t: kbe[h][:, t], lambda t: E0[h][:, t]).then_inc(w_done, 1)
                pe.wait_ge(proj_free, 2 * KINDS * i + 10)
                ada.total(pe, i, 0, side)
                for t in range(TT):
                    for h in range(HP):
                        n = 2 * i + h + 1
                        if t == 0:
                            pe.wait_ge(vb_ready, n)
                            pe.wait_ge(w_ready, n)
                        last = nc.tensor.matmul(ps[h][1][:, t], E0[h][:, t], vb[h][:, t], start=True, stop=t == 0)
                        if t:
                            pe.wait_ge(s_ready, 2 * (TT - 1) * i + 2 * (t - 1) + h + 1)
                            last = nc.tensor.matmul(ps[h][1][:, t], wT[h][:, t], S[:, h, (t - 1) % 2], start=False, stop=True)
                        last.then_inc(vn_done, 1)
                        if t:
                            if t == 1:
                                pe.wait_ge(qg_ready, n)
                            nc.tensor.matmul(ps[h][0][:, t], S[:, h, (t - 1) % 2], qg[h][:, t], start=True, stop=False)
                    for h in range(HP):
                        pe.wait_ge(vn_ready, 2 * TT * i + 2 * t + h + 1)
                        if t < TT - 1:
                            nc.tensor.matmul(ps[h][2][:, t], kdec[h][:, t], vn[h][:, t], start=True, stop=True).then_inc(s_done, 1)
                        last = nc.tensor.matmul(ps[h][0][:, t], vn[h][:, t], qkT[h][:, t], start=t == 0, stop=True)
                        if t == TT - 1:
                            last.then_inc(o_done, 1)
                for h in range(HP):
                    sum_squares(ps[h][1], P1[h], o_sq, h, o_norm)
                pe.wait_ge(ada.ready, 2 * i + 2)
                pe.sem_inc(ada.asked, 1)
            pe.wait_ge(o_ready, 2 * TURNS + 2)
            for n in range(4):
                pe.wait_ge(w_in[n % 2], 32 * TURNS + 16 * (n // 2) + 16)
                for t in range(TT):
                    j = n * TT + t
                    if j >= 2:
                        pe.wait_ge(out_used, j - 1)
                    else:
                        pe.wait_ge(proj_free, 2 * KINDS * TURNS + 2)
                    for k in range(KT):
                        last = nc.tensor.matmul(pj[j % 2][:, 0:PF], oT[:, k, t * P:(t + 1) * P], w[:, n % 2, k],
                                                start=k == 0, stop=k == KT - 1)
                    last.then_inc(out_done, 1)
    st.close(gathers=True, beside=ring.st)


def build(nc, A, out):
    h_rows = nc.dram_tensor("h_rows", (SEQ, D), F32).ap()
    y_rows = nc.dram_tensor("y_rows", (SEQ * TOPK, D), F32).ap()
    ada_rows = nc.dram_tensor("ada_rows", (2 * DEPTH, 3 * D), F32).ap()
    with ExitStack() as ctx:
        c = alloc_core(nc, ctx)
        setup_stage(nc, c, A)
        ring = attention_ring(nc, A)
        norm_stage(nc, c, A, None, 0, ring=ring)
        attention_stage(nc, c, A, ada_rows, ring)
        weights = ExpertWeights(nc, A, 0)
        norm_stage(nc, c, A, 0, 1, ada_rows, h_rows=h_rows, weights=weights)
        moe_stage(nc, c, A, 0, h_rows, y_rows, weights)
        ring = delta_ring(nc, A)
        norm_stage(nc, c, A, 1, 2, ada_rows, ring=ring)
        delta_stage(nc, c, A, ada_rows, ring)
        weights = ExpertWeights(nc, A, 1)
        norm_stage(nc, c, A, 2, 3, ada_rows, h_rows=h_rows, weights=weights)
        moe_stage(nc, c, A, 1, h_rows, y_rows, weights)
        norm_stage(nc, c, A, 3, None, out=out)


_INS = ("x", "c", "positions", "ada_w", "ada_b", "ln_g", "ln_b", "attn_w_in", "attn_w_out", "gdn_w_in", "gdn_conv_w",
        "gdn_a_log", "gdn_dt_bias", "gdn_norm_w", "gdn_w_out", "router_w", "router_bias", "expert_w1", "expert_w3",
        "expert_w2", "shared_w1", "shared_w3", "shared_w2")


def kernel(**inputs):
    import concourse.bacc as _bacc
    from concourse.bass_utils import run_bass_kernel_spmd as _run

    nc = _bacc.Bacc("TRN2", target_bir_lowering=False, num_devices=1)
    arrays, A = {}, {}
    for name in _INS:
        a = np.ascontiguousarray(inputs[name])
        arrays[f"in_{name}_dram"] = a
        A[name] = nc.dram_tensor(f"in_{name}_dram", a.shape, mybir.dt.from_np(a.dtype), kind="ExternalInput").ap()
    out = nc.dram_tensor("out_dram", (1, SEQ, D), F32, kind="ExternalOutput").ap()
    build(nc, A, out)
    r = _run(nc, [arrays], core_ids=[0])
    return r.results[0]["out_dram"]
```
